# Optimizing a Trainium2 kernel written in Bass

```python
import math
import jax, jax.numpy as jnp
from jax import lax
import numpy as np

D_MODEL = 1024
BATCH = 1
SEQ = 1024
DEPTH = 1
DEC_BATCH = 8
DEC_SEQ = 8
PAST_LEN = 4096
PAGE_SIZE = 128

HEAD_DIM = 64
N_ATT_HEADS = 8
ATT_BRANCHES = ((128, 1), (512, 4), (2048, 16))
MAX_WINDOW = 2048
ROPE_THETA = 500000.0
ROPE_DIM = HEAD_DIM // 4
N_RET_HEADS = 4
RET_QK_DIM = 64
RET_V_DIM = 128
RET_THETA = 10000.0
RET_CHUNK = 128
ATT_WIDTH = N_ATT_HEADS * HEAD_DIM
RET_QK_WIDTH = N_RET_HEADS * RET_QK_DIM
RET_V_WIDTH = N_RET_HEADS * RET_V_DIM
MIX_WIDTH = ATT_WIDTH + RET_V_WIDTH
IN_WIDTH = 3 * ATT_WIDTH + 2 * RET_QK_WIDTH + 2 * RET_V_WIDTH
D_FF = 4 * D_MODEL
EPS = 1e-6

kernel_name = 'hybrid_dilated_attn_retention_decode_step'

F32 = jnp.float32

def _rms(x):
    x32 = x.astype(F32)
    return (x32 * lax.rsqrt(jnp.mean(x32 * x32, axis=-1, keepdims=True) + EPS)).astype(x.dtype)

def _adaln(c, w, b, n):
    mod = jnp.dot(jax.nn.silu(c), w) + b
    return jnp.split(mod[:, None, :], n, axis=-1)

def _partial_rope(x, pos):
    half = ROPE_DIM // 2
    inv = ROPE_THETA ** (-jnp.arange(0, ROPE_DIM, 2, dtype=F32) / ROPE_DIM)
    ang = pos.astype(F32)[:, None] * inv[None, :]
    cos = jnp.cos(ang)[None, :, None, :]
    sin = jnp.sin(ang)[None, :, None, :]
    x32 = x.astype(F32)
    x1 = x32[..., :half]
    x2 = x32[..., half:ROPE_DIM]
    out = jnp.concatenate([x1 * cos - x2 * sin, x2 * cos + x1 * sin, x32[..., ROPE_DIM:]], axis=-1)
    return out.astype(x.dtype)

def _ret_rotate(x, pos):
    inv = RET_THETA ** (-jnp.linspace(0.0, 1.0, RET_QK_DIM // 2, dtype=F32))
    ang = pos.astype(F32)[:, None] * inv[None, :]
    cos = jnp.cos(ang)[None, :, None, :]
    sin = jnp.sin(ang)[None, :, None, :]
    xr = x.astype(F32).reshape(x.shape[:-1] + (RET_QK_DIM // 2, 2))
    x1, x2 = xr[..., 0], xr[..., 1]
    return jnp.stack([x1 * cos - x2 * sin, x2 * cos + x1 * sin], axis=-1).reshape(x.shape)

def _project(z, w_in, pos):
    B, T, _ = z.shape
    p = jnp.dot(z, w_in)
    o1 = ATT_WIDTH
    o2 = o1 + ATT_WIDTH
    o3 = o2 + ATT_WIDTH
    o4 = o3 + RET_QK_WIDTH
    o5 = o4 + RET_QK_WIDTH
    o6 = o5 + RET_V_WIDTH
    qa, ka, va, qr, kr, vr, gr = jnp.split(p, [o1, o2, o3, o4, o5, o6], axis=-1)
    qa = _partial_rope(qa.reshape(B, T, N_ATT_HEADS, HEAD_DIM), pos)
    ka = _partial_rope(ka.reshape(B, T, N_ATT_HEADS, HEAD_DIM), pos)
    va = va.reshape(B, T, N_ATT_HEADS, HEAD_DIM)
    qr = _ret_rotate(qr.reshape(B, T, N_RET_HEADS, RET_QK_DIM), pos)
    kr = _ret_rotate(kr.reshape(B, T, N_RET_HEADS, RET_QK_DIM), pos) * (RET_QK_DIM ** -0.5)
    vr = vr.reshape(B, T, N_RET_HEADS, RET_V_DIM).astype(F32)
    return qa, ka, va, qr, kr, vr, gr

def _masked_softmax(s, valid):
    s = jnp.where(valid, s, -jnp.inf)
    m = jnp.max(s, axis=-1, keepdims=True)
    p = jnp.exp(s - m)
    l = jnp.sum(p, axis=-1, keepdims=True)
    return p / l, (m + jnp.log(l))[..., 0]

def _dilated_branch_prompt(q, k, v, window, dil):
    B, S, H, Dh = q.shape
    n = window // dil
    M = S // dil
    nb = -(-M // n)
    pad = nb * n - M

    def blocks(t):
        t = t.reshape(B, M, dil, H, Dh).transpose(0, 2, 1, 3, 4)
        t = jnp.pad(t, ((0, 0), (0, 0), (0, pad), (0, 0), (0, 0)))
        return t.reshape(B, dil, nb, n, H, Dh)

    def with_prev(t):
        prev = jnp.pad(t, ((0, 0), (0, 0), (1, 0), (0, 0), (0, 0), (0, 0)))[:, :, :nb]
        return jnp.concatenate([prev, t], axis=3)

    qb = blocks(q)
    kw = with_prev(blocks(k))
    vw = with_prev(blocks(v))
    s = jnp.einsum('brcqhd,brckhd->brchqk', qb, kw).astype(F32) * (HEAD_DIM ** -0.5)
    qi = jnp.arange(n)[:, None]
    kj = jnp.arange(2 * n)[None, :]
    dist = qi + n - kj
    kg = jnp.arange(nb)[:, None, None] * n - n + kj[None]
    valid = (dist[None] >= 0) & (dist[None] <= n) & (kg >= 0)
    p, lse = _masked_softmax(s, valid[None, None, :, None])
    o = jnp.einsum('brchqk,brckhd->brcqhd', p, vw.astype(F32))
    o = o.reshape(B, dil, nb * n, H, Dh)[:, :, :M].transpose(0, 2, 1, 3, 4).reshape(B, S, H, Dh)
    lse = lse.transpose(0, 1, 2, 4, 3).reshape(B, dil, nb * n, H)[:, :, :M]
    lse = lse.transpose(0, 2, 1, 3).reshape(B, S, H)
    return o, lse

def _dilated_branch_sample(q, k_all, v_all, L, window, dil):
    T = q.shape[1]
    n = window // dil
    idx = L + jnp.arange(T)[:, None] - dil * jnp.arange(n + 1)[None, :]
    valid = idx >= 0
    idxc = jnp.maximum(idx, 0)
    kg = k_all[:, idxc]
    vg = v_all[:, idxc]
    s = jnp.einsum('bqhd,bqkhd->bhqk', q, kg).astype(F32) * (HEAD_DIM ** -0.5)
    p, lse = _masked_softmax(s, valid[None, None])
    o = jnp.einsum('bhqk,bqkhd->bqhd', p, vg.astype(F32))
    return o, lse.transpose(0, 2, 1)

def _combine(outs, lses):
    w = jax.nn.softmax(jnp.stack(lses, axis=0), axis=0)
    return jnp.sum(w[..., None] * jnp.stack(outs, axis=0), axis=0)

def _retention(q, k, v, state0):
    B, T, H, dk = q.shape
    dv = v.shape[-1]
    chunk = math.gcd(T, RET_CHUNK)
    nc = T // chunk
    log_g = jnp.log1p(-jnp.exp2(-5.0 - jnp.arange(H, dtype=F32)))
    i = jnp.arange(chunk, dtype=F32)
    rel = i[:, None] - i[None, :]
    dmask = jnp.where(rel[None] >= 0, jnp.exp(jnp.maximum(rel, 0.0)[None] * log_g[:, None, None]), 0.0)
    qc = q.reshape(B, nc, chunk, H, dk)
    kc = k.reshape(B, nc, chunk, H, dk)
    vc = v.reshape(B, nc, chunk, H, dv)
    s = jnp.einsum('bnqhd,bnkhd->bnhqk', qc, kc) * dmask
    inner = jnp.einsum('bnhqk,bnkhe->bnqhe', s, vc)
    d_in = jnp.exp((chunk - 1.0 - i)[:, None] * log_g[None, :])
    d_out = jnp.exp((i + 1.0)[:, None] * log_g[None, :])
    kv = jnp.einsum('bnkhd,bnkhe->nbhde', kc * d_in[:, :, None], vc)
    g_chunk = jnp.exp(chunk * log_g)[None, :, None, None]

    def step(st, kv_c):
        return g_chunk * st + kv_c, st

    s_final, s_prev = lax.scan(step, state0, kv)
    cross = jnp.einsum('bnqhd,nbhde->bnqhe', qc * d_out[:, :, None], s_prev)
    return (inner + cross).reshape(B, T, H, dv), s_final

def _ret_out(o, g, gain):
    B, T = o.shape[:2]
    mu = jnp.mean(o, axis=-1, keepdims=True)
    var = jnp.mean(jnp.square(o - mu), axis=-1, keepdims=True)
    on = ((o - mu) * lax.rsqrt(var + EPS)).reshape(B, T, RET_V_WIDTH) * gain
    return jax.nn.silu(g.astype(F32)) * on

def _mlp(z, w1, w2):
    return jnp.dot(jnp.square(jax.nn.relu(jnp.dot(z, w1))), w2)

def _prompt_layer(x, c, w_ada, b_ada, w_in, ret_gain, w_out, w_ff1, w_ff2):
    B, S, _ = x.shape
    pos = jnp.arange(S, dtype=jnp.int32)
    sh_a, sc_a, g_a, sh_f, sc_f, g_f = _adaln(c, w_ada, b_ada, 6)
    z = _rms(x) * (1 + sc_a) + sh_a
    qa, ka, va, qr, kr, vr, gr = _project(z, w_in, pos)
    outs, lses = [], []
    for window, dil in ATT_BRANCHES:
        o, lse = _dilated_branch_prompt(qa, ka, va, window, dil)
        outs.append(o)
        lses.append(lse)
    att = _combine(outs, lses).reshape(B, S, ATT_WIDTH)
    state0 = jnp.zeros((B, N_RET_HEADS, RET_QK_DIM, RET_V_DIM), F32)
    ret, state = _retention(qr, kr, vr, state0)
    mix = jnp.concatenate([att, _ret_out(ret, gr, ret_gain)], axis=-1).astype(x.dtype)
    x = x + g_a * jnp.dot(mix, w_out)
    x = x + g_f * _mlp(_rms(x) * (1 + sc_f) + sh_f, w_ff1, w_ff2)
    keep = min(MAX_WINDOW, S)
    return x, ka[:, S - keep:], va[:, S - keep:], state

def _sample_layer(x, c, ck, cv, st, w_ada, b_ada, w_in, ret_gain, w_out, w_ff1, w_ff2):
    DB, T, _ = x.shape
    L = ck.shape[1]
    pos = PAST_LEN + jnp.arange(T, dtype=jnp.int32)
    sh_a, sc_a, g_a, sh_f, sc_f, g_f = _adaln(c, w_ada, b_ada, 6)
    z = _rms(x) * (1 + sc_a) + sh_a
    qa, ka, va, qr, kr, vr, gr = _project(z, w_in, pos)
    k_all = jnp.concatenate([ck.astype(ka.dtype), ka], axis=1)
    v_all = jnp.concatenate([cv.astype(va.dtype), va], axis=1)
    outs, lses = [], []
    for window, dil in ATT_BRANCHES:
        o, lse = _dilated_branch_sample(qa, k_all, v_all, L, window, dil)
        outs.append(o)
        lses.append(lse)
    att = _combine(outs, lses).reshape(DB, T, ATT_WIDTH)
    ret, state = _retention(qr, kr, vr, st.astype(F32))
    mix = jnp.concatenate([att, _ret_out(ret, gr, ret_gain)], axis=-1).astype(x.dtype)
    x = x + g_a * jnp.dot(mix, w_out)
    x = x + g_f * _mlp(_rms(x) * (1 + sc_f) + sh_f, w_ff1, w_ff2)
    return x, ka, va, state

def _final_norm(x, c, w, b):
    sh, sc = _adaln(c, w, b, 2)
    return _rms(x) * (1 + sc) + sh

def setup_inputs(seed: int = 0) -> dict:
    key = jax.random.key(seed)
    ks = jax.random.split(key, 16)
    cache_len = min(MAX_WINDOW, PAST_LEN)

    def nrm(k, shape, s):
        return jax.random.normal(k, shape, F32) * s

    return {
        'x_prompt': nrm(ks[0], (BATCH, SEQ, D_MODEL), 1.0),
        'x_sample': nrm(ks[1], (DEC_BATCH, DEC_SEQ, D_MODEL), 1.0),
        'c_prompt': nrm(ks[2], (BATCH, D_MODEL), 1.0),
        'c_sample': nrm(ks[3], (DEC_BATCH, D_MODEL), 1.0),
        'cache_k': nrm(ks[4], (DEPTH, DEC_BATCH, cache_len, N_ATT_HEADS, HEAD_DIM), 1.0),
        'cache_v': nrm(ks[5], (DEPTH, DEC_BATCH, cache_len, N_ATT_HEADS, HEAD_DIM), 1.0),
        'state_ret': nrm(ks[6], (DEPTH, DEC_BATCH, N_RET_HEADS, RET_QK_DIM, RET_V_DIM), 1.0),
        'w_ada': nrm(ks[7], (DEPTH, D_MODEL, 6 * D_MODEL), 0.5 * D_MODEL ** -0.5),
        'b_ada': nrm(ks[8], (DEPTH, 6 * D_MODEL), 0.02),
        'w_in': nrm(ks[9], (DEPTH, D_MODEL, IN_WIDTH), D_MODEL ** -0.5),
        'ret_gain': 1.0 + nrm(ks[10], (DEPTH, RET_V_WIDTH), 0.02),
        'w_out': nrm(ks[11], (DEPTH, MIX_WIDTH, D_MODEL), MIX_WIDTH ** -0.5),
        'w_ff1': nrm(ks[12], (DEPTH, D_MODEL, D_FF), D_MODEL ** -0.5),
        'w_ff2': nrm(ks[13], (DEPTH, D_FF, D_MODEL), D_FF ** -0.5),
        'w_ada_f': nrm(ks[14], (D_MODEL, 2 * D_MODEL), 0.5 * D_MODEL ** -0.5),
        'b_ada_f': nrm(ks[15], (2 * D_MODEL,), 0.02),
    }

def reference(x_prompt, x_sample, c_prompt, c_sample, cache_k, cache_v, state_ret,
              w_ada, b_ada, w_in, ret_gain, w_out, w_ff1, w_ff2, w_ada_f, b_ada_f):
    xp, xs = x_prompt, x_sample
    kp_l, vp_l, sp_l, ks_l, vs_l, ss_l = [], [], [], [], [], []
    for l in range(DEPTH):
        xp, kp, vp, sp = _prompt_layer(xp, c_prompt, w_ada[l], b_ada[l], w_in[l], ret_gain[l],
                                       w_out[l], w_ff1[l], w_ff2[l])
        xs, ksn, vsn, ssn = _sample_layer(xs, c_sample, cache_k[l], cache_v[l], state_ret[l],
                                          w_ada[l], b_ada[l], w_in[l], ret_gain[l],
                                          w_out[l], w_ff1[l], w_ff2[l])
        kp_l.append(kp)
        vp_l.append(vp)
        sp_l.append(sp)
        ks_l.append(ksn)
        vs_l.append(vsn)
        ss_l.append(ssn)
    y_prompt = _final_norm(xp, c_prompt, w_ada_f, b_ada_f)
    y_sample = _final_norm(xs, c_sample, w_ada_f, b_ada_f)
    return (y_prompt, y_sample, jnp.stack(kp_l), jnp.stack(vp_l), jnp.stack(sp_l),
            jnp.stack(ks_l), jnp.stack(vs_l), jnp.stack(ss_l))


_drawn_inputs = setup_inputs


def setup_inputs(seed=0):
    import zlib

    import numpy as np

    out = dict(_drawn_inputs(seed))
    spreads = {}
    factors = {'cache_k': 3.201, 'ret_gain': 8.0}
    for name, (base, spread) in spreads.items():
        noise = np.random.default_rng([zlib.crc32(name.encode()), seed]).standard_normal(out[name].shape)
        drawn = base * np.exp(spread * noise) if base else spread * noise
        out[name] = __import__('jax').numpy.asarray(drawn.astype(out[name].dtype))
    for name, factor in factors.items():
        out[name] = (out[name] * factor).astype(out[name].dtype)
    return out
```

```python
import math
from contextlib import ExitStack

import numpy as np
import concourse.bass as bass
from concourse import mybir

F32 = mybir.dt.float32
F32R = mybir.dt.float32r
ALU = mybir.AluOpType
ACT = mybir.ActivationFunctionType
ds = bass.ds

P = 128
D = 1024
KT = D // P
S = 1024
TT = S // P
DB, DS = 8, 8
NS = DB * DS
PAST = 4096
L = 2048
H, HD = 8, 64
AW = H * HD
RH, RD, RV = 4, 64, 128
IN_W = 3 * AW + 2 * RH * RD + 2 * RH * RV
CH = 512
FF = 4 * D
MOD_W = 8 * D
SH_A, SC_A, G_A, SH_F, SC_F, G_F, SH_L, SC_L = range(8)
EPS = 1e-6
NEG = -1e30
BRANCHES = ((128, 1), (512, 4), (2048, 16))
SCALE = HD ** -0.5
OLD = 1536
KTILES = 10
NKEYS = KTILES * P + DS
GF = 256
NG = FF // GF



def log_count(dist):
    n = np.zeros(dist.shape)
    for window, dil in BRANCHES:
        n += (dist >= 0) & (dist <= window) & (dist % dil == 0)
    return np.where(n > 0, np.log(np.maximum(n, 1)), NEG).astype(np.float32)


def sample_positions():
    old = [16 * (16 * j + g) + r for j in range(6) for g in range(16) for r in range(8)]
    return np.array(old + list(range(OLD, L)) + list(range(L, L + DS)))


def angles(theta_powers, pos):
    inv = theta_powers.astype(np.float32)
    return (pos.astype(np.float32)[:, None] * inv[None, :]).astype(np.float32)


def constants():
    f = np.float32
    c = {"ident": np.eye(P, dtype=f)}
    p = np.arange(P)
    c["bias_p"] = log_count(p[:, None] - np.arange(S)[None, :] + (S - P))
    keys = sample_positions()
    t = np.tile(np.arange(DS), 2 * H)
    c["bias_s"] = log_count(L + t[:, None] - keys[None, :])
    pos_p = np.arange(S)
    pos_s = PAST + np.tile(np.arange(DS), DB)
    att = 500000.0 ** (-np.arange(0, 16, 2) / 16.0)
    ret = 10000.0 ** (-np.linspace(0.0, 1.0, RD // 2, dtype=f).astype(np.float64))

    def table(fn, powers, pos, heads):
        a = fn(angles(powers, pos).astype(np.float64)).astype(f)
        return np.tile(a, (1, heads))

    def by_tile(a):
        return np.ascontiguousarray(a.reshape(TT, P, -1).transpose(1, 0, 2).reshape(P, -1))

    c["rope_p"] = np.concatenate([np.tile(by_tile(table(g, att, pos_p, 2)), (1, 2)) for g in (np.cos, np.sin)], 1)
    c["rope_s"] = np.concatenate([table(g, att, pos_s, 2 * H) for g in (np.cos, np.sin)], 1)
    c["rot_p"] = np.concatenate([by_tile(table(g, ret, pos_p, 2)) for g in (np.cos, np.sin)], 1)
    c["rot_s"] = np.concatenate([table(g, ret, pos_s, 2 * RH) for g in (np.cos, np.sin)], 1)
    log_g = np.log1p(-np.exp2(-5.0 - np.arange(RH)))
    rel = p[None, :] - p[:, None]
    c["dmask_p"] = np.concatenate(
        [np.where(rel >= 0, np.exp(np.maximum(rel, 0) * g), 0.0) for g in log_g], 1).astype(f)
    c["dout_p"] = np.concatenate(
        [np.repeat(np.exp((p + 1.0)[None, :] * log_g[2 * a:2 * a + 2, None]), RD, 0) for a in range(2)], 1).astype(f)
    c["din_p"] = (np.exp((P - 1.0 - p)[:, None] * log_g[None, :]) * RD ** -0.5).astype(f)
    c["gchunk_p"] = np.stack([np.repeat(np.exp(P * log_g[2 * a:2 * a + 2]), RD) for a in range(2)], 1).astype(f)
    i = np.arange(NS)
    same = i[:, None] // DS == i[None, :] // DS
    rel = i[None, :] - i[:, None]
    c["dmask_s"] = np.concatenate(
        [np.where(same & (rel >= 0), np.exp(np.maximum(rel, 0) * g), 0.0) for g in log_g], 1).astype(f)
    b2 = np.repeat(np.arange(2), RD)
    c["dout_s"] = np.stack([np.stack([
        np.where((i[None, :] // DS) == 2 * bp + b2[:, None], np.exp((i % DS + 1.0) * g)[None, :], 0.0)
        for bp in range(4)], 1) for g in log_g], 1).reshape(P, -1).astype(f)
    c["din_s"] = np.stack([np.stack([
        np.where((i[:, None] // DS) == 2 * bp + b2[None, :],
                 (np.exp((DS - 1.0 - i % DS) * g) * RD ** -0.5)[:, None], 0.0)
        for bp in range(4)], 1) for g in log_g], 1).reshape(NS, -1).astype(f)
    return c


GCHUNK_S = [float(np.float32(math.exp(DS * math.log1p(-2.0 ** (-5 - h))))) for h in range(RH)]


class Steps:

    def __init__(self, eng, sem):
        self.eng, self.sem, self.n, self.base = eng, sem, 0, 0

    def done(self, ins):
        ins.then_inc(self.sem, 1)
        self.n += 1
        return self.n

    def then(self, ins):
        self.done(ins)
        self.eng.wait_ge(self.sem, self.base + self.n)

    def wait(self):
        self.eng.wait_ge(self.sem, self.base + self.n)


class Stage:

    def __init__(self, nc, name):
        self.nc, self.name, self.ctx, self.sems = nc, name, ExitStack(), []
        self.ctx.callback(self.clear)

    def sb(self, name, shape, dt=F32):
        return self.ctx.enter_context(self.nc.sbuf_tensor(f"{self.name}_{name}", shape, dt))

    def sem(self, name):
        self.sems.append(self.nc.alloc_semaphore(f"{self.name}_{name}"))
        return self.sems[-1]

    def clear(self):
        self.nc.clear_and_free_semaphores(self.sems)
        self.nc.all_engine_barrier()

    def block(self):
        return self.ctx.enter_context(self.nc.Block())



def stage_modulation(nc, io, ps, ident, mod_p):
    st = Stage(nc, "mod")
    with st.ctx:
        crow, ex, srow = (st.sb(n, [9, D]) for n in ("crow", "ex", "srow"))
        cT = st.sb("cT", [P, KT, 10])
        mrow = st.sb("mrow", [9, MOD_W])
        brow = st.sb("brow", [9, MOD_W])
        w = [st.sb(f"w{s}", [P, KT, CH]) for s in range(4)]
        c_in, b_in, exp_done, dve, turned = (st.sem(n) for n in ("c_in", "b_in", "exp_done", "dve", "turned"))
        w_in = [st.sem(f"w_in{s}") for s in range(4)]
        w_free, bank_free, stored, loaded = (st.sem(n) for n in ("w_free", "bank_free", "stored", "loaded"))
        silu_steps = 4
        wv = io["w_ada"].rearrange("o (k p) n -> p (o k) n", p=P)
        wf = io["w_ada_f"].rearrange("(k p) n -> p k n", p=P)
        block = st.block()

        @block.sync
        def _(sp):
            sp.dma_start(crow[0:1, :], io["c_prompt"]).then_inc(c_in, 16)
            sp.dma_start(crow[1:9, :], io["c_sample"]).then_inc(c_in, 16)
            sp.dma_start(ident[:], io["ident"]).then_inc(c_in, 16)
            sp.dma_start(brow[:, 0:6 * D], io["b_ada"][0].partition_broadcast(9)).then_inc(b_in, 16)
            sp.dma_start(brow[:, 6 * D:], io["b_ada_f"].partition_broadcast(9)).then_inc(b_in, 16)
            with sp.Fori(0, 3) as i:
                for s in range(4):
                    sp.wait_ge(w_free, 4 * i + s + 1)
                    sp.dma_start(w[s][:], wv[:, :, ds(i * 4 * CH + s * CH, CH)]).then_inc(w_in[s], 16)
            for s in range(4):
                sp.wait_ge(w_free, 12 + s + 1)
                sp.dma_start(w[s][:], wf[:, :, s * CH:(s + 1) * CH]).then_inc(w_in[s], 16)
            sp.wait_ge(dve, silu_steps + 3)
            sp.dma_start(io["mod"], mrow[:]).then_inc(stored, 16)
            sp.wait_ge(stored, 16)
            for j, m in enumerate((SH_A, SC_A, SH_F, SC_F)):
                sp.dma_start(mod_p[:, j, :], io["mod"][0, m * D:(m + 1) * D].rearrange("(k p) -> p k", p=P),
                             allow_slow_non_contiguous=True).then_inc(loaded, 16)
            sp.wait_ge(loaded, 64)

        @block.scalar
        def _(act):
            act.wait_ge(c_in, 48)
            act.activation(ex[:], crow[:], ACT.Exp, scale=-1.0).then_inc(exp_done, 1)

        @block.tensor
        def _(pe):
            pe.sem_inc(w_free, 4)
            pe.wait_ge(dve, silu_steps - 1)
            for k in range(KT):
                last = pe.transpose(ps[:, 7, k * 10:k * 10 + 9], srow[:, k * P:(k + 1) * P], ident[0:9, 0:9])
            last.then_inc(turned, 1)
            pe.wait_ge(dve, silu_steps)
            with pe.Fori(0, 4) as i:
                for s in range(4):
                    pe.wait_ge(w_in[s], 16 * i + 16)
                    pe.wait_ge(bank_free, 4 * i + s + 1)
                    for k in range(KT):
                        mm = pe.matmul(ps[0:9, s, :], cT[:, k, 0:9], w[s][:, k, :], start=(k == 0), stop=(k == KT - 1))
                    mm.then_inc(w_free, 1)

        @block.vector
        def _(dve_):
            dve_.sem_inc(bank_free, 4)
            steps = Steps(dve_, dve)
            dve_.wait_ge(exp_done, 1)
            steps.then(dve_.tensor_scalar(ex[:], ex[:], 1.0, None, ALU.add))
            steps.then(dve_.reciprocal(ex[:], ex[:]))
            steps.done(dve_.tensor_tensor(srow[:], crow[:], ex[:], ALU.mult))
            dve_.wait_ge(turned, 1)
            steps.done(dve_.tensor_copy(cT[:, :, 0:9], ps[:, 7, 0:80].rearrange("p (k c) -> p k c", c=10)[:, :, 0:9]))
            assert steps.n == silu_steps
            dve_.wait_ge(b_in, 32)
            with dve_.Fori(0, 4) as i:
                for s in range(4):
                    dve_.wait_ge(w_free, 4 * i + s + 5)
                    cols = ds(i * 4 * CH + s * CH, CH)
                    dve_.tensor_tensor(mrow[:, cols], ps[0:9, s, :], brow[:, cols], ALU.add).then_inc(bank_free, 1)
            dve_.wait_ge(bank_free, 20)
            for m in (SC_A, SC_F, SC_L):
                steps.done(dve_.tensor_scalar(mrow[:, m * D:(m + 1) * D], mrow[:, m * D:(m + 1) * D], 1.0, None, ALU.add))



def norm_stage_tensors(st):
    return dict(
        x=st.sb("x", [P, TT, D]), sq=[st.sb(f"sq{s}", [P, D]) for s in range(2)],
        ss=st.sb("ss", [P, 16]), v=st.sb("v", [P, 16]), r=st.sb("r", [P, 16]), t=st.sb("t", [P, 16]))


def load_rows(eng, io, prompt, sample, m, sem):
    if prompt is not None:
        eng.dma_start(prompt[:], io["mod"][0, m * D:(m + 1) * D].partition_broadcast(P)).then_inc(sem, 16)
    if sample is not None:
        for b in range(DB):
            eng.dma_start(sample[b * DS:(b + 1) * DS, :],
                          io["mod"][1 + b, m * D:(m + 1) * D].partition_broadcast(DS)).then_inc(sem, 16)


def rms_rows(steps, act_ready, root_ready, T, n):
    dve, ss, v, r, t = steps.eng, T["ss"], T["v"], T["r"], T["t"]
    steps.wait()
    steps.then(dve.tensor_scalar(v[:, 0:n], ss[:, 0:n], 1.0 / D, EPS, ALU.mult, ALU.add))
    dve.sem_inc(act_ready, 1)
    dve.wait_ge(root_ready, 1)
    steps.then(dve.reciprocal(r[:, 0:n], t[:, 0:n]))
    steps.then(dve.tensor_tensor(ss[:, 0:n], r[:, 0:n], r[:, 0:n], ALU.mult))
    steps.then(dve.tensor_tensor(ss[:, 0:n], ss[:, 0:n], v[:, 0:n], ALU.mult))
    steps.then(dve.tensor_scalar(ss[:, 0:n], ss[:, 0:n], -0.5, 1.5, ALU.mult, ALU.add))
    steps.then(dve.tensor_tensor(r[:, 0:n], r[:, 0:n], ss[:, 0:n], ALU.mult))


def stage_norm(nc, io, ps, ident, mod_p, z_hi, z_lo, zs, name, sh, sc, jsh, jsc, branch=None):
    src_p, src_s = io["x_prompt"][0], io["x_sample"].rearrange("b t d -> (b t) d")
    st = Stage(nc, name)
    with st.ctx:
        T = norm_stage_tensors(st)
        x = T["x"]
        xs, scs, shs = (st.sb(n, [NS, D]) for n in ("xs", "scs", "shs"))
        zf = [st.sb(f"zf{s}", [P, CH]) for s in range(4)]
        x_in, s_in, dve, v_ready, root = (st.sem(n) for n in ("x_in", "s_in", "dve", "v_ready", "root"))
        x_t = [st.sem(f"x_in{t}") for t in range(TT)]
        xn_ready, turned, zf_ready, hi_ready, lo_done = (
            st.sem(n) for n in ("xn_ready", "turned", "zf_ready", "hi_ready", "lo_done"))
        zs_turned, zs_hi = st.sem("zs_turned"), st.sem("zs_hi")
        if branch:
            br_dram, gate = branch
            br = [st.sb(f"br{s}", [P, D]) for s in range(2)]
            br_s = st.sb("br_s", [NS, 2, D])
            gate_p, gate_s = st.sb("gate_p", [P, D]), st.sb("gate_s", [NS, D])
            br_in = [st.sem(f"br_in{s}") for s in range(2)]
            brs_in, br_free, g_in, x1_ready, x1_put = (
                st.sem(n) for n in ("brs_in", "br_free", "g_in", "x1_ready", "x1_put"))
        block = st.block()
        units = [(h, k) for h in range(2) for k in range(KT)]

        @block.sync
        def _(sp):
            for t in range(TT):
                sp.dma_start(x[:, t, :], src_p[t * P:(t + 1) * P, :]).then_inc(x_t[t], 16)
            sp.dma_start(xs[:], src_s).then_inc(s_in, 16)
            if branch:
                load_rows(sp, io, gate_p, None, gate, g_in)
                load_rows(sp, io, None, gate_s, gate, g_in)
                sp.dma_start(br_s[:], br_dram[S:S + P, :].rearrange("(a n) d -> n a d", a=2)).then_inc(brs_in, 16)
            for dst, m in ((scs, sc), (shs, sh)):
                load_rows(sp, io, None, dst, m, s_in)
            if branch:
                for t in range(TT):
                    sp.wait_ge(br_free, t + 1)
                    sp.dma_start(br[t % 2][:], br_dram[t * P:(t + 1) * P, :]).then_inc(br_in[t % 2], 16)
                    if t:
                        sp.wait_ge(x1_ready, t)
                        sp.dma_start(io["x1"][(t - 1) * P:t * P, :], x[:, t - 1, :]).then_inc(x1_put, 16)
                sp.wait_ge(x1_ready, TT)
                sp.dma_start(io["x1"][S - P:S, :], x[:, TT - 1, :]).then_inc(x1_put, 16)
                sp.wait_ge(x1_ready, TT + 1)
                sp.dma_start(io["x1"][S:S + NS, :], xs[:]).then_inc(x1_put, 16)
                sp.wait_ge(x1_put, 16 * (TT + 1))

        @block.scalar
        def _(act):
            act.wait_ge(v_ready, 1)
            act.activation(T["t"][:, 0:9], T["v"][:, 0:9], ACT.Sqrt).then_inc(root, 1)
            for u, (h, k) in enumerate(units):
                act.wait_ge(zf_ready, u + 1)
                act.copy(z_hi[:, k, h * CH:(h + 1) * CH], zf[u % 4][:]).then_inc(hi_ready, 1)
            act.wait_ge(zs_turned, 1)
            act.copy(zs[:, :, 0:NS], ps[:, 7, :].rearrange("p (k n) -> p k n", n=NS)).then_inc(zs_hi, 1)

        @block.gpsimd
        def _(pool):
            for u, (h, k) in enumerate(units):
                pool.wait_ge(hi_ready, u + 1)
                pool.tensor_tensor(z_lo[:, k, h * CH:(h + 1) * CH], zf[u % 4][:],
                                   z_hi[:, k, h * CH:(h + 1) * CH].bitcast(F32), ALU.subtract).then_inc(lo_done, 1)

        @block.vector
        def _(dve_):
            steps = Steps(dve_, dve)
            dve_.memset(T["ss"][:], 1.0).then_inc(dve, 1)
            steps.n += 1
            steps.wait()
            if branch:
                dve_.sem_inc(br_free, 2)
                dve_.wait_ge(g_in, 16 * (1 + DB))
            for t in range(TT):
                dve_.wait_ge(x_t[t], 16)
                if branch:
                    dve_.wait_ge(br_in[t % 2], 16 * (t // 2) + 16)
                    steps.then(dve_.tensor_tensor(br[t % 2][:], br[t % 2][:], gate_p[:], ALU.mult))
                    steps.then(dve_.tensor_tensor(x[:, t, :], x[:, t, :], br[t % 2][:], ALU.add))
                    dve_.sem_inc(br_free, 1)
                    dve_.sem_inc(x1_ready, 1)
                steps.then(dve_.tensor_tensor_reduce(T["sq"][t % 2][:], x[:, t, :], x[:, t, :], 1.0, 0.0,
                                                     ALU.mult, ALU.add, T["ss"][:, t:t + 1]))
            dve_.wait_ge(s_in, 16 * 17)
            if branch:
                dve_.wait_ge(brs_in, 16)
                steps.then(dve_.tensor_tensor(br_s[:, 0], br_s[:, 0], br_s[:, 1], ALU.add))
                steps.then(dve_.tensor_tensor(br_s[:, 0], br_s[:, 0], gate_s[:], ALU.mult))
                steps.then(dve_.tensor_tensor(xs[:], xs[:], br_s[:, 0], ALU.add))
                dve_.sem_inc(x1_ready, 1)
            steps.then(dve_.tensor_tensor_reduce(T["sq"][0][0:NS, :], xs[:], xs[:], 1.0, 0.0,
                                                 ALU.mult, ALU.add, T["ss"][0:NS, 8:9]))
            rms_rows(steps, v_ready, root, T, 9)
            if branch:
                dve_.wait_ge(x1_put, 16 * (TT + 1))
            for t in range(TT):
                dve_.tensor_scalar(x[:, t, :], x[:, t, :], T["r"][:, t:t + 1], None, ALU.mult).then_inc(xn_ready, 1)
            steps.then(dve_.scalar_tensor_tensor(out=xs[:], in0=xs[:], scalar=T["r"][0:NS, 8:9], in1=scs[:],
                                                 op0=ALU.mult, op1=ALU.mult))
            dve_.tensor_tensor(xs[:], xs[:], shs[:], ALU.add).then_inc(xn_ready, 1)
            for u, (h, k) in enumerate(units):
                dve_.wait_ge(turned, u + 1)
                if u >= 4:
                    dve_.wait_ge(lo_done, u - 3)
                dve_.tensor_scalar(zf[u % 4][:], ps[:, u % 6, :], mod_p[:, jsc, k:k + 1], mod_p[:, jsh, k:k + 1],
                                   ALU.mult, ALU.add).then_inc(zf_ready, 1)
            dve_.wait_ge(zs_hi, 1)
            dve_.tensor_tensor(zs[:, :, NS:P], ps[:, 7, :].rearrange("p (k n) -> p k n", n=NS),
                               zs[:, :, 0:NS].bitcast(F32), ALU.subtract).then_inc(zf_ready, 1)

        @block.tensor
        def _(pe):
            for u, (h, k) in enumerate(units):
                pe.wait_ge(xn_ready, 4 * (h + 1))
                if u >= 6:
                    pe.wait_ge(zf_ready, u - 5)
                for j in range(4):
                    mm = pe.transpose(ps[:, u % 6, j * P:(j + 1) * P], x[:, 4 * h + j, k * P:(k + 1) * P], ident[:])
                mm.then_inc(turned, 1)
            pe.wait_ge(xn_ready, 9)
            for k in range(KT):
                mm = pe.transpose(ps[:, 7, k * NS:(k + 1) * NS], xs[:, k * P:(k + 1) * P], ident[0:NS, 0:NS])
            mm.then_inc(zs_turned, 1)



def stage_projection(nc, name, ps, w_dram, width, out, z_hi, z_lo, zs):
    st = Stage(nc, name)
    NCH = width // CH
    OUTS = TT + 1
    BANKS, ROWS = 6, 3
    with st.ctx:
        raw = [st.sb(f"raw{s}", [P, KT, CH]) for s in range(2)]
        w_hi = [st.sb(f"whi{s}", [P, KT, CH], F32R) for s in range(2)]
        w_lo = [st.sb(f"wlo{s}", [P, KT, CH], F32R) for s in range(2)]
        row = [st.sb(f"row{s}", [P, CH]) for s in range(ROWS)]
        raw_in = [st.sem(f"raw_in{s}") for s in range(2)]
        raw_free, w_free, w_hi_done, w_ready, made, bank_free = (
            st.sem(n) for n in ("raw_free", "w_free", "w_hi_done", "w_ready", "made", "bank_free"))
        row_free = [st.sem(f"row_free{s}") for s in range(ROWS)]
        wv = w_dram.rearrange("o (k p) n -> p (o k) n", p=P)
        block = st.block()

        @block.sync
        def _(sp):
            with sp.Fori(0, NCH // 2) as i:
                for s in range(2):
                    sp.wait_ge(raw_free, 2 * i + s + 1)
                    sp.dma_start(raw[s][:], wv[:, :, ds(i * 2 * CH + s * CH, CH)]).then_inc(raw_in[s], 16)

        @block.vector
        def _(dve):
            dve.sem_inc(raw_free, 2)
            with dve.Fori(0, NCH // 2) as i:
                for s in range(2):
                    dve.wait_ge(raw_in[s], 16 * i + 16)
                    dve.wait_ge(w_free, 2 * i + s + 1)
                    dve.tensor_copy(w_hi[s][:], raw[s][:]).then_inc(w_hi_done, 1)
                    dve.wait_ge(w_hi_done, 2 * i + s + 1)
                    dve.tensor_tensor(w_lo[s][:], raw[s][:], w_hi[s][:].bitcast(F32), ALU.subtract).then_inc(raw_free, 1)

        @block.tensor
        def _(pe):
            pe.sem_inc(w_free, 2)
            with pe.Fori(0, NCH // 2) as i:
                for s in range(2):
                    pe.wait_ge(raw_free, 2 * i + s + 3)
                    for o in range(OUTS):
                        n = s * OUTS + o
                        bank = ps[:, n % BANKS, :]
                        pe.wait_ge(bank_free, i * 2 * OUTS + n + 1)
                        if o < TT:
                            parts = ((z_hi, w_hi), (z_hi, w_lo), (z_lo, w_hi))
                            cols = slice(o * P, (o + 1) * P)
                        else:
                            parts = ((zs, w_hi), (zs, w_lo))
                            cols = slice(0, P)
                        for k in range(KT):
                            for a, (z, w) in enumerate(parts):
                                mm = pe.matmul(bank, z[:, k, cols], w[s][:, k, :], start=(k == 0 and a == 0),
                                               stop=(k == KT - 1 and a == len(parts) - 1))
                        mm.then_inc(made, 1)
                    pe.wait_ge(made, i * 2 * OUTS + (s + 1) * OUTS)
                    pe.sem_inc(w_free, 1)

        @block.scalar
        def _(act):
            act.sem_inc(bank_free, BANKS)
            for r in range(ROWS):
                act.sem_inc(row_free[r], 16)
            with act.Fori(0, NCH // 2) as i:
                for s in range(2):
                    for o in range(OUTS):
                        n = s * OUTS + o
                        act.wait_ge(made, i * 2 * OUTS + n + 1)
                        act.wait_ge(row_free[n % ROWS], i * (16 * 2 * OUTS // ROWS) + 16 * (n // ROWS) + 16)
                        act.copy(row[n % ROWS][:], ps[:, n % BANKS, :]).then_inc(bank_free, 1)
                        act.wait_ge(bank_free, i * 2 * OUTS + n + BANKS + 1)
                        act.dma_start(out[o * P:(o + 1) * P, ds(i * 2 * CH + s * CH, CH)],
                                      row[n % ROWS][:]).then_inc(row_free[n % ROWS], 16)
            for r in range(ROWS):
                act.wait_ge(row_free[r], 16 * (NCH * OUTS // ROWS) + 16)



def banks(ps, first, n):
    return ps[:, first:first + n, :].rearrange("p b c -> p (b c)")


def stage_prompt_attention(nc, io, ps, ident, mix_hi, mix_lo):
    st = Stage(nc, "att")
    UNITS = 2 * TT
    HALF = ROPE = 8
    with st.ctx:
        bias = st.sb("bias", [P, S])
        rope = st.sb("rope", [P, 2, 2 * TT, 2, HALF])
        qk = [st.sb(f"qk{s}", [P, 2 * TT, P]) for s in range(2)]
        v = [st.sb(f"v{s}", [P, TT, P]) for s in range(2)]
        tmp = [st.sb(f"tmp{s}", [P, 2 * TT, 2, HALF]) for s in range(4)]
        q_hi = [st.sb(f"qhi{h}", [P, S], F32R) for h in range(2)]
        q_lo = [st.sb(f"qlo{h}", [P, S], F32R) for h in range(2)]
        k_hi, k_lo = st.sb("khi", [P, S], F32R), st.sb("klo", [P, S], F32R)
        prob = [st.sb(f"prob{s}", [P, S]) for s in range(3)]
        probT = [st.sb(f"probT{s}", [P, S]) for s in range(2)]
        top, neg, total, inv = (st.sb(n, [P, UNITS]) for n in ("top", "neg", "total", "inv"))
        waited = st.sb("waited", [P, 1])
        tables, zeroed, roped, heads_free, turned, hi_done, split_done = (st.sem(n) for n in (
            "tables", "zeroed", "roped", "heads_free", "turned", "hi_done", "split_done"))
        made, scored, neg_done, exp_done, inv_done, prob_done, prob_turned, probT_done, pv_done, mix_hi_done = (
            st.sem(n) for n in ("made", "scored", "neg_done", "exp_done", "inv_done", "prob_done",
                                "prob_turned", "probT_done", "pv_done", "mix_hi_done"))
        mix_done = st.sem("mix_done")
        qkv_in = [st.sem(f"qkv_in{s}") for s in range(2)]
        kv_put = [st.sem(f"kv_put{s}") for s in range(2)]

        def unit(u):
            h, q = divmod(u, TT)
            return h, (TT - 1 - q if h else q)

        proj = io["proj"][0:S, :].rearrange("(t p) c -> p t c", p=P)
        k_out = io["k_prompt"].rearrange("o b (t p) h d -> p (o b t) (h d)", p=P)
        v_out = io["v_prompt"].rearrange("o b (t p) h d -> p (o b t) (h d)", p=P)
        block = st.block()

        @block.sync
        def _(sp):
            for s in range(2):
                sp.sem_inc(kv_put[s], 32)
            sp.dma_start(bias[:], io["bias_p"]).then_inc(tables, 16)
            sp.dma_start(rope[:].rearrange("p a b c d -> p (a b c d)"), io["rope_p"]).then_inc(tables, 16)
            with sp.Fori(0, 2) as i:
                for s in range(2):
                    cols = [sp.snap(i * 2 * P + s * P + j * AW) for j in range(3)]
                    sp.wait_ge(heads_free, 2 * i + s + 1)
                    sp.wait_ge(kv_put[s], 32 * i + 32)
                    for j, dst in ((0, qk[s][:, 0:TT, :]), (1, qk[s][:, TT:, :]), (2, v[s][:])):
                        sp.dma_start(dst, proj[:, :, ds(cols[j], P)]).then_inc(qkv_in[s], 16)
                    sp.wait_ge(roped, 6 * (2 * i + s) + 6)
                    sp.dma_start(k_out[:, :, ds(cols[0], P)], qk[s][:, TT:, :]).then_inc(kv_put[s], 16)
                    sp.dma_start(v_out[:, :, ds(cols[0], P)], v[s][:]).then_inc(kv_put[s], 16)
            for s in range(2):
                sp.wait_ge(kv_put[s], 96)

        @block.gpsimd
        def _(pool):
            pool.wait_ge(tables, 32)
            with pool.Fori(0, 2) as i:
                for s in range(2):
                    n = 6 * (2 * i + s)
                    pool.wait_ge(qkv_in[s], 48 * i + 48)
                    x = qk[s][:].rearrange("p t (h d) -> p t h d", h=2)
                    a, b = x[:, :, :, 0:HALF], x[:, :, :, HALF:2 * HALF]
                    for dst, u, w in ((0, a, 0), (1, b, 1), (2, b, 0), (3, a, 1)):
                        pool.tensor_tensor(tmp[dst][:], u, rope[:, w], ALU.mult).then_inc(roped, 1)
                    pool.wait_ge(roped, n + 4)
                    pool.tensor_tensor(a, tmp[0][:], tmp[1][:], ALU.subtract).then_inc(roped, 1)
                    pool.tensor_tensor(b, tmp[2][:], tmp[3][:], ALU.add).then_inc(roped, 1)
                    pool.wait_ge(roped, n + 6)

        @block.tensor
        def _(pe):
            pe.sem_inc(heads_free, 2)
            pe.sem_inc(prob_turned, 3)
            pe.sem_inc(pv_done, 2)
            with pe.Fori(0, 2) as i:
                for s in range(2):
                    base = i * 2 * UNITS + s * UNITS

                    def scores(u):
                        h, q = unit(u)
                        if u >= 2:
                            pe.wait_ge(scored, base + u - 1)
                        width = (q + 1) * P
                        for c in range(0, width, CH):
                            e = min(width, c + CH)
                            out = banks(ps, 2 * (u % 2), 2)[:, c:e]
                            for a, (x, y) in enumerate(((q_hi, k_hi), (q_hi, k_lo), (q_lo, k_hi))):
                                mm = pe.matmul(out, x[h][:, q * P:(q + 1) * P], y[:, c:e], start=(a == 0), stop=(a == 2))
                        mm.then_inc(made, 1)

                    def turn(u):
                        pe.wait_ge(prob_done, base + u + 1)
                        for k in range(unit(u)[1] + 1):
                            mm = pe.transpose(banks(ps, 4, 2)[:, k * P:(k + 1) * P], prob[u % 3][:, k * P:(k + 1) * P], ident[:])
                        mm.then_inc(prob_turned, 1)

                    def values(u):
                        h, q = unit(u)
                        for k in range(q + 1):
                            mm = pe.matmul(banks(ps, 6, 2)[HD * h:HD * (h + 1), q * P:(q + 1) * P],
                                           v[s][:, k, HD * h:HD * (h + 1)], probT[u % 2][:, k * P:(k + 1) * P],
                                           start=(k == 0), stop=(k == q))
                        mm.then_inc(pv_done, 1)

                    pe.wait_ge(roped, 6 * (2 * i + s) + 6)
                    for t in range(2 * TT):
                        mm = pe.transpose(banks(ps, 0, 4)[:, t * P:(t + 1) * P], qk[s][:, t, :], ident[:])
                    mm.then_inc(turned, 1)
                    pe.wait_ge(split_done, 3 * (2 * i + s) + 3)
                    scores(0)
                    scores(1)
                    scores(2)
                    turn(0)
                    for u in range(UNITS):
                        if u + 3 < UNITS:
                            scores(u + 3)
                        pe.wait_ge(probT_done, base + u + 1)
                        if u + 1 < UNITS:
                            turn(u + 1)
                        values(u)
                    pe.wait_ge(pv_done, base + UNITS + 2)
                    pe.sem_inc(heads_free, 1)

        @block.scalar
        def _(act):
            act.wait_ge(zeroed, 4)
            with act.Fori(0, 2) as i:
                for s in range(2):
                    base = i * 2 * UNITS + s * UNITS

                    def exponent(u):
                        act.wait_ge(neg_done, base + u + 1)
                        x = prob[u % 3][:, 0:(unit(u)[1] + 1) * P]
                        act.activation(x, x, ACT.Exp, bias=neg[:, u:u + 1], accum_out=total[:, u:u + 1]).then_inc(exp_done, 1)

                    act.wait_ge(turned, 2 * i + s + 1)
                    for h in range(2):
                        rows = slice(HD * h, HD * (h + 1))
                        act.mul(q_hi[h][rows, :], banks(ps, 0, 2)[rows, :], SCALE).then_inc(hi_done, 1)
                    act.copy(k_hi[:], banks(ps, 2, 2)).then_inc(hi_done, 1)
                    exponent(0)
                    for u in range(UNITS):
                        if u + 1 < UNITS:
                            exponent(u + 1)
                        act.wait_ge(prob_turned, base + u + 4)
                        act.wait_ge(pv_done, base + u + 1)
                        w = (unit(u)[1] + 1) * P
                        act.copy(probT[u % 2][:, 0:w], banks(ps, 4, 2)[:, 0:w]).then_inc(probT_done, 1)
                    act.wait_ge(pv_done, base + UNITS + 2)
                    act.copy(mix_hi[:, ds(2 * i + s, 1), :], banks(ps, 6, 2)).then_inc(mix_hi_done, 1)

        @block.vector
        def _(dve):
            for x in (q_hi, q_lo):
                for h in range(2):
                    rows = slice(HD * (1 - h), HD * (2 - h))
                    dve.memset(x[h][rows, :].bitcast(F32), 0.0).then_inc(zeroed, 1)
            dve.wait_ge(zeroed, 4)
            dve.wait_ge(tables, 32)
            with dve.Fori(0, 2) as i:
                for s in range(2):
                    base = i * 2 * UNITS + s * UNITS

                    def score(u):
                        w = (unit(u)[1] + 1) * P
                        dve.wait_ge(made, base + u + 1)
                        dve.wait_ge(prob_turned, base + u + 1)
                        dve.memset(waited[:], 0.0)
                        dve.tensor_tensor_reduce(prob[u % 3][:, 0:w], banks(ps, 2 * (u % 2), 2)[:, 0:w],
                                                 bias[:, S - w:S], 1.0, NEG, ALU.add, ALU.max,
                                                 top[:, u:u + 1]).then_inc(scored, 1)
                        dve.wait_ge(scored, base + u + 1)
                        dve.tensor_scalar(neg[:, u:u + 1], top[:, u:u + 1], -1.0, None, ALU.mult).then_inc(neg_done, 1)

                    def normalise(u):
                        w = (unit(u)[1] + 1) * P
                        dve.wait_ge(exp_done, base + u + 1)
                        dve.reciprocal(inv[:, u:u + 1], total[:, u:u + 1]).then_inc(inv_done, 1)
                        dve.wait_ge(inv_done, base + u + 1)
                        dve.tensor_scalar(prob[u % 3][:, 0:w], prob[u % 3][:, 0:w], inv[:, u:u + 1], None,
                                          ALU.mult).then_inc(prob_done, 1)

                    for h in range(2):
                        rows = slice(HD * h, HD * (h + 1))
                        dve.wait_ge(hi_done, 3 * (2 * i + s) + h + 1)
                        dve.scalar_tensor_tensor(out=q_lo[h][rows, :], in0=banks(ps, 0, 2)[rows, :], scalar=SCALE,
                                                 in1=q_hi[h][rows, :].bitcast(F32), op0=ALU.mult,
                                                 op1=ALU.subtract).then_inc(split_done, 1)
                    dve.wait_ge(hi_done, 3 * (2 * i + s) + 3)
                    dve.tensor_tensor(k_lo[:], banks(ps, 2, 2), k_hi[:].bitcast(F32), ALU.subtract).then_inc(split_done, 1)
                    score(0)
                    for u in range(UNITS):
                        if u + 1 < UNITS:
                            score(u + 1)
                        normalise(u)
                    dve.wait_ge(mix_hi_done, 2 * i + s + 1)
                    dve.tensor_tensor(mix_lo[:, ds(2 * i + s, 1), :], banks(ps, 6, 2),
                                      mix_hi[:, ds(2 * i + s, 1), :].bitcast(F32), ALU.subtract).then_inc(mix_done, 1)



def signal(steps, sem):
    steps.wait()
    steps.eng.sem_inc(sem, 1)


def rotate(steps, x, out, table, tmp):
    e = steps.eng
    a, b = x[..., 0], x[..., 1]
    cos, sin = table
    for dst, u, w in ((0, a, cos), (1, b, sin), (2, b, cos), (3, a, sin)):
        steps.done(e.tensor_tensor(tmp[dst], u, w, ALU.mult))
    steps.wait()
    steps.done(e.tensor_tensor(out[..., 0], tmp[0], tmp[1], ALU.subtract))
    steps.done(e.tensor_tensor(out[..., 1], tmp[2], tmp[3], ALU.add))


def group_norm(steps, v_ready, root, nth, src, dst, stats, mv, rows, n):
    e = steps.eng
    for j in range(n):
        steps.done(e.bn_stats(stats[rows, j, :], src(j)))
    steps.wait()
    for j in range(n):
        steps.done(e.bn_aggr(mv[rows, j, 0:2], stats[rows, j, :]))
    steps.wait()
    col = lambda c: mv[rows, 0:n, c]
    steps.done(e.tensor_scalar(col(1), col(1), EPS, None, ALU.add))
    signal(steps, v_ready)
    e.wait_ge(root, nth)
    steps.then(e.reciprocal(col(3), col(2)))
    steps.then(e.tensor_tensor(col(4), col(3), col(3), ALU.mult))
    steps.then(e.tensor_tensor(col(4), col(4), col(1), ALU.mult))
    steps.then(e.tensor_scalar(col(4), col(4), -0.5, 1.5, ALU.mult, ALU.add))
    steps.then(e.tensor_tensor(col(3), col(3), col(4), ALU.mult))
    for j in range(n):
        steps.done(e.tensor_scalar(dst(j), src(j), mv[rows, j, 0:1], mv[rows, j, 3:4], ALU.subtract, ALU.mult))
    steps.wait()


def stage_prompt_retention(nc, io, ps, ident, mix_hi, mix_lo):
    st = Stage(nc, "ret")
    W2 = 2 * RV
    with st.ctx:
        rot = st.sb("rot", [P, 2, TT, RD])
        dmask = st.sb("dmask", [P, RH, P])
        dout = st.sb("dout", [P, 2, P])
        din, gch = st.sb("din", [P, RH]), st.sb("gch", [P, 2])
        gain = st.sb("gain", [P, RH * RV])
        q_in = [st.sb(f"q{a}", [P, TT, P]) for a in range(2)]
        k_in = [st.sb(f"k{a}", [P, TT, P]) for a in range(2)]
        v = [st.sb(f"v{a}", [P, TT, W2]) for a in range(2)]
        g = [st.sb(f"g{a}", [P, TT, W2]) for a in range(2)]
        eg = st.sb("eg", [P, TT, W2])
        q_rot, k_rot = st.sb("q_rot", [P, TT, P]), st.sb("k_rot", [P, TT, P])
        kd = st.sb("kd", [P, TT, P])
        qT, kT, qdT = (st.sb(n, [P, S]) for n in ("qT", "kT", "qdT"))
        sT = [st.sb(f"sT{h}", [P, S]) for h in range(2)]
        state = st.sb("state", [P, TT, P])
        on = [st.sb(f"on{h}", [P, S]) for h in range(2)]
        tmp_q = [qT[:, j * 512:(j + 1) * 512].rearrange("p (t j) -> p t j", t=TT) for j in range(2)] + \
                [qdT[:, j * 512:(j + 1) * 512].rearrange("p (t j) -> p t j", t=TT) for j in range(2)]
        tmp_k = [st.sb(f"tmp_k{j}", [P, TT, RD]) for j in range(4)]
        stats = st.sb("stats", [P, TT, 6])
        mv = st.sb("mv", [P, TT, 5])
        tables, gate_sum, gate_inv = st.sem("tables"), st.sem("gate_sum"), st.sem("gate_inv")
        loaded = [st.sem(f"loaded{a}") for a in range(2)]
        dve_s, pool_s, act_s, pe_s = (st.sem(n) for n in ("dve_steps", "pool_steps", "act_steps", "pe_steps"))
        (q_ready, k_ready, q_turned, k_turned, qT_done, kT_done, qd_done, kd_done, kv_made, states_done, sT_made,
         sT_done, o_made, v_ready, root, on_ready, o_turned, hi_done, exp_done, gate_done, mixed, state_put) = (
            st.sem(n) for n in (
                "q_ready", "k_ready", "q_turned", "k_turned", "qT_done", "kT_done", "qd_done", "kd_done", "kv_made",
                "states_done", "sT_made", "sT_done", "o_made", "v_ready", "root", "on_ready", "o_turned", "hi_done",
                "exp_done", "gate_done", "mixed", "state_put"))
        proj = io["proj"][0:S, :].rearrange("(t p) c -> p t c", p=P)
        QC, KC, VC, GC = 3 * AW, 3 * AW + RH * RD, 3 * AW + 2 * RH * RD, 3 * AW + 2 * RH * RD + RH * RV
        even_odd = lambda x: x.rearrange("p t (j e) -> p t j e", e=2)
        by_chunk = lambda x: x.rearrange("p (t c) -> p t c", t=TT)
        O_BANK = (2, 4)
        T_BANK = (6, 0)
        block = st.block()

        @block.sync
        def _(sp):
            for a in range(2):
                sp.dma_start(q_in[a][:], proj[:, :, QC + a * P:QC + (a + 1) * P]).then_inc(loaded[a], 16)
                sp.dma_start(k_in[a][:], proj[:, :, KC + a * P:KC + (a + 1) * P]).then_inc(loaded[a], 16)
                if a == 0:
                    for dst, n in ((rot[:].rearrange("p a b c -> p (a b c)"), "rot_p"),
                                   (dmask[:].rearrange("p a b -> p (a b)"), "dmask_p"),
                                   (dout[:].rearrange("p a b -> p (a b)"), "dout_p"), (din[:], "din_p"), (gch[:], "gchunk_p")):
                        sp.dma_start(dst, io[n]).then_inc(tables, 16)
                    sp.dma_start(gain[:], io["ret_gain"][0].partition_broadcast(P)).then_inc(tables, 16)
                sp.dma_start(v[a][:], proj[:, :, VC + a * W2:VC + (a + 1) * W2]).then_inc(loaded[a], 16)
                sp.dma_start(g[a][:], proj[:, :, GC + a * W2:GC + (a + 1) * W2]).then_inc(loaded[a], 16)
            for a in range(2):
                sp.wait_ge(states_done, a + 1)
                sp.dma_start(io["ret_prompt"][0, 0, 2 * a:2 * a + 2].rearrange("h d e -> (h d) e"),
                             state[:, TT - 1, :]).then_inc(state_put, 16)
            sp.wait_ge(state_put, 32)

        @block.gpsimd
        def _(pool):
            steps = Steps(pool, pool_s)
            pool.wait_ge(tables, 96)
            for a in range(2):
                pool.wait_ge(loaded[a], 64)
                if a:
                    pool.wait_ge(k_turned, a)
                    pool.wait_ge(kd_done, a)
                rotate(steps, even_odd(k_in[a][:]), even_odd(k_rot[:]), (rot[:, 0], rot[:, 1]), [x[:] for x in tmp_k])
                signal(steps, k_ready)
                pool.wait_ge(exp_done, a + 1)
                if a:
                    pool.wait_ge(mixed, 2 * a)
                steps.then(pool.tensor_scalar(eg[:], eg[:], 1.0, 1.0, ALU.add, ALU.mult))
                signal(steps, gate_sum)
                pool.wait_ge(gate_inv, a + 1)
                steps.then(pool.tensor_tensor(g[a][:], g[a][:], eg[:], ALU.mult))
                steps.then(pool.tensor_tensor(g[a][:], g[a][:], gain[:, a * W2:(a + 1) * W2].unsqueeze(1).broadcast_to([P, TT, W2]),
                                              ALU.mult))
                signal(steps, gate_done)

        @block.scalar
        def _(act):
            steps = Steps(act, act_s)
            for a in range(2):
                act.wait_ge(loaded[a], 64)
                if a:
                    act.wait_ge(gate_done, a)
                act.activation(eg[:], g[a][:], ACT.Exp, scale=-1.0).then_inc(exp_done, 1)
                act.wait_ge(q_turned, a + 1)
                act.copy(qT[:], banks(ps, 0, 2)).then_inc(qT_done, 1)
                act.wait_ge(k_turned, a + 1)
                act.mul(kT[:], banks(ps, 2, 2), RD ** -0.5).then_inc(kT_done, 1)
                for h in range(2):
                    n = 2 * a + h
                    act.wait_ge(v_ready, n + 1)
                    act.activation(mv[:, :, 2], mv[:, :, 1], ACT.Sqrt).then_inc(root, 1)
                    act.wait_ge(o_turned, n + 1)
                    act.copy(mix_hi[:, 4 + n, :], banks(ps, T_BANK[h], 2)).then_inc(hi_done, 1)

        @block.vector
        def _(dve):
            steps = Steps(dve, dve_s)
            dve.wait_ge(tables, 96)
            for a in range(2):
                dve.wait_ge(loaded[a], 64)
                if a:
                    dve.wait_ge(o_made, 2 * a)
                rotate(steps, even_odd(q_in[a][:]), even_odd(q_rot[:]), (rot[:, 0], rot[:, 1]), tmp_q)
                signal(steps, q_ready)
                dve.wait_ge(k_ready, a + 1)
                if a:
                    dve.wait_ge(kv_made, a)
                for h in range(2):
                    cols = slice(RD * h, RD * (h + 1))
                    steps.done(dve.tensor_scalar(kd[:, :, cols], k_rot[:, :, cols], din[:, 2 * a + h:2 * a + h + 1],
                                                 None, ALU.mult))
                signal(steps, kd_done)
                dve.wait_ge(qT_done, a + 1)
                steps.done(dve.tensor_tensor(by_chunk(qdT[:]), by_chunk(qT[:]),
                                             dout[:, a, :].unsqueeze(1).broadcast_to([P, TT, P]), ALU.mult))
                signal(steps, qd_done)
                dve.wait_ge(kv_made, a + 1)
                if a:
                    dve.wait_ge(state_put, 16 * a)
                kv = by_chunk(banks(ps, 4, 2))
                steps.then(dve.tensor_copy(state[:, 0, :], kv[:, 0, :]))
                for t in range(1, TT):
                    steps.then(dve.scalar_tensor_tensor(out=state[:, t, :], in0=state[:, t - 1, :], scalar=gch[:, a:a + 1],
                                                        in1=kv[:, t, :], op0=ALU.mult, op1=ALU.add))
                signal(steps, states_done)
                for h in range(2):
                    dve.wait_ge(sT_made, 2 * a + h + 1)
                    steps.done(dve.tensor_tensor(by_chunk(sT[h][:]), by_chunk(banks(ps, T_BANK[h], 2)),
                                                 dmask[:, 2 * a + h, :].unsqueeze(1).broadcast_to([P, TT, P]), ALU.mult))
                    signal(steps, sT_done)
                dve.wait_ge(exp_done, a + 1)
                dve.wait_ge(gate_sum, a + 1)
                steps.done(dve.reciprocal(eg[:], eg[:]))
                signal(steps, gate_inv)
                for h in range(2):
                    n = 2 * a + h
                    o = by_chunk(banks(ps, O_BANK[h], 2))
                    dst = by_chunk(on[h][:])
                    dve.wait_ge(o_made, n + 1)
                    group_norm(steps, v_ready, root, n + 1, lambda j: o[:, j, :], lambda j: dst[:, j, :],
                               stats, mv, slice(0, P), TT)
                    dve.wait_ge(gate_done, a + 1)
                    steps.done(dve.tensor_tensor(dst, dst, g[a][:, :, RV * h:RV * (h + 1)], ALU.mult))
                    signal(steps, on_ready)
                    dve.wait_ge(hi_done, n + 1)
                    steps.done(dve.tensor_tensor(mix_lo[:, 4 + n, :], banks(ps, T_BANK[h], 2),
                                                 mix_hi[:, 4 + n, :].bitcast(F32), ALU.subtract))
                    signal(steps, mixed)

        @block.tensor
        def _(pe):
            def turn(src, first, sem):
                for t in range(TT):
                    mm = pe.transpose(banks(ps, first, 2)[:, t * P:(t + 1) * P], src(t), ident[:])
                mm.then_inc(sem, 1)

            for a in range(2):
                if a:
                    pe.wait_ge(mixed, 2 * a)
                pe.wait_ge(q_ready, a + 1)
                turn(lambda t: q_rot[:, t, :], 0, q_turned)
                pe.wait_ge(k_ready, a + 1)
                turn(lambda t: k_rot[:, t, :], 2, k_turned)
                pe.wait_ge(kd_done, a + 1)
                for h in range(2):
                    for t in range(TT):
                        mm = pe.matmul(banks(ps, 4, 2)[RD * h:RD * (h + 1), t * P:(t + 1) * P],
                                       kd[:, t, RD * h:RD * (h + 1)], v[a][:, t, RV * h:RV * (h + 1)],
                                       start=True, stop=True)
                mm.then_inc(kv_made, 1)
                pe.wait_ge(qT_done, a + 1)
                pe.wait_ge(kT_done, a + 1)
                pe.wait_ge(qd_done, a + 1)
                for h in range(2):
                    rows = slice(RD * h, RD * (h + 1))
                    for t in range(TT):
                        cols = slice(t * P, (t + 1) * P)
                        mm = pe.matmul(banks(ps, T_BANK[h], 2)[:, cols], kT[rows, cols], qT[rows, cols], start=True, stop=True)
                    mm.then_inc(sT_made, 1)
                pe.wait_ge(states_done, a + 1)
                for h in range(2):
                    rows = slice(RD * h, RD * (h + 1))
                    pe.wait_ge(sT_done, 2 * a + h + 1)
                    for t in range(TT):
                        cols = slice(t * P, (t + 1) * P)
                        out = banks(ps, O_BANK[h], 2)[:, cols]
                        mm = pe.matmul(out, sT[h][:, cols], v[a][:, t, RV * h:RV * (h + 1)], start=True, stop=(t == 0))
                        if t:
                            mm = pe.matmul(out, qdT[rows, cols], state[rows, t - 1, :], start=False, stop=True)
                    mm.then_inc(o_made, 1)
                for h in range(2):
                    pe.wait_ge(on_ready, 2 * a + h + 1)
                    turn(lambda t: on[h][:, t * P:(t + 1) * P], T_BANK[h], o_turned)



def stage_sample_heads(nc, io, ps, ident, mix_s, q_blocks, kT_new):
    st = Stage(nc, "smp")
    QC, KC, VC, GC = 3 * AW, 3 * AW + RH * RD, 3 * AW + 2 * RH * RD, 3 * AW + 2 * RH * RD + RH * RV
    with st.ctx:
        x, lo_rows = st.sb("x", [NS, IN_W]), st.sb("lo_rows", [NS, IN_W])
        rope = st.sb("rope", [NS, 2, 2 * H, 8])
        rot = st.sb("rot", [NS, 2, 2 * RH * RD // 2])
        dmask = st.sb("dmask", [NS, RH * NS])
        dout = st.sb("dout", [P, RH, 4, NS])
        din = st.sb("din", [NS, RH, 4, P])
        gain = st.sb("gain", [NS, RH * RV])
        state = st.sb("state", [P, 4, RH, RV])
        tmp = [st.sb(f"tmp{j}", [NS, 256]) for j in range(4)]
        turned_qk = st.sb("rotated", [NS, 1, 2 * RH * RD])
        twice = st.sb("twice", [NS, 2 * RH, 2, RD])
        qT, kT = st.sb("qT", [P, RH, NS]), st.sb("kT", [P, RH, NS])
        q_masked = st.sb("q_masked", [P, RH, 4, NS])
        k_masked = st.sb("k_masked", [NS, RH, 4, P])
        sT = st.sb("sT", [NS, RH * NS])
        on = st.sb("on", [NS, RH * RV])
        eg = st.sb("eg", [NS, RH * RV])
        stats, mv = st.sb("stats", [NS, RH, 6]), st.sb("mv", [NS, RH, 5])
        (tables, x_in, s_in, dve_s, roped, put, rotated, att_turned, ret_turned, qT_done, sT_made, sT_done, kv_made, o_made,
         v_ready, root, on_ready, o_turned, hi_done, exp_done, state_done, g_ready, all_masked) = (st.sem(n) for n in (
            "tables", "x_in", "s_in", "dve_steps", "roped", "put", "rotated", "att_turned", "ret_turned", "qT_done", "sT_made",
            "sT_done", "kv_made", "o_made", "v_ready", "root", "on_ready", "o_turned", "hi_done", "exp_done", "state_done",
            "g_ready", "all_masked"))
        flat = lambda t: t[:].rearrange("p a b -> p (a b)")
        flat4 = lambda t: t[:].rearrange("p a b c -> p (a b c)")
        st_in = io["state_ret"][0].rearrange("(q b) h d e -> b d q h e", b=2)
        st_out = io["ret_sample"][0].rearrange("(q b) h d e -> b d q h e", b=2)
        block = st.block()

        @block.sync
        def _(sp):
            sp.dma_start(x[:], io["proj"][S:S + NS, :]).then_inc(x_in, 16)
            sp.dma_start(lo_rows[:], io["proj"][S + NS:S + P, :]).then_inc(x_in, 16)
            sp.dma_start(flat4(rope), io["rope_s"]).then_inc(tables, 16)
            for dst, n in ((flat(rot), "rot_s"), (dmask[:], "dmask_s"), (flat4(dout), "dout_s"), (flat4(din), "din_s")):
                sp.dma_start(dst, io[n]).then_inc(tables, 16)
            sp.dma_start(gain[:], io["ret_gain"][0].partition_broadcast(NS)).then_inc(tables, 16)
            for b in range(2):
                for q in range(4):
                    sp.dma_start(state[RD * b:RD * (b + 1), q], st_in[b, :, q]).then_inc(s_in, 16)
            sp.wait_ge(roped, 1)
            sp.dma_start(io["k_sample"].rearrange("o b t h d -> (o b t) (h d)"), x[:, AW:2 * AW]).then_inc(put, 16)
            sp.dma_start(io["v_sample"].rearrange("o b t h d -> (o b t) (h d)"), x[:, 2 * AW:3 * AW]).then_inc(put, 16)
            sp.wait_ge(state_done, 1)
            for b in range(2):
                for q in range(4):
                    sp.dma_start(st_out[b, :, q], state[RD * b:RD * (b + 1), q]).then_inc(put, 16)
            sp.wait_ge(put, 16 * 10)

        @block.vector
        def _(dve):
            steps = Steps(dve, dve_s)
            steps.done(dve.memset(q_blocks[:], 0.0))
            dve.wait_ge(x_in, 32)
            steps.then(dve.tensor_tensor(x[:], x[:], lo_rows[:], ALU.add))
            signal(steps, g_ready)
            dve.wait_ge(tables, 96)
            heads = x[:, 0:2 * AW].rearrange("p (h d) -> p h d", d=HD)
            a, b = heads[:, :, 0:8], heads[:, :, 8:16]
            t8 = [t[:, 0:128].rearrange("p (h j) -> p h j", j=8) for t in tmp]
            for dst, u, w in ((0, a, 0), (1, b, 1), (2, b, 0), (3, a, 1)):
                steps.done(dve.tensor_tensor(t8[dst], u, rope[:, w], ALU.mult))
            steps.wait()
            steps.done(dve.tensor_tensor(a, t8[0], t8[1], ALU.subtract))
            steps.done(dve.tensor_tensor(b, t8[2], t8[3], ALU.add))
            signal(steps, roped)
            qk = x[:, QC:VC].rearrange("p (o j e) -> p o j e", o=1, e=2)
            rotate(steps, qk, turned_qk[:].rearrange("p o (j e) -> p o j e", e=2),
                   (rot[:, 0:1], rot[:, 1:2]), [t[:].unsqueeze(1) for t in tmp])
            steps.wait()
            rr = turned_qk[:, 0].rearrange("p (h d) -> p h d", d=RD)
            steps.done(dve.tensor_copy(twice[:], rr.unsqueeze(2).broadcast_to([NS, 2 * RH, 2, RD])))
            signal(steps, rotated)
            for h in range(RH):
                dup = twice[:, RH + h].rearrange("p a d -> p (a d)")
                steps.done(dve.tensor_tensor(k_masked[:, h], dup.unsqueeze(1).broadcast_to([NS, 4, P]), din[:, h], ALU.mult))
            dve.wait_ge(att_turned, 1)
            for h in range(H):
                rows = slice(HD * (h % 2), HD * (h % 2 + 1))
                src = ps[rows, 0, (h // 2) * NS:(h // 2 + 1) * NS].rearrange("p (b t) -> p b t", b=DB)
                steps.done(dve.tensor_scalar(q_blocks[rows, :, h // 2, h * DS:(h + 1) * DS], src, SCALE, None, ALU.mult))
            steps.done(dve.tensor_copy(kT_new[:], ps[:, 0, 4 * NS:8 * NS].rearrange("p (c n) -> p c n", n=NS)))
            dve.wait_ge(ret_turned, 1)
            steps.done(dve.tensor_copy(flat(qT), ps[:, 1, 0:RH * NS]))
            steps.done(dve.tensor_scalar(flat(kT), ps[:, 1, RH * NS:2 * RH * NS], RD ** -0.5, None, ALU.mult))
            steps.wait()
            for h in range(RH):
                steps.done(dve.tensor_tensor(q_masked[:, h], qT[:, h].unsqueeze(1).broadcast_to([P, 4, NS]), dout[:, h], ALU.mult))
            signal(steps, qT_done)
            dve.wait_ge(sT_made, 1)
            steps.done(dve.tensor_tensor(sT[:], ps[0:NS, 2, 0:RH * NS], dmask[:], ALU.mult))
            signal(steps, sT_done)
            dve.wait_ge(exp_done, 1)
            steps.then(dve.tensor_scalar(eg[:], eg[:], 1.0, None, ALU.add))
            steps.then(dve.reciprocal(eg[:], eg[:]))
            steps.then(dve.tensor_tensor(eg[:], eg[:], x[:, GC:], ALU.mult))
            steps.then(dve.tensor_tensor(eg[:], eg[:], gain[:], ALU.mult))
            dve.wait_ge(o_made, 1)
            o = ps[0:NS, 3, :].rearrange("p (h e) -> p h e", e=RV)
            oo = on[:].rearrange("p (h e) -> p h e", e=RV)
            group_norm(steps, v_ready, root, 1, lambda j: o[:, j, :], lambda j: oo[:, j, :], stats, mv, slice(0, NS), RH)
            steps.done(dve.tensor_tensor(on[:], on[:], eg[:], ALU.mult))
            signal(steps, on_ready)
            dve.wait_ge(kv_made, 1)
            for h in range(RH):
                steps.done(dve.scalar_tensor_tensor(out=state[:, :, h, :], in0=state[:, :, h, :], scalar=GCHUNK_S[h],
                                                    in1=ps[:, 4:8, h * RV:(h + 1) * RV], op0=ALU.mult, op1=ALU.add))
            signal(steps, state_done)
            dve.wait_ge(hi_done, 1)
            src = ps[:, 2, 0:RH * NS].rearrange("p (h n) -> p h n", n=NS)
            steps.then(dve.tensor_tensor(mix_s[:, 4:8, NS:P], src, mix_s[:, 4:8, 0:NS].bitcast(F32), ALU.subtract))

        @block.scalar
        def _(act):
            act.wait_ge(g_ready, 1)
            act.activation(eg[:], x[:, GC:], ACT.Exp, scale=-1.0).then_inc(exp_done, 1)
            act.wait_ge(v_ready, 1)
            act.activation(mv[:, :, 2], mv[:, :, 1], ACT.Sqrt).then_inc(root, 1)
            act.wait_ge(o_turned, 1)
            act.copy(mix_s[:, 4:8, 0:NS], ps[:, 2, 0:RH * NS].rearrange("p (h n) -> p h n", n=NS)).then_inc(hi_done, 1)

        @block.tensor
        def _(pe):
            pe.wait_ge(roped, 1)
            for c in range(8):
                mm = pe.transpose(ps[:, 0, c * NS:(c + 1) * NS], x[:, c * P:(c + 1) * P], ident[0:NS, 0:NS])
            mm.then_inc(att_turned, 1)
            pe.wait_ge(rotated, 1)
            for c in range(2 * RH):
                mm = pe.transpose(ps[:, 1, c * NS:(c + 1) * NS], twice[:, c].rearrange("p a d -> p (a d)"), ident[0:NS, 0:NS])
            mm.then_inc(ret_turned, 1)
            pe.wait_ge(qT_done, 1)
            pe.wait_ge(s_in, 128)
            vcols = lambda h: x[:, VC + h * RV:VC + (h + 1) * RV]
            for h in range(RH):
                mm = pe.matmul(ps[0:NS, 2, h * NS:(h + 1) * NS], kT[0:RD, h, :], qT[0:RD, h, :], start=True, stop=True)
            mm.then_inc(sT_made, 1)
            for h in range(RH):
                for b in range(4):
                    mm = pe.matmul(ps[:, 4 + b, h * RV:(h + 1) * RV], k_masked[:, h, b, :], vcols(h), start=True, stop=True)
            mm.then_inc(kv_made, 1)
            pe.wait_ge(sT_done, 1)
            for h in range(RH):
                out = ps[0:NS, 3, h * RV:(h + 1) * RV]
                pe.matmul(out, sT[:, h * NS:(h + 1) * NS], vcols(h), start=True, stop=False)
                for b in range(4):
                    mm = pe.matmul(out, q_masked[:, h, b, :], state[:, b, h, :], start=False, stop=(b == 3))
            mm.then_inc(o_made, 1)
            pe.wait_ge(on_ready, 1)
            for h in range(RH):
                mm = pe.transpose(ps[:, 2, h * NS:(h + 1) * NS], on[:, h * RV:(h + 1) * RV], ident[0:NS, 0:NS])
            mm.then_inc(o_turned, 1)



def stage_sample_attention(nc, io, ps, ident, mix_s, q_blocks, kT_new):
    st = Stage(nc, "cache")
    CHUNKS = ((0, 4), (4, 4), (8, 2))
    with st.ctx:
        bias = st.sb("bias", [P, NKEYS])
        K = [st.sb(f"K{b}", [P, KTILES, AW]) for b in range(2)]
        V = [st.sb(f"V{b}", [P, KTILES, AW]) for b in range(2)]
        v_new = [st.sb(f"v_new{b}", [DS, AW]) for b in range(2)]
        q_now = st.sb("q_now", [P, 2, 4, NS])
        k_now = st.sb("k_now", [P, 4, 2 * DS])
        kT = [st.sb(f"kT{s}", [P, 4, CH]) for s in range(2)]
        prob = st.sb("prob", [P, NKEYS])
        probT = st.sb("probT", [P, KTILES + 1, P])
        rows = st.sb("rows", [P, AW])
        top, neg, total, inv, waited = (st.sb(n, [P, 1]) for n in ("top", "neg", "total", "inv", "waited"))
        mix_f = st.sb("mix_f", [P, 4, NS])
        k_in, v_in = ([st.sem(f"{n}_in{b}") for b in range(2)] for n in "kv")
        (tables, k_free, v_free, q_staged, turned, kT_act, kT_dve, scored, s_made, neg_done, exp_done, inv_done, p_turned,
         pT_act, pT_dve, pv_made, rows_done, rows_turned, out_act, out_dve, hi_done, mixed) = (st.sem(n) for n in (
            "tables", "k_free", "v_free", "q_staged", "turned", "kT_act", "kT_dve", "scored", "s_made", "neg_done", "exp_done",
            "inv_done", "p_turned", "pT_act", "pT_dve", "pv_made", "rows_done", "rows_turned", "out_act", "out_dve",
            "hi_done", "mixed"))
        v_put = io["v_sample"].rearrange("o b t h d -> t (o b) (h d)")
        block = st.block()

        @block.sync
        def _(sp):
            sp.dma_start(bias[:], io["bias_s"]).then_inc(tables, 16)
            with sp.Fori(0, 4) as i:
                for b in range(2):
                    seq = sp.snap(2 * i + b)
                    sp.wait_ge(k_free, 2 * i + b + 1)
                    for cache, dst, sem in ((io["cache_k"], K[b], k_in[b]), (io["cache_v"], V[b], v_in[b])):
                        if sem is v_in[b]:
                            sp.wait_ge(v_free, 2 * i + b + 1)
                        src = cache[0, ds(seq, 1)].rearrange("o n h d -> (o n) (h d)")
                        old = src[0:OLD, :].rearrange("(j g r) c -> j g r c", g=16, r=16)
                        for j in range(6):
                            sp.dma_start(dst[:, j, :], old[j, :, 0:8]).then_inc(sem, 16)
                        sp.dma_start(dst[:, 6:, :], src[OLD:, :].rearrange("(j p) c -> p j c", p=P)).then_inc(sem, 16)
                    sp.dma_start(v_new[b][:], v_put[:, ds(seq, 1), :]).then_inc(v_in[b], 16)

        @block.tensor
        def _(pe):
            pe.sem_inc(k_free, 2)
            pe.sem_inc(v_free, 2)
            with pe.Fori(0, 4) as i:
                def turn(n):
                    b, (first, count) = n // 3, CHUNKS[n % 3]
                    if n % 3 == 0:
                        pe.wait_ge(k_in[b], 16 * 7 * i + 16 * 7)
                    for c in range(4):
                        for j in range(count):
                            mm = pe.transpose(ps[:, c, j * P:(j + 1) * P], K[b][:, first + j, c * P:(c + 1) * P], ident[:])
                    mm.then_inc(turned, 1)

                def scores(n):
                    b, (first, count) = n // 3, CHUNKS[n % 3]
                    w = count * P + (DS if n % 3 == 2 else 0)
                    if n == 0:
                        pe.wait_ge(q_staged, 2 * i + 2)
                    for c in range(4):
                        mm = pe.matmul(ps[NS * b:NS * (b + 1), 4 + n % 3, 0:w], q_now[:, b, c, :], kT[n % 2][:, c, 0:w],
                                       start=(c == 0), stop=(c == 3))
                    mm.then_inc(scored, 1)

                turn(0)
                for n in range(6):
                    pe.wait_ge(kT_act, 6 * i + n + 1)
                    pe.wait_ge(kT_dve, 6 * i + n + 1)
                    if n + 1 < 6:
                        turn(n + 1)
                    scores(n)
                    if n % 3 == 2:
                        pe.wait_ge(scored, 6 * i + n + 1)
                        pe.sem_inc(k_free, 1)
                pe.wait_ge(exp_done, i + 1)
                for j in range(KTILES + 1):
                    w = P if j < KTILES else DS
                    out = ps[:, j // 4, (j % 4) * P:(j % 4 + 1) * P] if j < KTILES else ps[0:DS, 3, 0:P]
                    mm = pe.transpose(out, prob[:, j * P:j * P + w], ident[:])
                mm.then_inc(p_turned, 1)
                pe.wait_ge(pT_act, 2 * i + 2)
                pe.wait_ge(pT_dve, 2 * i + 2)
                for b in range(2):
                    cols = slice(NS * b, NS * (b + 1))
                    pe.wait_ge(v_in[b], 16 * 8 * i + 16 * 8)
                    for j in range(KTILES):
                        pe.matmul(ps[cols, 7, :], probT[:, j, cols], V[b][:, j, :], start=(j == 0), stop=False)
                    mm = pe.matmul(ps[cols, 7, :], probT[0:DS, KTILES, cols], v_new[b][:], start=False, stop=True)
                    mm.then_inc(pv_made, 1)
                pe.wait_ge(pv_made, 2 * i + 2)
                pe.sem_inc(v_free, 2)
                pe.wait_ge(rows_done, i + 1)
                for c in range(4):
                    mm = pe.transpose(ps[:, 4, c * P:(c + 1) * P], rows[:, c * P:(c + 1) * P], ident[:])
                mm.then_inc(rows_turned, 1)

        def head_rows(i, h):
            part = slice(HD * (h % 2), HD * (h % 2 + 1))
            src = ps[part, 4, (h // 2) * P:(h // 2 + 1) * P].rearrange("p (b h t) -> p b h t", b=2, t=DS)[:, :, h, :]
            dst = mix_f[part, h // 2, ds(i * 2 * DS, 2 * DS)].rearrange("p (b t) -> p b t", b=2)
            return dst, src

        @block.scalar
        def _(act):
            with act.Fori(0, 4) as i:
                act.copy(q_now[:], q_blocks[:, ds(2 * i, 2)]).then_inc(q_staged, 1)
                act.copy(k_now[:], kT_new[:, :, ds(i * 2 * DS, 2 * DS)]).then_inc(q_staged, 1)
                for n in range(6):
                    w = CHUNKS[n % 3][1] * P
                    act.wait_ge(turned, 6 * i + n + 1)
                    act.copy(kT[n % 2][:, 0:2, 0:w], ps[:, 0:2, 0:w]).then_inc(kT_act, 1)
                act.wait_ge(neg_done, i + 1)
                act.activation(prob[:], prob[:], ACT.Exp, bias=neg[:], accum_out=total[:]).then_inc(exp_done, 1)
                act.wait_ge(p_turned, i + 1)
                act.copy(probT[:, 0:4, :], ps[:, 0, :].rearrange("p (j n) -> p j n", n=P)).then_inc(pT_act, 1)
                act.copy(probT[:, 4:8, :], ps[:, 1, :].rearrange("p (j n) -> p j n", n=P)).then_inc(pT_act, 1)
                act.wait_ge(rows_turned, i + 1)
                for h in range(0, H, 2):
                    dst, src = head_rows(i, h)
                    act.copy(dst, src).then_inc(out_act, 1)
                act.wait_ge(out_act, 4 * i + 4)
            act.wait_ge(out_dve, 16)
            act.copy(mix_s[:, 0:4, 0:NS], mix_f[:]).then_inc(hi_done, 1)

        @block.vector
        def _(dve):
            dve.wait_ge(tables, 16)
            with dve.Fori(0, 4) as i:
                for n in range(6):
                    w = CHUNKS[n % 3][1] * P
                    dve.wait_ge(turned, 6 * i + n + 1)
                    copy = dve.tensor_copy(kT[n % 2][:, 2:4, 0:w], ps[:, 2:4, 0:w])
                    if n % 3 == 2:
                        b = n // 3
                        dve.wait_ge(q_staged, 2 * i + 2)
                        copy = dve.tensor_copy(kT[n % 2][:, :, w:w + DS], k_now[:, :, b * DS:(b + 1) * DS])
                    copy.then_inc(kT_dve, 1)
                dve.wait_ge(scored, 6 * i + 6)
                dve.memset(waited[:], 0.0)
                dve.tensor_tensor_reduce(prob[:], banks(ps, 4, 3)[:, 0:NKEYS], bias[:], 1.0, NEG, ALU.add, ALU.max,
                                         top[:]).then_inc(s_made, 1)
                dve.wait_ge(s_made, i + 1)
                dve.tensor_scalar(neg[:], top[:], -1.0, None, ALU.mult).then_inc(neg_done, 1)
                dve.wait_ge(exp_done, i + 1)
                dve.reciprocal(inv[:], total[:]).then_inc(inv_done, 1)
                dve.wait_ge(p_turned, i + 1)
                dve.tensor_copy(probT[:, 8:10, :], ps[:, 2, 0:2 * P].rearrange("p (j n) -> p j n", n=P)).then_inc(pT_dve, 1)
                dve.tensor_copy(probT[0:DS, 10, :], ps[0:DS, 3, 0:P]).then_inc(pT_dve, 1)
                dve.wait_ge(pv_made, 2 * i + 2)
                dve.wait_ge(inv_done, i + 1)
                dve.tensor_scalar(rows[:], ps[:, 7, :], inv[:], None, ALU.mult).then_inc(rows_done, 1)
                dve.wait_ge(out_act, 4 * i + 4)
                for h in range(1, H, 2):
                    dst, src = head_rows(i, h)
                    dve.tensor_copy(dst, src).then_inc(out_dve, 1)
                dve.wait_ge(out_dve, 4 * i + 4)
            dve.wait_ge(hi_done, 1)
            dve.tensor_tensor(mix_s[:, 0:4, NS:P], mix_f[:], mix_s[:, 0:4, 0:NS].bitcast(F32), ALU.subtract).then_inc(mixed, 1)



def stage_mlp(nc, io, ps, ident, z_hi, z_lo, zs, y, ys):
    st = Stage(nc, "mlp")
    J = GF // P
    turned_s = lambda ps: ps[:, 4, GF:GF + J * P].rearrange("p (j n) -> p j n", n=P)[:, :, 0:NS]
    MAIN = 2 * J
    OUTS = 2 * (TT + 1)
    with st.ctx:
        w1_raw, w2_raw = st.sb("w1_raw", [P, KT, GF]), st.sb("w2_raw", [P, J, D])
        w1_hi, w1_lo = (st.sb(n, [P, KT, GF], F32R) for n in ("w1_hi", "w1_lo"))
        w2_hi, w2_lo = (st.sb(n, [P, J, D], F32R) for n in ("w2_hi", "w2_lo"))
        h_hi, h_lo = ([st.sb(f"{n}{s}", [P, J, S], F32R) for s in range(2)] for n in ("h_hi", "h_lo"))
        hs = [st.sb(f"hs{s}", [P, J, P], F32R) for s in range(2)]
        pos = [st.sb(f"pos{s}", [P, CH]) for s in range(2)]
        lo_part, hid_s = st.sb("lo_part", [NS, GF]), st.sb("hid_s", [P, GF])
        (w1_in, w2_in, w1_free, w2_free, w1_hi_done, w2_hi_done, w1_ready, w2_ready, made1, relu_done, sq_done, h_hi_done,
         h_ready, s_made, s_lo, s_sum, hid_done, s_turned, hs_hi, hs_ready, made2, added, h_free, zeroed) = (st.sem(n) for n in (
            "w1_in", "w2_in", "w1_free", "w2_free", "w1_hi_done", "w2_hi_done", "w1_ready", "w2_ready", "made1", "relu_done",
            "sq_done", "h_hi_done", "h_ready", "s_made", "s_lo", "s_sum", "hid_done", "s_turned", "hs_hi", "hs_ready",
            "made2", "added", "h_free", "zeroed"))
        w1v = io["w_ff1"].rearrange("o (k p) n -> p (o k) n", p=P)
        w2v = io["w_ff2"].rearrange("o (j p) n -> p (o j) n", p=P)
        block = st.block()


        @block.sync
        def _(sp):
            with sp.Fori(0, NG) as g:
                col, tile = sp.snap(g * GF), sp.snap(g * J)
                sp.wait_ge(w1_ready, g + 1)
                sp.dma_start(w1_raw[:], w1v[:, :, ds(col, GF)]).then_inc(w1_in, 16)
                sp.wait_ge(w2_ready, g + 1)
                sp.dma_start(w2_raw[:], w2v[:, ds(tile, J), :]).then_inc(w2_in, 16)

        @block.gpsimd
        def _(pool):
            pool.sem_inc(w1_ready, 1)
            pool.sem_inc(w2_ready, 1)
            pool.memset(y[:], 0.0).then_inc(zeroed, 1)
            pool.memset(ys[:], 0.0).then_inc(zeroed, 1)
            pool.memset(hid_s[:], 0.0).then_inc(zeroed, 1)

            def split_lo(lo, raw, hi, hi_done, ready, g):
                pool.wait_ge(hi_done, g + 1)
                pool.tensor_tensor(lo[:], raw[:], hi[:].bitcast(F32), ALU.subtract).then_inc(ready, 1)

            def square(g, s, u):
                j, half = divmod(u, 2)
                pool.wait_ge(relu_done, MAIN * g + u + 1)
                x = pos[u % 2][:]
                pool.tensor_tensor(x, x, x, ALU.mult).then_inc(sq_done, 1)

            def group(g, s, last=False):
                for u in range(MAIN):
                    square(g, s, u)
                if not last:
                    split_lo(w1_lo, w1_raw, w1_hi, w1_hi_done, w1_ready, g + 1)
                split_lo(w2_lo, w2_raw, w2_hi, w2_hi_done, w2_ready, g)

            split_lo(w1_lo, w1_raw, w1_hi, w1_hi_done, w1_ready, 0)
            with pool.Fori(0, NG // 2 - 1) as i:
                for s in range(2):
                    group(2 * i + s, s)
            group(NG - 2, 0)
            group(NG - 1, 1, last=True)

        @block.scalar
        def _(act):
            def split_hi(hi, raw, raw_in, free, hi_done, g):
                act.wait_ge(raw_in, 16 * g + 16)
                act.wait_ge(free, g + 1)
                act.copy(hi[:], raw[:]).then_inc(hi_done, 1)

            def hidden(g, s, u):
                j, half = divmod(u, 2)
                act.wait_ge(sq_done, MAIN * g + u + 1)
                act.copy(h_hi[s][:, j, half * CH:(half + 1) * CH], pos[u % 2][:]).then_inc(h_hi_done, 1)

            def group(g, s, last=False):
                for u in range(MAIN):
                    act.wait_ge(made1, MAIN * g + u + 1)
                    act.wait_ge(h_ready, MAIN * g + u + 1)
                    act.activation(pos[u % 2][:], ps[:, u, :], ACT.Relu).then_inc(relu_done, 1)
                    if u == 0:
                        act.wait_ge(h_free, g + 1)
                    if u:
                        hidden(g, s, u - 1)
                hidden(g, s, MAIN - 1)
                act.wait_ge(s_made, g + 1)
                act.copy(lo_part[:], ps[NS:P, 4, 0:GF]).then_inc(s_lo, 1)
                if not last:
                    split_hi(w1_hi, w1_raw, w1_in, w1_free, w1_hi_done, g + 1)
                act.wait_ge(s_turned, g + 1)
                act.copy(hs[s][:, :, 0:NS], turned_s(ps)).then_inc(hs_hi, 1)
                split_hi(w2_hi, w2_raw, w2_in, w2_free, w2_hi_done, g)

            split_hi(w1_hi, w1_raw, w1_in, w1_free, w1_hi_done, 0)
            with act.Fori(0, NG // 2 - 1) as i:
                for s in range(2):
                    group(2 * i + s, s)
            group(NG - 2, 0)
            group(NG - 1, 1, last=True)

        @block.vector
        def _(dve):
            dve.sem_inc(h_ready, 2)
            dve.sem_inc(added, 3)
            dve.sem_inc(hs_ready, 1)
            dve.wait_ge(zeroed, 3)

            def hidden(g, s):
                for u in range(MAIN):
                    j, half = divmod(u, 2)
                    cols = slice(half * CH, (half + 1) * CH)
                    dve.wait_ge(h_hi_done, MAIN * g + u + 1)
                    dve.tensor_tensor(h_lo[s][:, j, cols], pos[u % 2][:], h_hi[s][:, j, cols].bitcast(F32),
                                      ALU.subtract).then_inc(h_ready, 1)
                dve.wait_ge(s_lo, g + 1)
                dve.tensor_tensor(hid_s[0:NS, :], ps[0:NS, 4, 0:GF], lo_part[:], ALU.add).then_inc(s_sum, 1)
                dve.wait_ge(s_sum, g + 1)
                dve.scalar_tensor_tensor(out=hid_s[0:NS, :], in0=hid_s[0:NS, :], scalar=0.0, in1=hid_s[0:NS, :], op0=ALU.max,
                                         op1=ALU.mult).then_inc(hid_done, 1)

            def hidden_sample(g, s):
                dve.wait_ge(hs_hi, g + 1)
                dve.tensor_tensor(hs[s][:, :, NS:P], turned_s(ps),
                                  hs[s][:, :, 0:NS].bitcast(F32), ALU.subtract).then_inc(hs_ready, 1)

            def add(g):
                for o in range(OUTS):
                    t, c = divmod(o, 2)
                    cols = slice(c * CH, (c + 1) * CH)
                    dst = y[:, t, cols] if t < TT else ys[:, cols]
                    dve.wait_ge(made2, OUTS * g + o + 1)
                    dve.tensor_tensor(dst, dst, ps[:, 5 + o % 3, :], ALU.add).then_inc(added, 1)
                dve.wait_ge(added, OUTS * g + OUTS + 3)

            hidden(0, 0)
            hidden_sample(0, 0)
            with dve.Fori(0, NG // 2 - 1) as i:
                for s in range(2):
                    g = 2 * i + s
                    hidden(g + 1, 1 - s)
                    add(g)
                    hidden_sample(g + 1, 1 - s)
            hidden(NG - 1, 1)
            add(NG - 2)
            hidden_sample(NG - 1, 1)
            add(NG - 1)

        @block.tensor
        def _(pe):
            pe.sem_inc(w1_free, 1)
            pe.sem_inc(w2_free, 1)
            pe.sem_inc(h_free, 2)

            def first(g, s):
                pe.wait_ge(w1_ready, g + 2)
                for u in range(MAIN):
                    j, half = divmod(u, 2)
                    rows = slice(half * CH, (half + 1) * CH)
                    for k in range(KT):
                        for a, (w, z) in enumerate(((w1_hi, z_hi), (w1_hi, z_lo), (w1_lo, z_hi))):
                            mm = pe.matmul(ps[:, u, :], w[:, k, j * P:(j + 1) * P], z[:, k, rows],
                                           start=(k == 0 and a == 0), stop=(k == KT - 1 and a == 2))
                    mm.then_inc(made1, 1)
                pe.wait_ge(hs_ready, g + 1)
                for k in range(KT):
                    for a, w in enumerate((w1_hi, w1_lo)):
                        mm = pe.matmul(ps[:, 4, 0:GF], zs[:, k, :], w[:, k, :], start=(k == 0 and a == 0),
                                       stop=(k == KT - 1 and a == 1))
                mm.then_inc(s_made, 1)
                pe.wait_ge(s_made, g + 1)
                pe.sem_inc(w1_free, 1)

            def turn_sample(g, s):
                pe.wait_ge(hid_done, g + 1)
                for j in range(J):
                    mm = pe.transpose(ps[:, 4, GF + j * P:GF + (j + 1) * P], hid_s[:, j * P:(j + 1) * P], ident[:])
                mm.then_inc(s_turned, 1)

            def second(g, s):
                pe.wait_ge(w2_ready, g + 2)
                pe.wait_ge(h_ready, MAIN * g + MAIN + 2)
                for o in range(OUTS):
                    t, c = divmod(o, 2)
                    cols = slice(c * CH, (c + 1) * CH)
                    out = ps[:, 5 + o % 3, :]
                    pe.wait_ge(added, OUTS * g + o + 1)
                    if t < TT:
                        parts = [(h[s][:, j, t * P:(t + 1) * P], w[:, j, cols]) for j in range(J)
                                 for h, w in ((h_hi, w2_hi), (h_hi, w2_lo), (h_lo, w2_hi))]
                    else:
                        if c == 0:
                            pe.wait_ge(hs_ready, g + 2)
                        parts = [(hs[s][:, j, :], w[:, j, cols]) for j in range(J) for w in (w2_hi, w2_lo)]
                    for a, (h, w) in enumerate(parts):
                        mm = pe.matmul(out, h, w, start=(a == 0), stop=(a == len(parts) - 1))
                    mm.then_inc(made2, 1)
                pe.wait_ge(made2, OUTS * g + OUTS)
                pe.sem_inc(w2_free, 1)
                pe.sem_inc(h_free, 1)

            first(0, 0)
            turn_sample(0, 0)
            with pe.Fori(0, NG // 2 - 1) as i:
                for s in range(2):
                    g = 2 * i + s
                    first(g + 1, 1 - s)
                    second(g, s)
                    turn_sample(g + 1, 1 - s)
            first(NG - 1, 1)
            second(NG - 2, 0)
            turn_sample(NG - 1, 1)
            second(NG - 1, 1)



def stage_last(nc, io, y, ys):
    st = Stage(nc, "last")
    with st.ctx:
        x1 = st.sb("x1", [P, TT, D])
        x1s, y_lo = st.sb("x1s", [NS, D]), st.sb("y_lo", [NS, D])
        gate, sc, sh = (st.sb(n, [P, D]) for n in ("gate", "sc", "sh"))
        gate_s, sc_s, sh_s = (st.sb(n, [NS, D]) for n in ("gate_s", "sc_s", "sh_s"))
        T = dict(ss=st.sb("ss", [P, 16]), v=st.sb("v", [P, 16]), r=st.sb("r", [P, 16]), t=st.sb("t", [P, 16]))
        sq = st.sb("sq", [P, D])
        x_in, s_in, m_in, dve_s, v_ready, root, scaled, done, put = (
            st.sem(n) for n in ("x_in", "s_in", "m_in", "dve_steps", "v_ready", "root", "scaled", "done", "put"))
        y_out = io["y_prompt"][0].rearrange("(t p) d -> p t d", p=P)
        block = st.block()

        @block.sync
        def _(sp):
            sp.dma_start(x1[:], io["x1"][0:S, :].rearrange("(t p) d -> p t d", p=P)).then_inc(x_in, 16)
            sp.dma_start(x1s[:], io["x1"][S:, :]).then_inc(s_in, 16)
            for p, s, m in ((gate, gate_s, G_F), (sc, sc_s, SC_L), (sh, sh_s, SH_L)):
                load_rows(sp, io, p, s, m, m_in)
            for t in range(TT):
                sp.wait_ge(done, t + 1)
                sp.dma_start(y_out[:, t, :], y[:, t, :]).then_inc(put, 16)
            sp.wait_ge(done, TT + 1)
            sp.dma_start(io["y_sample"].rearrange("b t d -> (b t) d"), x1s[:]).then_inc(put, 16)
            sp.wait_ge(put, 16 * (TT + 1))

        @block.scalar
        def _(act):
            act.wait_ge(v_ready, 1)
            act.activation(T["t"][:, 0:9], T["v"][:, 0:9], ACT.Sqrt).then_inc(root, 1)

        @block.gpsimd
        def _(pool):
            for t in range(TT):
                pool.wait_ge(scaled, t + 1)
                pool.tensor_tensor(y[:, t, :], x1[:, t, :], sh[:], ALU.add).then_inc(done, 1)
            pool.wait_ge(scaled, TT + 1)
            pool.tensor_tensor(x1s[:], x1s[:], sh_s[:], ALU.add).then_inc(done, 1)

        @block.vector
        def _(dve):
            steps = Steps(dve, dve_s)
            steps.then(dve.memset(T["ss"][:], 1.0))
            dve.wait_ge(m_in, 16 * 3 * (1 + DB))
            dve.wait_ge(x_in, 16)
            for t in range(TT):
                steps.then(dve.tensor_tensor(y[:, t, :], y[:, t, :], gate[:], ALU.mult))
                steps.then(dve.tensor_tensor(x1[:, t, :], x1[:, t, :], y[:, t, :], ALU.add))
                steps.then(dve.tensor_tensor_reduce(sq[:], x1[:, t, :], x1[:, t, :], 1.0, 0.0, ALU.mult, ALU.add,
                                                    T["ss"][:, t:t + 1]))
            dve.wait_ge(s_in, 16)
            steps.then(dve.tensor_copy(y_lo[:], ys[NS:P, :]))
            steps.then(dve.tensor_tensor(y_lo[:], y_lo[:], ys[0:NS, :], ALU.add))
            steps.then(dve.tensor_tensor(y_lo[:], y_lo[:], gate_s[:], ALU.mult))
            steps.then(dve.tensor_tensor(x1s[:], x1s[:], y_lo[:], ALU.add))
            steps.then(dve.tensor_tensor_reduce(sq[0:NS, :], x1s[:], x1s[:], 1.0, 0.0, ALU.mult, ALU.add, T["ss"][0:NS, 8:9]))
            rms_rows(steps, v_ready, root, T, 9)
            for t in range(TT):
                dve.scalar_tensor_tensor(out=x1[:, t, :], in0=x1[:, t, :], scalar=T["r"][:, t:t + 1], in1=sc[:],
                                         op0=ALU.mult, op1=ALU.mult).then_inc(scaled, 1)
            dve.scalar_tensor_tensor(out=x1s[:], in0=x1s[:], scalar=T["r"][0:NS, 8:9], in1=sc_s[:],
                                     op0=ALU.mult, op1=ALU.mult).then_inc(scaled, 1)


def program(nc, io):
    with ExitStack() as ctx:
        held = lambda c, n, shape, dt=F32: c.enter_context(nc.sbuf_tensor(n, shape, dt))
        ps = ctx.enter_context(nc.psum_tensor("ps", [P, 8, CH], F32))
        ident, mod_p = held(ctx, "ident", [P, P]), held(ctx, "mod_p", [P, 4, KT])
        stage_modulation(nc, io, ps, ident, mod_p)
        with ExitStack() as c:
            z_hi, z_lo, zs = held(c, "z_hi", [P, KT, S], F32R), held(c, "z_lo", [P, KT, S], F32R), held(c, "zs", [P, KT, P], F32R)
            stage_norm(nc, io, ps, ident, mod_p, z_hi, z_lo, zs, "norm_a", SH_A, SC_A, 0, 1)
            stage_projection(nc, "inp", ps, io["w_in"], IN_W, io["proj"], z_hi, z_lo, zs)
        with ExitStack() as c:
            mix_hi, mix_lo = held(c, "mix_hi", [P, KT, S], F32R), held(c, "mix_lo", [P, KT, S], F32R)
            mix_s = held(c, "mix_s", [P, KT, P], F32R)
            stage_prompt_attention(nc, io, ps, ident, mix_hi, mix_lo)
            stage_prompt_retention(nc, io, ps, ident, mix_hi, mix_lo)
            with ExitStack() as cc:
                q_blocks, kT_new = held(cc, "q_blocks", [P, DB, 4, NS]), held(cc, "kT_new", [P, 4, NS])
                stage_sample_heads(nc, io, ps, ident, mix_s, q_blocks, kT_new)
                stage_sample_attention(nc, io, ps, ident, mix_s, q_blocks, kT_new)
            stage_projection(nc, "outp", ps, io["w_out"], D, io["branch"], mix_hi, mix_lo, mix_s)
        with ExitStack() as c:
            y, ys = held(c, "y", [P, TT, D]), held(c, "ys", [P, D])
            with ExitStack() as cc:
                u_hi, u_lo, us = held(cc, "u_hi", [P, KT, S], F32R), held(cc, "u_lo", [P, KT, S], F32R), held(cc, "us", [P, KT, P], F32R)
                stage_norm(nc, io, ps, ident, mod_p, u_hi, u_lo, us, "norm_f", SH_F, SC_F, 2, 3, (io["branch"], G_A))
                stage_mlp(nc, io, ps, ident, u_hi, u_lo, us, y, ys)
            stage_last(nc, io, y, ys)


_INS = ["x_prompt", "x_sample", "c_prompt", "c_sample", "cache_k", "cache_v", "state_ret",
        "w_ada", "b_ada", "w_in", "ret_gain", "w_out", "w_ff1", "w_ff2", "w_ada_f", "b_ada_f"]
_OUTS = [("y_prompt", (1, S, D)), ("y_sample", (DB, DS, D)),
         ("k_prompt", (1, 1, S, H, HD)), ("v_prompt", (1, 1, S, H, HD)), ("ret_prompt", (1, 1, RH, RD, RV)),
         ("k_sample", (1, DB, DS, H, HD)), ("v_sample", (1, DB, DS, H, HD)), ("ret_sample", (1, DB, RH, RD, RV))]


def build(nc, shapes):
    io = {n: nc.dram_tensor(f"in_{n}", s, F32, kind="ExternalInput").ap() for n, s in shapes.items()}
    for n, s in _OUTS:
        io[n] = nc.dram_tensor(f"out_{n}", s, F32, kind="ExternalOutput").ap()
    io["mod"] = nc.dram_tensor("mod", (9, MOD_W), F32).ap()
    io["proj"] = nc.dram_tensor("proj", (S + P, IN_W), F32).ap()
    io["branch"] = nc.dram_tensor("branch", (S + P, D), F32).ap()
    io["x1"] = nc.dram_tensor("x1", (S + NS, D), F32).ap()
    program(nc, io)


def kernel(**inputs):
    import concourse.bacc as bacc
    from concourse.bass_utils import run_bass_kernel_spmd

    arrays = {n: np.ascontiguousarray(inputs[n]) for n in _INS}
    arrays.update(constants())
    nc = bacc.Bacc("TRN2", target_bir_lowering=False, num_devices=1)
    build(nc, {n: a.shape for n, a in arrays.items()})
    r = run_bass_kernel_spmd(nc, [{f"in_{n}": a for n, a in arrays.items()}], core_ids=[0])
    return tuple(r.results[0][f"out_{n}"] for n, _ in _OUTS)
```

```python
import math
from contextlib import ExitStack

import numpy as np
import concourse.bass as bass
from concourse import mybir

F32 = mybir.dt.float32
F32R = mybir.dt.float32r
ALU = mybir.AluOpType
ACT = mybir.ActivationFunctionType
ds = bass.ds

P = 128
D = 1024
KT = D // P
S = 1024
TT = S // P
DB, DS = 8, 8
NS = DB * DS
PAST = 4096
L = 2048
H, HD = 8, 64
AW = H * HD
RH, RD, RV = 4, 64, 128
IN_W = 3 * AW + 2 * RH * RD + 2 * RH * RV
CH = 512
FF = 4 * D
MOD_W = 8 * D
SH_A, SC_A, G_A, SH_F, SC_F, G_F, SH_L, SC_L = range(8)
EPS = 1e-6
NEG = -1e30
BRANCHES = ((128, 1), (512, 4), (2048, 16))
SCALE = HD ** -0.5
OLD = 1536
KTILES = 10
NKEYS = KTILES * P + DS
GF = 256
NG = FF // GF



def log_count(dist):
    n = np.zeros(dist.shape)
    for window, dil in BRANCHES:
        n += (dist >= 0) & (dist <= window) & (dist % dil == 0)
    return np.where(n > 0, np.log(np.maximum(n, 1)), NEG).astype(np.float32)


def sample_positions():
    old = [16 * (16 * j + g) + r for j in range(6) for g in range(16) for r in range(8)]
    return np.array(old + list(range(OLD, L)) + list(range(L, L + DS)))


def angles(theta_powers, pos):
    inv = theta_powers.astype(np.float32)
    return (pos.astype(np.float32)[:, None] * inv[None, :]).astype(np.float32)


def constants():
    f = np.float32
    c = {"ident": np.eye(P, dtype=f)}
    p = np.arange(P)
    c["bias_p"] = log_count(p[:, None] - np.arange(S)[None, :] + (S - P))
    keys = sample_positions()
    t = np.tile(np.arange(DS), 2 * H)
    c["bias_s"] = log_count(L + t[:, None] - keys[None, :])
    pos_p = np.arange(S)
    pos_s = PAST + np.tile(np.arange(DS), DB)
    att = 500000.0 ** (-np.arange(0, 16, 2) / 16.0)
    ret = 10000.0 ** (-np.linspace(0.0, 1.0, RD // 2, dtype=f).astype(np.float64))

    def table(fn, powers, pos, heads):
        a = fn(angles(powers, pos).astype(np.float64)).astype(f)
        return np.tile(a, (1, heads))

    def by_tile(a):
        return np.ascontiguousarray(a.reshape(TT, P, -1).transpose(1, 0, 2).reshape(P, -1))

    c["rope_p"] = np.concatenate([np.tile(by_tile(table(g, att, pos_p, 2)), (1, 2)) for g in (np.cos, np.sin)], 1)
    c["rope_s"] = np.concatenate([table(g, att, pos_s, 2 * H) for g in (np.cos, np.sin)], 1)
    c["rot_p"] = np.concatenate([by_tile(table(g, ret, pos_p, 2)) for g in (np.cos, np.sin)], 1)
    c["rot_s"] = np.concatenate([table(g, ret, pos_s, 2 * RH) for g in (np.cos, np.sin)], 1)
    log_g = np.log1p(-np.exp2(-5.0 - np.arange(RH)))
    rel = p[None, :] - p[:, None]
    c["dmask_p"] = np.concatenate(
        [np.where(rel >= 0, np.exp(np.maximum(rel, 0) * g), 0.0) for g in log_g], 1).astype(f)
    c["dout_p"] = np.concatenate(
        [np.repeat(np.exp((p + 1.0)[None, :] * log_g[2 * a:2 * a + 2, None]), RD, 0) for a in range(2)], 1).astype(f)
    c["din_p"] = (np.exp((P - 1.0 - p)[:, None] * log_g[None, :]) * RD ** -0.5).astype(f)
    c["gchunk_p"] = np.stack([np.repeat(np.exp(P * log_g[2 * a:2 * a + 2]), RD) for a in range(2)], 1).astype(f)
    i = np.arange(NS)
    same = i[:, None] // DS == i[None, :] // DS
    rel = i[None, :] - i[:, None]
    c["dmask_s"] = np.concatenate(
        [np.where(same & (rel >= 0), np.exp(np.maximum(rel, 0) * g), 0.0) for g in log_g], 1).astype(f)
    b2 = np.repeat(np.arange(2), RD)
    c["dout_s"] = np.stack([np.stack([
        np.where((i[None, :] // DS) == 2 * bp + b2[:, None], np.exp((i % DS + 1.0) * g)[None, :], 0.0)
        for bp in range(4)], 1) for g in log_g], 1).reshape(P, -1).astype(f)
    c["din_s"] = np.stack([np.stack([
        np.where((i[:, None] // DS) == 2 * bp + b2[None, :],
                 (np.exp((DS - 1.0 - i % DS) * g) * RD ** -0.5)[:, None], 0.0)
        for bp in range(4)], 1) for g in log_g], 1).reshape(NS, -1).astype(f)
    return c


GCHUNK_S = [float(np.float32(math.exp(DS * math.log1p(-2.0 ** (-5 - h))))) for h in range(RH)]


class Steps:

    def __init__(self, eng, sem):
        self.eng, self.sem, self.n, self.base = eng, sem, 0, 0

    def done(self, ins):
        ins.then_inc(self.sem, 1)
        self.n += 1
        return self.n

    def then(self, ins):
        self.done(ins)
        self.eng.wait_ge(self.sem, self.base + self.n)

    def wait(self):
        self.eng.wait_ge(self.sem, self.base + self.n)


class Stage:

    def __init__(self, nc, name):
        self.nc, self.name, self.ctx, self.sems = nc, name, ExitStack(), []
        self.ctx.callback(self.clear)

    def sb(self, name, shape, dt=F32):
        return self.ctx.enter_context(self.nc.sbuf_tensor(f"{self.name}_{name}", shape, dt))

    def sem(self, name):
        self.sems.append(self.nc.alloc_semaphore(f"{self.name}_{name}"))
        return self.sems[-1]

    def clear(self):
        self.nc.clear_and_free_semaphores(self.sems)
        self.nc.all_engine_barrier()

    def block(self):
        return self.ctx.enter_context(self.nc.Block())



def stage_modulation(nc, io, ps, ident, mod_p, x, xs, ss):
    st = Stage(nc, "mod")
    with st.ctx:
        crow, ex, srow = (st.sb(n, [9, D]) for n in ("crow", "ex", "srow"))
        cT = st.sb("cT", [P, KT, 10])
        mrow = st.sb("mrow", [9, MOD_W])
        sq = [st.sb(f"sq{s}", [P, D]) for s in range(2)]
        w = [st.sb(f"w{s}", [P, KT, CH]) for s in range(4)]
        c_in, b_in, exp_done, dve, turned = (st.sem(n) for n in ("c_in", "b_in", "exp_done", "dve", "turned"))
        w_in = [st.sem(f"w_in{s}") for s in range(4)]
        x_in = [st.sem(f"x_in{t}") for t in range(TT + 1)]
        squared = st.sem("squared")
        w_free, bank_free, stored, loaded = (st.sem(n) for n in ("w_free", "bank_free", "stored", "loaded"))
        silu_steps = 4
        wv = io["w_ada"].rearrange("o (k p) n -> p (o k) n", p=P)
        wf = io["w_ada_f"].rearrange("(k p) n -> p k n", p=P)
        block = st.block()

        @block.sync
        def _(sp):
            sp.dma_start(crow[0:1, :], io["c_prompt"]).then_inc(c_in, 16)
            sp.dma_start(crow[1:9, :], io["c_sample"]).then_inc(c_in, 16)
            sp.dma_start(ident[:], io["ident"]).then_inc(c_in, 16)
            sp.dma_start(mrow[:, 0:6 * D], io["b_ada"][0].partition_broadcast(9)).then_inc(b_in, 16)
            sp.dma_start(mrow[:, 6 * D:], io["b_ada_f"].partition_broadcast(9)).then_inc(b_in, 16)

            def weights(i):
                for s in range(4):
                    sp.wait_ge(w_free, 4 * i + s + 1)
                    sp.dma_start(w[s][:], wv[:, :, ds(i * 4 * CH + s * CH, CH)]).then_inc(w_in[s], 16)

            weights(0)
            for t in range(TT):
                sp.dma_start(x[:, t, :], io["x_prompt"][0, t * P:(t + 1) * P, :]).then_inc(x_in[t], 16)
            sp.dma_start(xs[:], io["x_sample"].rearrange("b t d -> (b t) d")).then_inc(x_in[TT], 16)
            with sp.Fori(1, 3) as i:
                weights(i)
            for s in range(4):
                sp.wait_ge(w_free, 12 + s + 1)
                sp.dma_start(w[s][:], wf[:, :, s * CH:(s + 1) * CH]).then_inc(w_in[s], 16)
            sp.wait_ge(dve, silu_steps + 3)
            sp.dma_start(io["mod"], mrow[:]).then_inc(stored, 16)
            sp.wait_ge(stored, 16)
            for j, m in enumerate((SH_A, SC_A, SH_F, SC_F)):
                sp.dma_start(mod_p[:, j, :], io["mod"][0, m * D:(m + 1) * D].rearrange("(k p) -> p k", p=P),
                             allow_slow_non_contiguous=True).then_inc(loaded, 16)
            sp.wait_ge(loaded, 64)

        @block.scalar
        def _(act):
            act.wait_ge(c_in, 48)
            act.activation(ex[:], crow[:], ACT.Exp, scale=-1.0).then_inc(exp_done, 1)

        @block.tensor
        def _(pe):
            pe.sem_inc(w_free, 4)
            pe.wait_ge(dve, silu_steps - 1)
            for k in range(KT):
                last = pe.transpose(ps[:, 7, k * 10:k * 10 + 9], srow[:, k * P:(k + 1) * P], ident[0:9, 0:9])
            last.then_inc(turned, 1)
            pe.wait_ge(dve, silu_steps)
            with pe.Fori(0, 4) as i:
                for s in range(4):
                    pe.wait_ge(w_in[s], 16 * i + 16)
                    pe.wait_ge(bank_free, 4 * i + s + 1)
                    for k in range(KT):
                        mm = pe.matmul(ps[0:9, s, :], cT[:, k, 0:9], w[s][:, k, :], start=(k == 0), stop=(k == KT - 1))
                    mm.then_inc(w_free, 1)

        @block.vector
        def _(dve_):
            dve_.sem_inc(bank_free, 4)
            steps = Steps(dve_, dve)
            dve_.wait_ge(exp_done, 1)
            steps.then(dve_.tensor_scalar(ex[:], ex[:], 1.0, None, ALU.add))
            steps.then(dve_.reciprocal(ex[:], ex[:]))
            steps.done(dve_.tensor_tensor(srow[:], crow[:], ex[:], ALU.mult))
            dve_.wait_ge(turned, 1)
            steps.done(dve_.tensor_copy(cT[:, :, 0:9], ps[:, 7, 0:80].rearrange("p (k c) -> p k c", c=10)[:, :, 0:9]))
            assert steps.n == silu_steps
            dve_.memset(ss[:], 0.0).then_inc(squared, 1)
            dve_.wait_ge(squared, 1)
            for t in range(TT):
                dve_.wait_ge(x_in[t], 16)
                if t >= 2:
                    dve_.wait_ge(squared, t)
                dve_.tensor_tensor_reduce(sq[t % 2][:], x[:, t, :], x[:, t, :], 1.0, 0.0, ALU.mult, ALU.add,
                                          ss[:, 0, t:t + 1]).then_inc(squared, 1)
            dve_.wait_ge(x_in[TT], 16)
            dve_.wait_ge(squared, TT)
            dve_.tensor_tensor_reduce(sq[0][0:NS, :], xs[:], xs[:], 1.0, 0.0, ALU.mult, ALU.add,
                                      ss[0:NS, 0, TT:TT + 1]).then_inc(squared, 1)
            dve_.wait_ge(b_in, 32)
            with dve_.Fori(0, 4) as i:
                for s in range(4):
                    dve_.wait_ge(w_free, 4 * i + s + 5)
                    cols = ds(i * 4 * CH + s * CH, CH)
                    dve_.tensor_tensor(mrow[:, cols], ps[0:9, s, :], mrow[:, cols], ALU.add).then_inc(bank_free, 1)
            dve_.wait_ge(bank_free, 20)
            for m in (SC_A, SC_F, SC_L):
                steps.done(dve_.tensor_scalar(mrow[:, m * D:(m + 1) * D], mrow[:, m * D:(m + 1) * D], 1.0, None, ALU.add))



def load_rows(eng, io, prompt, sample, m, sem):
    if prompt is not None:
        eng.dma_start(prompt[:], io["mod"][0, m * D:(m + 1) * D].partition_broadcast(P)).then_inc(sem, 16)
    if sample is not None:
        for b in range(DB):
            eng.dma_start(sample[b * DS:(b + 1) * DS, :],
                          io["mod"][1 + b, m * D:(m + 1) * D].partition_broadcast(DS)).then_inc(sem, 16)


def rms_rows(steps, act_ready, root_ready, T, n, nth=1):
    dve, ss, v, r, t = steps.eng, T["ss"], T["v"], T["r"], T["t"]
    steps.wait()
    steps.then(dve.tensor_scalar(v[:, 0:n], ss[:, 0:n], 1.0 / D, EPS, ALU.mult, ALU.add))
    dve.sem_inc(act_ready, 1)
    dve.wait_ge(root_ready, nth)
    steps.then(dve.reciprocal(r[:, 0:n], t[:, 0:n]))
    steps.then(dve.tensor_tensor(ss[:, 0:n], r[:, 0:n], r[:, 0:n], ALU.mult))
    steps.then(dve.tensor_tensor(ss[:, 0:n], ss[:, 0:n], v[:, 0:n], ALU.mult))
    steps.then(dve.tensor_scalar(ss[:, 0:n], ss[:, 0:n], -0.5, 1.5, ALU.mult, ALU.add))
    steps.then(dve.tensor_tensor(r[:, 0:n], r[:, 0:n], ss[:, 0:n], ALU.mult))


def stage_norm(nc, io, ps, ident, mod_p, z_hi, z_lo, zs, name, sh, sc, jsh, jsc, x, xs, ss):
    st = Stage(nc, name)
    with st.ctx:
        T = {n: st.sb(n, [P, 16]) for n in "vrt"}
        T["ss"] = st.sb("sum", [P, 16])
        scs, shs = (st.sb(n, [NS, D]) for n in ("scs", "shs"))
        zf = [st.sb(f"zf{s}", [P, CH]) for s in range(4)]
        s_in, dve, v_ready, root = (st.sem(n) for n in ("s_in", "dve", "v_ready", "root"))
        r_ready, xn_dve, xn_act, xs_ready, turned, zf_ready, hi_ready, lo_dve, lo_pool = (
            st.sem(n) for n in ("r_ready", "xn_dve", "xn_act", "xs_ready", "turned", "zf_ready", "hi_ready", "lo_dve", "lo_pool"))
        zs_turned, zs_hi = st.sem("zs_turned"), st.sem("zs_hi")
        block = st.block()
        units = [(h, k) for h in range(2) for k in range(KT)]

        @block.sync
        def _(sp):
            for dst, m in ((scs, sc), (shs, sh)):
                load_rows(sp, io, None, dst, m, s_in)

        def low_part(eng, u, done):
            h, k = units[u]
            cols = slice(h * CH, (h + 1) * CH)
            eng.wait_ge(hi_ready, u + 1)
            eng.tensor_tensor(z_lo[:, k, cols], zf[u % 4][:], z_hi[:, k, cols].bitcast(F32), ALU.subtract).then_inc(done, 1)

        @block.scalar
        def _(act):
            act.wait_ge(v_ready, 1)
            act.activation(T["t"][:, 0:9], T["v"][:, 0:9], ACT.Sqrt).then_inc(root, 1)
            act.wait_ge(r_ready, 1)
            for t in range(1, TT, 2):
                act.mul(x[:, t, :], x[:, t, :], T["r"][:, t:t + 1]).then_inc(xn_act, 1)
            for u, (h, k) in enumerate(units):
                act.wait_ge(zf_ready, u + 1)
                act.copy(z_hi[:, k, h * CH:(h + 1) * CH], zf[u % 4][:]).then_inc(hi_ready, 1)
            act.wait_ge(zs_turned, 1)
            act.copy(zs[:, :, 0:NS], ps[:, 7, :].rearrange("p (k n) -> p k n", n=NS)).then_inc(zs_hi, 1)

        @block.gpsimd
        def _(pool):
            for u in range(1, len(units), 2):
                low_part(pool, u, lo_pool)

        @block.vector
        def _(dve_):
            steps = Steps(dve_, dve)
            steps.then(dve_.tensor_tensor(T["ss"][:, 0:9], ss[:, 0, 0:9], ss[:, 1, 0:9], ALU.add))
            rms_rows(steps, v_ready, root, T, 9)
            dve_.sem_inc(r_ready, 1)
            for t in range(0, TT, 2):
                dve_.tensor_scalar(x[:, t, :], x[:, t, :], T["r"][:, t:t + 1], None, ALU.mult).then_inc(xn_dve, 1)

            def sample():
                dve_.wait_ge(s_in, 16 * 16)
                steps.then(dve_.scalar_tensor_tensor(out=xs[:], in0=xs[:], scalar=T["r"][0:NS, 8:9], in1=scs[:],
                                                     op0=ALU.mult, op1=ALU.mult))
                dve_.tensor_tensor(xs[:], xs[:], shs[:], ALU.add).then_inc(xs_ready, 1)

            for u, (h, k) in enumerate(units):
                dve_.wait_ge(turned, u + 1)
                if u >= 4 and u % 2:
                    dve_.wait_ge(lo_pool, u // 2 - 1)
                elif u >= 4:
                    dve_.wait_ge(lo_dve, u // 2 - 1)
                dve_.tensor_scalar(zf[u % 4][:], ps[:, u % 6, :], mod_p[:, jsc, k:k + 1], mod_p[:, jsh, k:k + 1],
                                   ALU.mult, ALU.add).then_inc(zf_ready, 1)
                if u == KT:
                    sample()
                if u % 2:
                    low_part(dve_, u - 1, lo_dve)
            dve_.wait_ge(zs_hi, 1)
            dve_.tensor_tensor(zs[:, :, NS:P], ps[:, 7, :].rearrange("p (k n) -> p k n", n=NS),
                               zs[:, :, 0:NS].bitcast(F32), ALU.subtract).then_inc(zf_ready, 1)

        @block.tensor
        def _(pe):
            for u, (h, k) in enumerate(units):
                pe.wait_ge(xn_dve, 2 * (h + 1))
                pe.wait_ge(xn_act, 2 * (h + 1))
                if u >= 6:
                    pe.wait_ge(zf_ready, u - 5)
                for j in range(4):
                    mm = pe.transpose(ps[:, u % 6, j * P:(j + 1) * P], x[:, 4 * h + j, k * P:(k + 1) * P], ident[:])
                mm.then_inc(turned, 1)
            pe.wait_ge(xs_ready, 1)
            for k in range(KT):
                mm = pe.transpose(ps[:, 7, k * NS:(k + 1) * NS], xs[:, k * P:(k + 1) * P], ident[0:NS, 0:NS])
            mm.then_inc(zs_turned, 1)



def stage_projection(nc, name, ps, w_dram, width, out, z_hi, z_lo, zs, room):
    st = Stage(nc, name)
    NCH = width // CH
    OUTS = TT + 1
    BANKS, ROWS = 6, 3
    QUARTERS = 4
    quarter = lambda q: slice(q * KT // QUARTERS, (q + 1) * KT // QUARTERS)
    with st.ctx:
        raw = [room[:, s * TT // 2:(s + 1) * TT // 2, :].rearrange("p t (a c) -> p (t a) c", c=CH) for s in range(2)]
        w_hi = [st.sb(f"whi{s}", [P, KT, CH], F32R) for s in range(2)]
        w_lo = [st.sb(f"wlo{s}", [P, KT, CH], F32R) for s in range(2)]
        row = [st.sb(f"row{s}", [P, CH]) for s in range(ROWS)]
        raw_in = [[st.sem(f"raw_in{s}_{q}") for q in range(QUARTERS)] for s in range(2)]
        raw_free, w_free, w_hi_done, w_ready, made, bank_free = (
            st.sem(n) for n in ("raw_free", "w_free", "w_hi_done", "w_ready", "made", "bank_free"))
        row_free = [st.sem(f"row_free{s}") for s in range(ROWS)]
        wv = w_dram.rearrange("o (k p) n -> p (o k) n", p=P)
        block = st.block()

        @block.sync
        def _(sp):
            with sp.Fori(0, NCH // 2) as i:
                for s in range(2):
                    sp.wait_ge(raw_free, QUARTERS * (2 * i + s) + QUARTERS)
                    for q in range(QUARTERS):
                        sp.dma_start(raw[s][:, quarter(q), :],
                                     wv[:, quarter(q), ds(i * 2 * CH + s * CH, CH)]).then_inc(raw_in[s][q], 16)

        @block.vector
        def _(dve):
            dve.sem_inc(raw_free, 2 * QUARTERS)
            with dve.Fori(0, NCH // 2) as i:
                for s in range(2):
                    dve.wait_ge(w_free, 2 * i + s + 1)
                    for q in range(QUARTERS):
                        k = quarter(q)
                        dve.wait_ge(raw_in[s][q], 16 * i + 16)
                        dve.tensor_copy(w_hi[s][:, k, :], raw[s][:, k, :]).then_inc(w_hi_done, 1)
                        dve.wait_ge(w_hi_done, QUARTERS * (2 * i + s) + q + 1)
                        dve.tensor_tensor(w_lo[s][:, k, :], raw[s][:, k, :], w_hi[s][:, k, :].bitcast(F32),
                                          ALU.subtract).then_inc(raw_free, 1)

        @block.tensor
        def _(pe):
            pe.sem_inc(w_free, 2)
            with pe.Fori(0, NCH // 2) as i:
                for s in range(2):
                    for o in range(OUTS):
                        n = s * OUTS + o
                        bank = ps[:, n % BANKS, :]
                        pe.wait_ge(bank_free, i * 2 * OUTS + n + 1)
                        if o < TT:
                            parts = ((z_hi, w_hi), (z_hi, w_lo), (z_lo, w_hi))
                            cols = slice(o * P, (o + 1) * P)
                        else:
                            parts = ((zs, w_hi), (zs, w_lo))
                            cols = slice(0, P)
                        for k in range(KT):
                            if o == 0 and k % (KT // QUARTERS) == 0:
                                pe.wait_ge(raw_free, QUARTERS * (2 * i + s) + 2 * QUARTERS + k // (KT // QUARTERS) + 1)
                            for a, (z, w) in enumerate(parts):
                                mm = pe.matmul(bank, z[:, k, cols], w[s][:, k, :], start=(k == 0 and a == 0),
                                               stop=(k == KT - 1 and a == len(parts) - 1))
                        mm.then_inc(made, 1)
                    pe.wait_ge(made, i * 2 * OUTS + (s + 1) * OUTS)
                    pe.sem_inc(w_free, 1)

        @block.scalar
        def _(act):
            act.sem_inc(bank_free, BANKS)
            for r in range(ROWS):
                act.sem_inc(row_free[r], 16)
            with act.Fori(0, NCH // 2) as i:
                for s in range(2):
                    for o in range(OUTS):
                        n = s * OUTS + o
                        act.wait_ge(made, i * 2 * OUTS + n + 1)
                        act.wait_ge(row_free[n % ROWS], i * (16 * 2 * OUTS // ROWS) + 16 * (n // ROWS) + 16)
                        act.copy(row[n % ROWS][:], ps[:, n % BANKS, :]).then_inc(bank_free, 1)
                        act.wait_ge(bank_free, i * 2 * OUTS + n + BANKS + 1)
                        act.dma_start(out[o * P:(o + 1) * P, ds(i * 2 * CH + s * CH, CH)],
                                      row[n % ROWS][:]).then_inc(row_free[n % ROWS], 16)
            for r in range(ROWS):
                act.wait_ge(row_free[r], 16 * (NCH * OUTS // ROWS) + 16)



def banks(ps, first, n):
    return ps[:, first:first + n, :].rearrange("p b c -> p (b c)")


def stage_prompt_attention(nc, io, ps, ident, mix_hi, mix_lo):
    st = Stage(nc, "att")
    UNITS = 2 * TT
    HALF = ROPE = 8
    with st.ctx:
        bias = st.sb("bias", [P, S])
        rope = st.sb("rope", [P, 2, 2 * TT, 2, HALF])
        qk = [st.sb(f"qk{s}", [P, 2 * TT, P]) for s in range(2)]
        v = [st.sb(f"v{s}", [P, TT, P]) for s in range(2)]
        tmp = [st.sb(f"tmp{s}", [P, 2 * TT, 2, HALF]) for s in range(4)]
        q_hi = [st.sb(f"qhi{h}", [P, S], F32R) for h in range(2)]
        q_lo = [st.sb(f"qlo{h}", [P, S], F32R) for h in range(2)]
        k_hi, k_lo = st.sb("khi", [P, S], F32R), st.sb("klo", [P, S], F32R)
        prob = [st.sb(f"prob{s}", [P, S]) for s in range(3)]
        probT = [st.sb(f"probT{s}", [P, S]) for s in range(2)]
        top, neg, total, inv = (st.sb(n, [P, UNITS]) for n in ("top", "neg", "total", "inv"))
        waited = st.sb("waited", [P, 1])
        tables, zeroed, roped, heads_free, turned, hi_done, split_done = (st.sem(n) for n in (
            "tables", "zeroed", "roped", "heads_free", "turned", "hi_done", "split_done"))
        made, scored, neg_done, exp_done, inv_done, prob_done, prob_turned, probT_done, pv_done, mix_hi_done = (
            st.sem(n) for n in ("made", "scored", "neg_done", "exp_done", "inv_done", "prob_done",
                                "prob_turned", "probT_done", "pv_done", "mix_hi_done"))
        mix_done = st.sem("mix_done")
        qkv_in = [st.sem(f"qkv_in{s}") for s in range(2)]
        kv_put = [st.sem(f"kv_put{s}") for s in range(2)]

        def unit(u):
            h, q = divmod(u, TT)
            return h, (TT - 1 - q if h else q)

        proj = io["proj"][0:S, :].rearrange("(t p) c -> p t c", p=P)
        k_out = io["k_prompt"].rearrange("o b (t p) h d -> p (o b t) (h d)", p=P)
        v_out = io["v_prompt"].rearrange("o b (t p) h d -> p (o b t) (h d)", p=P)
        block = st.block()

        @block.sync
        def _(sp):
            for s in range(2):
                sp.sem_inc(kv_put[s], 32)
            sp.dma_start(bias[:], io["bias_p"]).then_inc(tables, 16)
            sp.dma_start(rope[:].rearrange("p a b c d -> p (a b c d)"), io["rope_p"]).then_inc(tables, 16)
            with sp.Fori(0, 2) as i:
                for s in range(2):
                    cols = [sp.snap(i * 2 * P + s * P + j * AW) for j in range(3)]
                    sp.wait_ge(heads_free, 2 * i + s + 1)
                    sp.wait_ge(kv_put[s], 32 * i + 32)
                    for j, dst in ((0, qk[s][:, 0:TT, :]), (1, qk[s][:, TT:, :]), (2, v[s][:])):
                        sp.dma_start(dst, proj[:, :, ds(cols[j], P)]).then_inc(qkv_in[s], 16)
                    sp.wait_ge(roped, 6 * (2 * i + s) + 6)
                    sp.dma_start(k_out[:, :, ds(cols[0], P)], qk[s][:, TT:, :]).then_inc(kv_put[s], 16)
                    sp.dma_start(v_out[:, :, ds(cols[0], P)], v[s][:]).then_inc(kv_put[s], 16)
            for s in range(2):
                sp.wait_ge(kv_put[s], 96)

        @block.gpsimd
        def _(pool):
            pool.wait_ge(tables, 32)
            with pool.Fori(0, 2) as i:
                for s in range(2):
                    n = 6 * (2 * i + s)
                    pool.wait_ge(qkv_in[s], 48 * i + 48)
                    x = qk[s][:].rearrange("p t (h d) -> p t h d", h=2)
                    a, b = x[:, :, :, 0:HALF], x[:, :, :, HALF:2 * HALF]
                    for dst, u, w in ((0, a, 0), (1, b, 1), (2, b, 0), (3, a, 1)):
                        pool.tensor_tensor(tmp[dst][:], u, rope[:, w], ALU.mult).then_inc(roped, 1)
                    pool.wait_ge(roped, n + 4)
                    pool.tensor_tensor(a, tmp[0][:], tmp[1][:], ALU.subtract).then_inc(roped, 1)
                    pool.tensor_tensor(b, tmp[2][:], tmp[3][:], ALU.add).then_inc(roped, 1)
                    pool.wait_ge(roped, n + 6)

        @block.tensor
        def _(pe):
            pe.sem_inc(heads_free, 2)
            pe.sem_inc(prob_turned, 3)
            pe.sem_inc(pv_done, 2)
            with pe.Fori(0, 2) as i:
                for s in range(2):
                    base = i * 2 * UNITS + s * UNITS

                    def scores(u):
                        h, q = unit(u)
                        if u >= 2:
                            pe.wait_ge(scored, base + u - 1)
                        width = (q + 1) * P
                        for c in range(0, width, CH):
                            e = min(width, c + CH)
                            out = banks(ps, 2 * (u % 2), 2)[:, c:e]
                            for a, (x, y) in enumerate(((q_hi, k_hi), (q_hi, k_lo), (q_lo, k_hi))):
                                mm = pe.matmul(out, x[h][:, q * P:(q + 1) * P], y[:, c:e], start=(a == 0), stop=(a == 2))
                        mm.then_inc(made, 1)

                    def turn(u):
                        pe.wait_ge(prob_done, base + u + 1)
                        for k in range(unit(u)[1] + 1):
                            mm = pe.transpose(banks(ps, 4, 2)[:, k * P:(k + 1) * P], prob[u % 3][:, k * P:(k + 1) * P], ident[:])
                        mm.then_inc(prob_turned, 1)

                    def values(u):
                        h, q = unit(u)
                        for k in range(q + 1):
                            mm = pe.matmul(banks(ps, 6, 2)[HD * h:HD * (h + 1), q * P:(q + 1) * P],
                                           v[s][:, k, HD * h:HD * (h + 1)], probT[u % 2][:, k * P:(k + 1) * P],
                                           start=(k == 0), stop=(k == q))
                        mm.then_inc(pv_done, 1)

                    pe.wait_ge(roped, 6 * (2 * i + s) + 6)
                    for t in range(2 * TT):
                        mm = pe.transpose(banks(ps, 0, 4)[:, t * P:(t + 1) * P], qk[s][:, t, :], ident[:])
                    mm.then_inc(turned, 1)
                    pe.wait_ge(split_done, 3 * (2 * i + s) + 3)
                    scores(0)
                    scores(1)
                    scores(2)
                    turn(0)
                    for u in range(UNITS):
                        if u + 3 < UNITS:
                            scores(u + 3)
                        pe.wait_ge(probT_done, base + u + 1)
                        if u + 1 < UNITS:
                            turn(u + 1)
                        values(u)
                    pe.wait_ge(pv_done, base + UNITS + 2)
                    pe.sem_inc(heads_free, 1)

        @block.scalar
        def _(act):
            act.wait_ge(zeroed, 4)
            with act.Fori(0, 2) as i:
                for s in range(2):
                    base = i * 2 * UNITS + s * UNITS

                    def exponent(u):
                        act.wait_ge(neg_done, base + u + 1)
                        x = prob[u % 3][:, 0:(unit(u)[1] + 1) * P]
                        act.activation(x, x, ACT.Exp, bias=neg[:, u:u + 1], accum_out=total[:, u:u + 1]).then_inc(exp_done, 1)

                    act.wait_ge(turned, 2 * i + s + 1)
                    for h in range(2):
                        rows = slice(HD * h, HD * (h + 1))
                        act.mul(q_hi[h][rows, :], banks(ps, 0, 2)[rows, :], SCALE).then_inc(hi_done, 1)
                    act.copy(k_hi[:], banks(ps, 2, 2)).then_inc(hi_done, 1)
                    exponent(0)
                    for u in range(UNITS):
                        if u + 1 < UNITS:
                            exponent(u + 1)
                        act.wait_ge(prob_turned, base + u + 4)
                        act.wait_ge(pv_done, base + u + 1)
                        w = (unit(u)[1] + 1) * P
                        act.copy(probT[u % 2][:, 0:w], banks(ps, 4, 2)[:, 0:w]).then_inc(probT_done, 1)
                    act.wait_ge(pv_done, base + UNITS + 2)
                    act.copy(mix_hi[:, ds(2 * i + s, 1), :], banks(ps, 6, 2)).then_inc(mix_hi_done, 1)

        @block.vector
        def _(dve):
            for x in (q_hi, q_lo):
                for h in range(2):
                    rows = slice(HD * (1 - h), HD * (2 - h))
                    dve.memset(x[h][rows, :].bitcast(F32), 0.0).then_inc(zeroed, 1)
            dve.wait_ge(zeroed, 4)
            dve.wait_ge(tables, 32)
            with dve.Fori(0, 2) as i:
                for s in range(2):
                    base = i * 2 * UNITS + s * UNITS

                    def score(u):
                        w = (unit(u)[1] + 1) * P
                        dve.wait_ge(made, base + u + 1)
                        dve.wait_ge(prob_turned, base + u + 1)
                        dve.memset(waited[:], 0.0)
                        dve.tensor_tensor_reduce(prob[u % 3][:, 0:w], banks(ps, 2 * (u % 2), 2)[:, 0:w],
                                                 bias[:, S - w:S], 1.0, NEG, ALU.add, ALU.max,
                                                 top[:, u:u + 1]).then_inc(scored, 1)
                        dve.wait_ge(scored, base + u + 1)
                        dve.tensor_scalar(neg[:, u:u + 1], top[:, u:u + 1], -1.0, None, ALU.mult).then_inc(neg_done, 1)

                    def normalise(u):
                        w = (unit(u)[1] + 1) * P
                        dve.wait_ge(exp_done, base + u + 1)
                        dve.reciprocal(inv[:, u:u + 1], total[:, u:u + 1]).then_inc(inv_done, 1)
                        dve.wait_ge(inv_done, base + u + 1)
                        dve.tensor_scalar(prob[u % 3][:, 0:w], prob[u % 3][:, 0:w], inv[:, u:u + 1], None,
                                          ALU.mult).then_inc(prob_done, 1)

                    for h in range(2):
                        rows = slice(HD * h, HD * (h + 1))
                        dve.wait_ge(hi_done, 3 * (2 * i + s) + h + 1)
                        dve.scalar_tensor_tensor(out=q_lo[h][rows, :], in0=banks(ps, 0, 2)[rows, :], scalar=SCALE,
                                                 in1=q_hi[h][rows, :].bitcast(F32), op0=ALU.mult,
                                                 op1=ALU.subtract).then_inc(split_done, 1)
                    dve.wait_ge(hi_done, 3 * (2 * i + s) + 3)
                    dve.tensor_tensor(k_lo[:], banks(ps, 2, 2), k_hi[:].bitcast(F32), ALU.subtract).then_inc(split_done, 1)
                    score(0)
                    for u in range(UNITS):
                        if u + 1 < UNITS:
                            score(u + 1)
                        normalise(u)
                    dve.wait_ge(mix_hi_done, 2 * i + s + 1)
                    dve.tensor_tensor(mix_lo[:, ds(2 * i + s, 1), :], banks(ps, 6, 2),
                                      mix_hi[:, ds(2 * i + s, 1), :].bitcast(F32), ALU.subtract).then_inc(mix_done, 1)



def signal(steps, sem):
    steps.wait()
    steps.eng.sem_inc(sem, 1)


def rotate(steps, x, out, table, tmp):
    e = steps.eng
    a, b = x[..., 0], x[..., 1]
    cos, sin = table
    for dst, u, w in ((0, a, cos), (1, b, sin), (2, b, cos), (3, a, sin)):
        steps.done(e.tensor_tensor(tmp[dst], u, w, ALU.mult))
    steps.wait()
    steps.done(e.tensor_tensor(out[..., 0], tmp[0], tmp[1], ALU.subtract))
    steps.done(e.tensor_tensor(out[..., 1], tmp[2], tmp[3], ALU.add))


def group_norm(steps, v_ready, root, nth, src, dst, stats, mv, rows, n):
    e = steps.eng
    for j in range(n):
        steps.done(e.bn_stats(stats[rows, j, :], src(j)))
    steps.wait()
    for j in range(n):
        steps.done(e.bn_aggr(mv[rows, j, 0:2], stats[rows, j, :]))
    steps.wait()
    col = lambda c: mv[rows, 0:n, c]
    steps.done(e.tensor_scalar(col(1), col(1), EPS, None, ALU.add))
    signal(steps, v_ready)
    e.wait_ge(root, nth)
    steps.then(e.reciprocal(col(3), col(2)))
    steps.then(e.tensor_tensor(col(4), col(3), col(3), ALU.mult))
    steps.then(e.tensor_tensor(col(4), col(4), col(1), ALU.mult))
    steps.then(e.tensor_scalar(col(4), col(4), -0.5, 1.5, ALU.mult, ALU.add))
    steps.then(e.tensor_tensor(col(3), col(3), col(4), ALU.mult))
    for j in range(n):
        steps.done(e.tensor_scalar(dst(j), src(j), mv[rows, j, 0:1], mv[rows, j, 3:4], ALU.subtract, ALU.mult))
    steps.wait()


def stage_prompt_retention(nc, io, ps, ident, mix_hi, mix_lo):
    st = Stage(nc, "ret")
    W2 = 2 * RV
    with st.ctx:
        rot = st.sb("rot", [P, 2, TT, RD])
        dmask = st.sb("dmask", [P, RH, P])
        dout = st.sb("dout", [P, 2, P])
        din, gch = st.sb("din", [P, RH]), st.sb("gch", [P, 2])
        gain = st.sb("gain", [P, RH * RV])
        q_in = [st.sb(f"q{a}", [P, TT, P]) for a in range(2)]
        k_in = [st.sb(f"k{a}", [P, TT, P]) for a in range(2)]
        v = [st.sb(f"v{a}", [P, TT, W2]) for a in range(2)]
        g = [st.sb(f"g{a}", [P, TT, W2]) for a in range(2)]
        eg = st.sb("eg", [P, TT, W2])
        q_rot, k_rot = st.sb("q_rot", [P, TT, P]), st.sb("k_rot", [P, TT, P])
        kd = st.sb("kd", [P, TT, P])
        qT, kT, qdT = (st.sb(n, [P, S]) for n in ("qT", "kT", "qdT"))
        sT = [st.sb(f"sT{h}", [P, S]) for h in range(2)]
        state = st.sb("state", [P, TT, P])
        on = [st.sb(f"on{h}", [P, S]) for h in range(2)]
        tmp_q = [qT[:, j * 512:(j + 1) * 512].rearrange("p (t j) -> p t j", t=TT) for j in range(2)] + \
                [qdT[:, j * 512:(j + 1) * 512].rearrange("p (t j) -> p t j", t=TT) for j in range(2)]
        tmp_k = [st.sb(f"tmp_k{j}", [P, TT, RD]) for j in range(4)]
        stats = st.sb("stats", [P, TT, 6])
        mv = st.sb("mv", [P, TT, 5])
        tables, gate_sum, gate_inv = st.sem("tables"), st.sem("gate_sum"), st.sem("gate_inv")
        loaded = [st.sem(f"loaded{a}") for a in range(2)]
        dve_s, pool_s, act_s, pe_s = (st.sem(n) for n in ("dve_steps", "pool_steps", "act_steps", "pe_steps"))
        (q_ready, k_ready, q_turned, k_turned, qT_done, kT_done, qd_done, kd_done, kv_made, states_done, sT_made,
         sT_done, o_made, v_ready, root, on_ready, o_turned, hi_done, exp_done, gate_done, mixed, state_put) = (
            st.sem(n) for n in (
                "q_ready", "k_ready", "q_turned", "k_turned", "qT_done", "kT_done", "qd_done", "kd_done", "kv_made",
                "states_done", "sT_made", "sT_done", "o_made", "v_ready", "root", "on_ready", "o_turned", "hi_done",
                "exp_done", "gate_done", "mixed", "state_put"))
        proj = io["proj"][0:S, :].rearrange("(t p) c -> p t c", p=P)
        QC, KC, VC, GC = 3 * AW, 3 * AW + RH * RD, 3 * AW + 2 * RH * RD, 3 * AW + 2 * RH * RD + RH * RV
        even_odd = lambda x: x.rearrange("p t (j e) -> p t j e", e=2)
        by_chunk = lambda x: x.rearrange("p (t c) -> p t c", t=TT)
        O_BANK = (2, 4)
        T_BANK = (6, 0)
        block = st.block()

        @block.sync
        def _(sp):
            for a in range(2):
                sp.dma_start(q_in[a][:], proj[:, :, QC + a * P:QC + (a + 1) * P]).then_inc(loaded[a], 16)
                sp.dma_start(k_in[a][:], proj[:, :, KC + a * P:KC + (a + 1) * P]).then_inc(loaded[a], 16)
                if a == 0:
                    for dst, n in ((rot[:].rearrange("p a b c -> p (a b c)"), "rot_p"),
                                   (dmask[:].rearrange("p a b -> p (a b)"), "dmask_p"),
                                   (dout[:].rearrange("p a b -> p (a b)"), "dout_p"), (din[:], "din_p"), (gch[:], "gchunk_p")):
                        sp.dma_start(dst, io[n]).then_inc(tables, 16)
                    sp.dma_start(gain[:], io["ret_gain"][0].partition_broadcast(P)).then_inc(tables, 16)
                sp.dma_start(v[a][:], proj[:, :, VC + a * W2:VC + (a + 1) * W2]).then_inc(loaded[a], 16)
                sp.dma_start(g[a][:], proj[:, :, GC + a * W2:GC + (a + 1) * W2]).then_inc(loaded[a], 16)
            for a in range(2):
                sp.wait_ge(states_done, a + 1)
                sp.dma_start(io["ret_prompt"][0, 0, 2 * a:2 * a + 2].rearrange("h d e -> (h d) e"),
                             state[:, TT - 1, :]).then_inc(state_put, 16)
            sp.wait_ge(state_put, 32)

        @block.gpsimd
        def _(pool):
            steps = Steps(pool, pool_s)
            pool.wait_ge(tables, 96)
            for a in range(2):
                pool.wait_ge(loaded[a], 64)
                if a:
                    pool.wait_ge(k_turned, a)
                    pool.wait_ge(kd_done, a)
                rotate(steps, even_odd(k_in[a][:]), even_odd(k_rot[:]), (rot[:, 0], rot[:, 1]), [x[:] for x in tmp_k])
                signal(steps, k_ready)
                pool.wait_ge(exp_done, a + 1)
                if a:
                    pool.wait_ge(mixed, 2 * a)
                steps.then(pool.tensor_scalar(eg[:], eg[:], 1.0, 1.0, ALU.add, ALU.mult))
                signal(steps, gate_sum)
                pool.wait_ge(gate_inv, a + 1)
                steps.then(pool.tensor_tensor(g[a][:], g[a][:], eg[:], ALU.mult))
                steps.then(pool.tensor_tensor(g[a][:], g[a][:], gain[:, a * W2:(a + 1) * W2].unsqueeze(1).broadcast_to([P, TT, W2]),
                                              ALU.mult))
                signal(steps, gate_done)

        @block.scalar
        def _(act):
            steps = Steps(act, act_s)
            for a in range(2):
                act.wait_ge(loaded[a], 64)
                if a:
                    act.wait_ge(gate_done, a)
                act.activation(eg[:], g[a][:], ACT.Exp, scale=-1.0).then_inc(exp_done, 1)
                act.wait_ge(q_turned, a + 1)
                act.copy(qT[:], banks(ps, 0, 2)).then_inc(qT_done, 1)
                act.wait_ge(k_turned, a + 1)
                act.mul(kT[:], banks(ps, 2, 2), RD ** -0.5).then_inc(kT_done, 1)
                for h in range(2):
                    n = 2 * a + h
                    act.wait_ge(v_ready, n + 1)
                    act.activation(mv[:, :, 2], mv[:, :, 1], ACT.Sqrt).then_inc(root, 1)
                    act.wait_ge(o_turned, n + 1)
                    act.copy(mix_hi[:, 4 + n, :], banks(ps, T_BANK[h], 2)).then_inc(hi_done, 1)

        @block.vector
        def _(dve):
            steps = Steps(dve, dve_s)
            dve.wait_ge(tables, 96)
            for a in range(2):
                dve.wait_ge(loaded[a], 64)
                if a:
                    dve.wait_ge(o_made, 2 * a)
                rotate(steps, even_odd(q_in[a][:]), even_odd(q_rot[:]), (rot[:, 0], rot[:, 1]), tmp_q)
                signal(steps, q_ready)
                dve.wait_ge(k_ready, a + 1)
                if a:
                    dve.wait_ge(kv_made, a)
                for h in range(2):
                    cols = slice(RD * h, RD * (h + 1))
                    steps.done(dve.tensor_scalar(kd[:, :, cols], k_rot[:, :, cols], din[:, 2 * a + h:2 * a + h + 1],
                                                 None, ALU.mult))
                signal(steps, kd_done)
                dve.wait_ge(qT_done, a + 1)
                steps.done(dve.tensor_tensor(by_chunk(qdT[:]), by_chunk(qT[:]),
                                             dout[:, a, :].unsqueeze(1).broadcast_to([P, TT, P]), ALU.mult))
                signal(steps, qd_done)
                dve.wait_ge(kv_made, a + 1)
                if a:
                    dve.wait_ge(state_put, 16 * a)
                kv = by_chunk(banks(ps, 4, 2))
                steps.then(dve.tensor_copy(state[:, 0, :], kv[:, 0, :]))
                for t in range(1, TT):
                    steps.then(dve.scalar_tensor_tensor(out=state[:, t, :], in0=state[:, t - 1, :], scalar=gch[:, a:a + 1],
                                                        in1=kv[:, t, :], op0=ALU.mult, op1=ALU.add))
                signal(steps, states_done)
                for h in range(2):
                    dve.wait_ge(sT_made, 2 * a + h + 1)
                    steps.done(dve.tensor_tensor(by_chunk(sT[h][:]), by_chunk(banks(ps, T_BANK[h], 2)),
                                                 dmask[:, 2 * a + h, :].unsqueeze(1).broadcast_to([P, TT, P]), ALU.mult))
                    signal(steps, sT_done)
                dve.wait_ge(exp_done, a + 1)
                dve.wait_ge(gate_sum, a + 1)
                steps.done(dve.reciprocal(eg[:], eg[:]))
                signal(steps, gate_inv)
                for h in range(2):
                    n = 2 * a + h
                    o = by_chunk(banks(ps, O_BANK[h], 2))
                    dst = by_chunk(on[h][:])
                    dve.wait_ge(o_made, n + 1)
                    group_norm(steps, v_ready, root, n + 1, lambda j: o[:, j, :], lambda j: dst[:, j, :],
                               stats, mv, slice(0, P), TT)
                    dve.wait_ge(gate_done, a + 1)
                    steps.done(dve.tensor_tensor(dst, dst, g[a][:, :, RV * h:RV * (h + 1)], ALU.mult))
                    signal(steps, on_ready)
                    dve.wait_ge(hi_done, n + 1)
                    steps.done(dve.tensor_tensor(mix_lo[:, 4 + n, :], banks(ps, T_BANK[h], 2),
                                                 mix_hi[:, 4 + n, :].bitcast(F32), ALU.subtract))
                    signal(steps, mixed)

        @block.tensor
        def _(pe):
            def turn(src, first, sem):
                for t in range(TT):
                    mm = pe.transpose(banks(ps, first, 2)[:, t * P:(t + 1) * P], src(t), ident[:])
                mm.then_inc(sem, 1)

            for a in range(2):
                if a:
                    pe.wait_ge(mixed, 2 * a)
                pe.wait_ge(q_ready, a + 1)
                turn(lambda t: q_rot[:, t, :], 0, q_turned)
                pe.wait_ge(k_ready, a + 1)
                turn(lambda t: k_rot[:, t, :], 2, k_turned)
                pe.wait_ge(kd_done, a + 1)
                for h in range(2):
                    for t in range(TT):
                        mm = pe.matmul(banks(ps, 4, 2)[RD * h:RD * (h + 1), t * P:(t + 1) * P],
                                       kd[:, t, RD * h:RD * (h + 1)], v[a][:, t, RV * h:RV * (h + 1)],
                                       start=True, stop=True)
                mm.then_inc(kv_made, 1)
                pe.wait_ge(qT_done, a + 1)
                pe.wait_ge(kT_done, a + 1)
                pe.wait_ge(qd_done, a + 1)
                for h in range(2):
                    rows = slice(RD * h, RD * (h + 1))
                    for t in range(TT):
                        cols = slice(t * P, (t + 1) * P)
                        mm = pe.matmul(banks(ps, T_BANK[h], 2)[:, cols], kT[rows, cols], qT[rows, cols], start=True, stop=True)
                    mm.then_inc(sT_made, 1)
                pe.wait_ge(states_done, a + 1)
                for h in range(2):
                    rows = slice(RD * h, RD * (h + 1))
                    pe.wait_ge(sT_done, 2 * a + h + 1)
                    for t in range(TT):
                        cols = slice(t * P, (t + 1) * P)
                        out = banks(ps, O_BANK[h], 2)[:, cols]
                        mm = pe.matmul(out, sT[h][:, cols], v[a][:, t, RV * h:RV * (h + 1)], start=True, stop=(t == 0))
                        if t:
                            mm = pe.matmul(out, qdT[rows, cols], state[rows, t - 1, :], start=False, stop=True)
                    mm.then_inc(o_made, 1)
                for h in range(2):
                    pe.wait_ge(on_ready, 2 * a + h + 1)
                    turn(lambda t: on[h][:, t * P:(t + 1) * P], T_BANK[h], o_turned)



def stage_sample_heads(nc, io, ps, ident, mix_s, q_blocks, kT_new):
    st = Stage(nc, "smp")
    QC, KC, VC, GC = 3 * AW, 3 * AW + RH * RD, 3 * AW + 2 * RH * RD, 3 * AW + 2 * RH * RD + RH * RV
    with st.ctx:
        x, lo_rows = st.sb("x", [NS, IN_W]), st.sb("lo_rows", [NS, IN_W])
        rope = st.sb("rope", [NS, 2, 2 * H, 8])
        rot = st.sb("rot", [NS, 2, 2 * RH * RD // 2])
        dmask = st.sb("dmask", [NS, RH * NS])
        dout = st.sb("dout", [P, RH, 4, NS])
        din = st.sb("din", [NS, RH, 4, P])
        gain = st.sb("gain", [NS, RH * RV])
        state = st.sb("state", [P, 4, RH, RV])
        tmp = [st.sb(f"tmp{j}", [NS, 256]) for j in range(4)]
        turned_qk = st.sb("rotated", [NS, 1, 2 * RH * RD])
        twice = st.sb("twice", [NS, 2 * RH, 2, RD])
        qT, kT = st.sb("qT", [P, RH, NS]), st.sb("kT", [P, RH, NS])
        q_masked = st.sb("q_masked", [P, RH, 4, NS])
        k_masked = st.sb("k_masked", [NS, RH, 4, P])
        sT = st.sb("sT", [NS, RH * NS])
        on = st.sb("on", [NS, RH * RV])
        eg = st.sb("eg", [NS, RH * RV])
        stats, mv = st.sb("stats", [NS, RH, 6]), st.sb("mv", [NS, RH, 5])
        (tables, x_in, s_in, dve_s, roped, put, rotated, att_turned, ret_turned, qT_done, sT_made, sT_done, kv_made, o_made,
         v_ready, root, on_ready, o_turned, hi_done, exp_done, state_done, g_ready, all_masked) = (st.sem(n) for n in (
            "tables", "x_in", "s_in", "dve_steps", "roped", "put", "rotated", "att_turned", "ret_turned", "qT_done", "sT_made",
            "sT_done", "kv_made", "o_made", "v_ready", "root", "on_ready", "o_turned", "hi_done", "exp_done", "state_done",
            "g_ready", "all_masked"))
        flat = lambda t: t[:].rearrange("p a b -> p (a b)")
        flat4 = lambda t: t[:].rearrange("p a b c -> p (a b c)")
        st_in = io["state_ret"][0].rearrange("(q b) h d e -> b d q h e", b=2)
        st_out = io["ret_sample"][0].rearrange("(q b) h d e -> b d q h e", b=2)
        block = st.block()

        @block.sync
        def _(sp):
            sp.dma_start(x[:], io["proj"][S:S + NS, :]).then_inc(x_in, 16)
            sp.dma_start(lo_rows[:], io["proj"][S + NS:S + P, :]).then_inc(x_in, 16)
            sp.dma_start(flat4(rope), io["rope_s"]).then_inc(tables, 16)
            for dst, n in ((flat(rot), "rot_s"), (dmask[:], "dmask_s"), (flat4(dout), "dout_s"), (flat4(din), "din_s")):
                sp.dma_start(dst, io[n]).then_inc(tables, 16)
            sp.dma_start(gain[:], io["ret_gain"][0].partition_broadcast(NS)).then_inc(tables, 16)
            for b in range(2):
                for q in range(4):
                    sp.dma_start(state[RD * b:RD * (b + 1), q], st_in[b, :, q]).then_inc(s_in, 16)
            sp.wait_ge(roped, 1)
            sp.dma_start(io["k_sample"].rearrange("o b t h d -> (o b t) (h d)"), x[:, AW:2 * AW]).then_inc(put, 16)
            sp.dma_start(io["v_sample"].rearrange("o b t h d -> (o b t) (h d)"), x[:, 2 * AW:3 * AW]).then_inc(put, 16)
            sp.wait_ge(state_done, 1)
            for b in range(2):
                for q in range(4):
                    sp.dma_start(st_out[b, :, q], state[RD * b:RD * (b + 1), q]).then_inc(put, 16)
            sp.wait_ge(put, 16 * 10)

        @block.vector
        def _(dve):
            steps = Steps(dve, dve_s)
            steps.done(dve.memset(q_blocks[:], 0.0))
            dve.wait_ge(x_in, 32)
            steps.then(dve.tensor_tensor(x[:], x[:], lo_rows[:], ALU.add))
            signal(steps, g_ready)
            dve.wait_ge(tables, 96)
            heads = x[:, 0:2 * AW].rearrange("p (h d) -> p h d", d=HD)
            a, b = heads[:, :, 0:8], heads[:, :, 8:16]
            t8 = [t[:, 0:128].rearrange("p (h j) -> p h j", j=8) for t in tmp]
            for dst, u, w in ((0, a, 0), (1, b, 1), (2, b, 0), (3, a, 1)):
                steps.done(dve.tensor_tensor(t8[dst], u, rope[:, w], ALU.mult))
            steps.wait()
            steps.done(dve.tensor_tensor(a, t8[0], t8[1], ALU.subtract))
            steps.done(dve.tensor_tensor(b, t8[2], t8[3], ALU.add))
            signal(steps, roped)
            qk = x[:, QC:VC].rearrange("p (o j e) -> p o j e", o=1, e=2)
            rotate(steps, qk, turned_qk[:].rearrange("p o (j e) -> p o j e", e=2),
                   (rot[:, 0:1], rot[:, 1:2]), [t[:].unsqueeze(1) for t in tmp])
            steps.wait()
            rr = turned_qk[:, 0].rearrange("p (h d) -> p h d", d=RD)
            steps.done(dve.tensor_copy(twice[:], rr.unsqueeze(2).broadcast_to([NS, 2 * RH, 2, RD])))
            signal(steps, rotated)
            for h in range(RH):
                dup = twice[:, RH + h].rearrange("p a d -> p (a d)")
                steps.done(dve.tensor_tensor(k_masked[:, h], dup.unsqueeze(1).broadcast_to([NS, 4, P]), din[:, h], ALU.mult))
            dve.wait_ge(att_turned, 1)
            for h in range(H):
                rows = slice(HD * (h % 2), HD * (h % 2 + 1))
                src = ps[rows, 0, (h // 2) * NS:(h // 2 + 1) * NS].rearrange("p (b t) -> p b t", b=DB)
                steps.done(dve.tensor_scalar(q_blocks[rows, :, h // 2, h * DS:(h + 1) * DS], src, SCALE, None, ALU.mult))
            steps.done(dve.tensor_copy(kT_new[:], ps[:, 0, 4 * NS:8 * NS].rearrange("p (c n) -> p c n", n=NS)))
            dve.wait_ge(ret_turned, 1)
            steps.done(dve.tensor_copy(flat(qT), ps[:, 1, 0:RH * NS]))
            steps.done(dve.tensor_scalar(flat(kT), ps[:, 1, RH * NS:2 * RH * NS], RD ** -0.5, None, ALU.mult))
            steps.wait()
            for h in range(RH):
                steps.done(dve.tensor_tensor(q_masked[:, h], qT[:, h].unsqueeze(1).broadcast_to([P, 4, NS]), dout[:, h], ALU.mult))
            signal(steps, qT_done)
            dve.wait_ge(sT_made, 1)
            steps.done(dve.tensor_tensor(sT[:], ps[0:NS, 2, 0:RH * NS], dmask[:], ALU.mult))
            signal(steps, sT_done)
            dve.wait_ge(exp_done, 1)
            steps.then(dve.tensor_scalar(eg[:], eg[:], 1.0, None, ALU.add))
            steps.then(dve.reciprocal(eg[:], eg[:]))
            steps.then(dve.tensor_tensor(eg[:], eg[:], x[:, GC:], ALU.mult))
            steps.then(dve.tensor_tensor(eg[:], eg[:], gain[:], ALU.mult))
            dve.wait_ge(o_made, 1)
            o = ps[0:NS, 3, :].rearrange("p (h e) -> p h e", e=RV)
            oo = on[:].rearrange("p (h e) -> p h e", e=RV)
            group_norm(steps, v_ready, root, 1, lambda j: o[:, j, :], lambda j: oo[:, j, :], stats, mv, slice(0, NS), RH)
            steps.done(dve.tensor_tensor(on[:], on[:], eg[:], ALU.mult))
            signal(steps, on_ready)
            dve.wait_ge(kv_made, 1)
            for h in range(RH):
                steps.done(dve.scalar_tensor_tensor(out=state[:, :, h, :], in0=state[:, :, h, :], scalar=GCHUNK_S[h],
                                                    in1=ps[:, 4:8, h * RV:(h + 1) * RV], op0=ALU.mult, op1=ALU.add))
            signal(steps, state_done)
            dve.wait_ge(hi_done, 1)
            src = ps[:, 2, 0:RH * NS].rearrange("p (h n) -> p h n", n=NS)
            steps.then(dve.tensor_tensor(mix_s[:, 4:8, NS:P], src, mix_s[:, 4:8, 0:NS].bitcast(F32), ALU.subtract))

        @block.scalar
        def _(act):
            act.wait_ge(g_ready, 1)
            act.activation(eg[:], x[:, GC:], ACT.Exp, scale=-1.0).then_inc(exp_done, 1)
            act.wait_ge(v_ready, 1)
            act.activation(mv[:, :, 2], mv[:, :, 1], ACT.Sqrt).then_inc(root, 1)
            act.wait_ge(o_turned, 1)
            act.copy(mix_s[:, 4:8, 0:NS], ps[:, 2, 0:RH * NS].rearrange("p (h n) -> p h n", n=NS)).then_inc(hi_done, 1)

        @block.tensor
        def _(pe):
            pe.wait_ge(roped, 1)
            for c in range(8):
                mm = pe.transpose(ps[:, 0, c * NS:(c + 1) * NS], x[:, c * P:(c + 1) * P], ident[0:NS, 0:NS])
            mm.then_inc(att_turned, 1)
            pe.wait_ge(rotated, 1)
            for c in range(2 * RH):
                mm = pe.transpose(ps[:, 1, c * NS:(c + 1) * NS], twice[:, c].rearrange("p a d -> p (a d)"), ident[0:NS, 0:NS])
            mm.then_inc(ret_turned, 1)
            pe.wait_ge(qT_done, 1)
            pe.wait_ge(s_in, 128)
            vcols = lambda h: x[:, VC + h * RV:VC + (h + 1) * RV]
            for h in range(RH):
                mm = pe.matmul(ps[0:NS, 2, h * NS:(h + 1) * NS], kT[0:RD, h, :], qT[0:RD, h, :], start=True, stop=True)
            mm.then_inc(sT_made, 1)
            for h in range(RH):
                for b in range(4):
                    mm = pe.matmul(ps[:, 4 + b, h * RV:(h + 1) * RV], k_masked[:, h, b, :], vcols(h), start=True, stop=True)
            mm.then_inc(kv_made, 1)
            pe.wait_ge(sT_done, 1)
            for h in range(RH):
                out = ps[0:NS, 3, h * RV:(h + 1) * RV]
                pe.matmul(out, sT[:, h * NS:(h + 1) * NS], vcols(h), start=True, stop=False)
                for b in range(4):
                    mm = pe.matmul(out, q_masked[:, h, b, :], state[:, b, h, :], start=False, stop=(b == 3))
            mm.then_inc(o_made, 1)
            pe.wait_ge(on_ready, 1)
            for h in range(RH):
                mm = pe.transpose(ps[:, 2, h * NS:(h + 1) * NS], on[:, h * RV:(h + 1) * RV], ident[0:NS, 0:NS])
            mm.then_inc(o_turned, 1)



def stage_sample_attention(nc, io, ps, ident, mix_s, q_blocks, kT_new):
    st = Stage(nc, "cache")
    CHUNKS = ((0, 4), (4, 4), (8, 2))
    with st.ctx:
        bias = st.sb("bias", [P, NKEYS])
        K = [st.sb(f"K{b}", [P, KTILES, AW]) for b in range(2)]
        V = [st.sb(f"V{b}", [P, KTILES, AW]) for b in range(2)]
        v_new = [st.sb(f"v_new{b}", [DS, AW]) for b in range(2)]
        q_now = st.sb("q_now", [P, 2, 4, NS])
        k_now = st.sb("k_now", [P, 4, 2 * DS])
        kT = [st.sb(f"kT{s}", [P, 4, CH]) for s in range(2)]
        prob = st.sb("prob", [P, NKEYS])
        probT = st.sb("probT", [P, KTILES + 1, P])
        rows = st.sb("rows", [P, AW])
        top, neg, total, inv, waited = (st.sb(n, [P, 1]) for n in ("top", "neg", "total", "inv", "waited"))
        mix_f = st.sb("mix_f", [P, 4, NS])
        k_in, v_in = ([st.sem(f"{n}_in{b}") for b in range(2)] for n in "kv")
        (tables, k_free, v_free, q_staged, turned, kT_act, kT_dve, scored, s_made, neg_done, exp_done, inv_done, p_turned,
         pT_act, pT_dve, pv_made, rows_done, rows_turned, out_act, out_dve, hi_done, mixed) = (st.sem(n) for n in (
            "tables", "k_free", "v_free", "q_staged", "turned", "kT_act", "kT_dve", "scored", "s_made", "neg_done", "exp_done",
            "inv_done", "p_turned", "pT_act", "pT_dve", "pv_made", "rows_done", "rows_turned", "out_act", "out_dve",
            "hi_done", "mixed"))
        v_put = io["v_sample"].rearrange("o b t h d -> t (o b) (h d)")
        block = st.block()

        @block.sync
        def _(sp):
            sp.dma_start(bias[:], io["bias_s"]).then_inc(tables, 16)
            with sp.Fori(0, 4) as i:
                for b in range(2):
                    seq = sp.snap(2 * i + b)
                    sp.wait_ge(k_free, 2 * i + b + 1)
                    for cache, dst, sem in ((io["cache_k"], K[b], k_in[b]), (io["cache_v"], V[b], v_in[b])):
                        if sem is v_in[b]:
                            sp.wait_ge(v_free, 2 * i + b + 1)
                        src = cache[0, ds(seq, 1)].rearrange("o n h d -> (o n) (h d)")
                        old = src[0:OLD, :].rearrange("(j g r) c -> j g r c", g=16, r=16)
                        for j in range(6):
                            sp.dma_start(dst[:, j, :], old[j, :, 0:8]).then_inc(sem, 16)
                        sp.dma_start(dst[:, 6:, :], src[OLD:, :].rearrange("(j p) c -> p j c", p=P)).then_inc(sem, 16)
                    sp.dma_start(v_new[b][:], v_put[:, ds(seq, 1), :]).then_inc(v_in[b], 16)

        @block.tensor
        def _(pe):
            pe.sem_inc(k_free, 2)
            pe.sem_inc(v_free, 2)
            with pe.Fori(0, 4) as i:
                def turn(n):
                    b, (first, count) = n // 3, CHUNKS[n % 3]
                    if n % 3 == 0:
                        pe.wait_ge(k_in[b], 16 * 7 * i + 16 * 7)
                    for c in range(4):
                        for j in range(count):
                            mm = pe.transpose(ps[:, c, j * P:(j + 1) * P], K[b][:, first + j, c * P:(c + 1) * P], ident[:])
                    mm.then_inc(turned, 1)

                def scores(n):
                    b, (first, count) = n // 3, CHUNKS[n % 3]
                    w = count * P + (DS if n % 3 == 2 else 0)
                    if n == 0:
                        pe.wait_ge(q_staged, 2 * i + 2)
                    for c in range(4):
                        mm = pe.matmul(ps[NS * b:NS * (b + 1), 4 + n % 3, 0:w], q_now[:, b, c, :], kT[n % 2][:, c, 0:w],
                                       start=(c == 0), stop=(c == 3))
                    mm.then_inc(scored, 1)

                turn(0)
                for n in range(6):
                    pe.wait_ge(kT_act, 6 * i + n + 1)
                    pe.wait_ge(kT_dve, 6 * i + n + 1)
                    if n + 1 < 6:
                        turn(n + 1)
                    scores(n)
                    if n % 3 == 2:
                        pe.wait_ge(scored, 6 * i + n + 1)
                        pe.sem_inc(k_free, 1)
                pe.wait_ge(exp_done, i + 1)
                for j in range(KTILES + 1):
                    w = P if j < KTILES else DS
                    out = ps[:, j // 4, (j % 4) * P:(j % 4 + 1) * P] if j < KTILES else ps[0:DS, 3, 0:P]
                    mm = pe.transpose(out, prob[:, j * P:j * P + w], ident[:])
                mm.then_inc(p_turned, 1)
                pe.wait_ge(pT_act, 2 * i + 2)
                pe.wait_ge(pT_dve, 2 * i + 2)
                for b in range(2):
                    cols = slice(NS * b, NS * (b + 1))
                    pe.wait_ge(v_in[b], 16 * 8 * i + 16 * 8)
                    for j in range(KTILES):
                        pe.matmul(ps[cols, 7, :], probT[:, j, cols], V[b][:, j, :], start=(j == 0), stop=False)
                    mm = pe.matmul(ps[cols, 7, :], probT[0:DS, KTILES, cols], v_new[b][:], start=False, stop=True)
                    mm.then_inc(pv_made, 1)
                pe.wait_ge(pv_made, 2 * i + 2)
                pe.sem_inc(v_free, 2)
                pe.wait_ge(rows_done, i + 1)
                for c in range(4):
                    mm = pe.transpose(ps[:, 4, c * P:(c + 1) * P], rows[:, c * P:(c + 1) * P], ident[:])
                mm.then_inc(rows_turned, 1)

        def head_rows(i, h):
            part = slice(HD * (h % 2), HD * (h % 2 + 1))
            src = ps[part, 4, (h // 2) * P:(h // 2 + 1) * P].rearrange("p (b h t) -> p b h t", b=2, t=DS)[:, :, h, :]
            dst = mix_f[part, h // 2, ds(i * 2 * DS, 2 * DS)].rearrange("p (b t) -> p b t", b=2)
            return dst, src

        @block.scalar
        def _(act):
            with act.Fori(0, 4) as i:
                act.copy(q_now[:], q_blocks[:, ds(2 * i, 2)]).then_inc(q_staged, 1)
                act.copy(k_now[:], kT_new[:, :, ds(i * 2 * DS, 2 * DS)]).then_inc(q_staged, 1)
                for n in range(6):
                    w = CHUNKS[n % 3][1] * P
                    act.wait_ge(turned, 6 * i + n + 1)
                    act.copy(kT[n % 2][:, 0:2, 0:w], ps[:, 0:2, 0:w]).then_inc(kT_act, 1)
                act.wait_ge(neg_done, i + 1)
                act.activation(prob[:], prob[:], ACT.Exp, bias=neg[:], accum_out=total[:]).then_inc(exp_done, 1)
                act.wait_ge(p_turned, i + 1)
                act.copy(probT[:, 0:4, :], ps[:, 0, :].rearrange("p (j n) -> p j n", n=P)).then_inc(pT_act, 1)
                act.copy(probT[:, 4:8, :], ps[:, 1, :].rearrange("p (j n) -> p j n", n=P)).then_inc(pT_act, 1)
                act.wait_ge(rows_turned, i + 1)
                for h in range(0, H, 2):
                    dst, src = head_rows(i, h)
                    act.copy(dst, src).then_inc(out_act, 1)
                act.wait_ge(out_act, 4 * i + 4)
            act.wait_ge(out_dve, 16)
            act.copy(mix_s[:, 0:4, 0:NS], mix_f[:]).then_inc(hi_done, 1)

        @block.vector
        def _(dve):
            dve.wait_ge(tables, 16)
            with dve.Fori(0, 4) as i:
                for n in range(6):
                    w = CHUNKS[n % 3][1] * P
                    dve.wait_ge(turned, 6 * i + n + 1)
                    copy = dve.tensor_copy(kT[n % 2][:, 2:4, 0:w], ps[:, 2:4, 0:w])
                    if n % 3 == 2:
                        b = n // 3
                        dve.wait_ge(q_staged, 2 * i + 2)
                        copy = dve.tensor_copy(kT[n % 2][:, :, w:w + DS], k_now[:, :, b * DS:(b + 1) * DS])
                    copy.then_inc(kT_dve, 1)
                dve.wait_ge(scored, 6 * i + 6)
                dve.memset(waited[:], 0.0)
                dve.tensor_tensor_reduce(prob[:], banks(ps, 4, 3)[:, 0:NKEYS], bias[:], 1.0, NEG, ALU.add, ALU.max,
                                         top[:]).then_inc(s_made, 1)
                dve.wait_ge(s_made, i + 1)
                dve.tensor_scalar(neg[:], top[:], -1.0, None, ALU.mult).then_inc(neg_done, 1)
                dve.wait_ge(exp_done, i + 1)
                dve.reciprocal(inv[:], total[:]).then_inc(inv_done, 1)
                dve.wait_ge(p_turned, i + 1)
                dve.tensor_copy(probT[:, 8:10, :], ps[:, 2, 0:2 * P].rearrange("p (j n) -> p j n", n=P)).then_inc(pT_dve, 1)
                dve.tensor_copy(probT[0:DS, 10, :], ps[0:DS, 3, 0:P]).then_inc(pT_dve, 1)
                dve.wait_ge(pv_made, 2 * i + 2)
                dve.wait_ge(inv_done, i + 1)
                dve.tensor_scalar(rows[:], ps[:, 7, :], inv[:], None, ALU.mult).then_inc(rows_done, 1)
                dve.wait_ge(out_act, 4 * i + 4)
                for h in range(1, H, 2):
                    dst, src = head_rows(i, h)
                    dve.tensor_copy(dst, src).then_inc(out_dve, 1)
                dve.wait_ge(out_dve, 4 * i + 4)
            dve.wait_ge(hi_done, 1)
            dve.tensor_tensor(mix_s[:, 0:4, NS:P], mix_f[:], mix_s[:, 0:4, 0:NS].bitcast(F32), ALU.subtract).then_inc(mixed, 1)



def stage_output(nc, io, ps, mix_hi, mix_lo, mix_s, x, xs, ss):
    st = Stage(nc, "outp")
    NCH, OUTS, BANKS = D // CH, TT + 1, 6
    QUARTERS = 4
    quarter = lambda q: slice(q * KT // QUARTERS, (q + 1) * KT // QUARTERS)
    with st.ctx:
        raw = st.sb("raw", [P, KT, CH])
        w_hi = [st.sb(f"whi{s}", [P, KT, CH], F32R) for s in range(NCH)]
        w_lo = [st.sb(f"wlo{s}", [P, KT, CH], F32R) for s in range(NCH)]
        gate, gate_s = st.sb("gate", [P, D]), st.sb("gate_s", [NS, D])
        row = [st.sb(f"row{s}", [P, CH]) for s in range(2)]
        sq = st.sb("sq", [P, CH])
        raw_in = [st.sem(f"raw_in{q}") for q in range(QUARTERS)]
        x_in = [st.sem(f"x_in{t}") for t in range(TT + 1)]
        g_in, gs_in, w_hi_done, w_lo_done, made, lo_done, sum_done, gated, added, squared, put, zeroed = (st.sem(n) for n in (
            "g_in", "gs_in", "w_hi_done", "w_lo_done", "made", "lo_done", "sum_done", "gated", "added", "squared", "put", "zeroed"))
        wv = io["w_out"].rearrange("o (k p) n -> p (o k) n", p=P)
        block = st.block()

        @block.sync
        def _(sp):
            def weights(c):
                for q in range(QUARTERS):
                    if c:
                        sp.wait_ge(w_lo_done, q + 1)
                    sp.dma_start(raw[:, quarter(q), :], wv[:, quarter(q), c * CH:(c + 1) * CH]).then_inc(raw_in[q], 16)

            weights(0)
            load_rows(sp, io, gate, None, G_A, g_in)
            load_rows(sp, io, None, gate_s, G_A, gs_in)
            for t in range(TT):
                sp.dma_start(x[:, t, :], io["x_prompt"][0, t * P:(t + 1) * P, :]).then_inc(x_in[t], 16)
            sp.dma_start(xs[:], io["x_sample"].rearrange("b t d -> (b t) d")).then_inc(x_in[TT], 16)
            weights(1)
            for t in range(TT):
                sp.wait_ge(added, OUTS + t + 1)
                sp.dma_start(io["x1"][t * P:(t + 1) * P, :], x[:, t, :]).then_inc(put, 16)
            sp.wait_ge(added, 2 * OUTS)
            sp.dma_start(io["x1"][S:S + NS, :], xs[:]).then_inc(put, 16)
            sp.wait_ge(put, 16 * (TT + 1))

        @block.gpsimd
        def _(pool):
            pool.memset(ss[:], 0.0).then_inc(zeroed, 1)
            for c in range(NCH):
                for o in range(OUTS):
                    n = c * OUTS + o
                    dst = x[:, o, c * CH:(c + 1) * CH] if o < TT else xs[:, c * CH:(c + 1) * CH]
                    r = row[n % 2][:] if o < TT else row[n % 2][0:NS, :]
                    pool.wait_ge(gated, n + 1)
                    pool.wait_ge(x_in[o], 16)
                    pool.tensor_tensor(dst, dst, r, ALU.add).then_inc(added, 1)

        @block.scalar
        def _(act):
            act.wait_ge(zeroed, 1)
            for c in range(NCH):
                for q in range(QUARTERS):
                    act.wait_ge(raw_in[q], 16 * c + 16)
                    act.copy(w_hi[c][:, quarter(q), :], raw[:, quarter(q), :]).then_inc(w_hi_done, 1)
            for c in range(NCH):
                for o in range(OUTS):
                    n = c * OUTS + o
                    if o == TT:
                        act.wait_ge(made, n + 1)
                        act.wait_ge(squared, n)
                        act.copy(sq[0:NS, :], ps[NS:P, n % BANKS, :]).then_inc(lo_done, 1)
                        act.wait_ge(sum_done, c + 1)
                    dst = x[:, o, c * CH:(c + 1) * CH] if o < TT else xs[:, c * CH:(c + 1) * CH]
                    rows = slice(0, P if o < TT else NS)
                    act.wait_ge(added, n + 1)
                    if n:
                        act.wait_ge(squared, n)
                    act.activation(sq[rows, :], dst, ACT.Square, accum_out=ss[rows, c, o:o + 1]).then_inc(squared, 1)

        @block.vector
        def _(dve):
            for c in range(NCH):
                for q in range(QUARTERS):
                    dve.wait_ge(w_hi_done, QUARTERS * c + q + 1)
                    dve.tensor_tensor(w_lo[c][:, quarter(q), :], raw[:, quarter(q), :],
                                      w_hi[c][:, quarter(q), :].bitcast(F32), ALU.subtract).then_inc(w_lo_done, 1)
            dve.wait_ge(g_in, 16)
            dve.wait_ge(gs_in, 16 * DB)
            for c in range(NCH):
                cols = slice(c * CH, (c + 1) * CH)
                for o in range(OUTS):
                    n = c * OUTS + o
                    dve.wait_ge(made, n + 1)
                    if n >= 2:
                        dve.wait_ge(added, n - 1)
                    if o < TT:
                        dve.tensor_tensor(row[n % 2][:], ps[:, n % BANKS, :], gate[:, cols], ALU.mult).then_inc(gated, 1)
                    else:
                        dve.wait_ge(lo_done, c + 1)
                        dve.tensor_tensor(row[n % 2][0:NS, :], ps[0:NS, n % BANKS, :], sq[0:NS, :], ALU.add).then_inc(sum_done, 1)
                        dve.wait_ge(sum_done, c + 1)
                        dve.tensor_tensor(row[n % 2][0:NS, :], row[n % 2][0:NS, :], gate_s[:, cols], ALU.mult).then_inc(gated, 1)

        @block.tensor
        def _(pe):
            for c in range(NCH):
                for o in range(OUTS):
                    n = c * OUTS + o
                    bank = ps[:, n % BANKS, :]
                    if n >= BANKS:
                        pe.wait_ge(gated, n - BANKS + 1)
                    if o < TT:
                        parts = ((mix_hi, w_hi), (mix_hi, w_lo), (mix_lo, w_hi))
                        cols = slice(o * P, (o + 1) * P)
                    else:
                        parts = ((mix_s, w_hi), (mix_s, w_lo))
                        cols = slice(0, P)
                    for k in range(KT):
                        if o == 0 and k % (KT // QUARTERS) == 0:
                            pe.wait_ge(w_lo_done, QUARTERS * c + k // (KT // QUARTERS) + 1)
                        for a, (z, w) in enumerate(parts):
                            mm = pe.matmul(bank, z[:, k, cols], w[c][:, k, :], start=(k == 0 and a == 0),
                                           stop=(k == KT - 1 and a == len(parts) - 1))
                    mm.then_inc(made, 1)



def stage_mlp(nc, io, ps, ident, z_hi, z_lo, zs, y, ys, last_rows):
    st = Stage(nc, "mlp")
    J = GF // P
    turned_s = lambda ps: ps[:, 4, GF:GF + J * P].rearrange("p (j n) -> p j n", n=P)[:, :, 0:NS]
    MAIN = 2 * J
    OUTS = 2 * (TT + 1)
    with st.ctx:
        w1_raw, w2_raw = st.sb("w1_raw", [P, KT, GF]), st.sb("w2_raw", [P, J, D])
        w1_hi, w1_lo = (st.sb(n, [P, KT, GF], F32R) for n in ("w1_hi", "w1_lo"))
        w2_hi, w2_lo = (st.sb(n, [P, J, D], F32R) for n in ("w2_hi", "w2_lo"))
        h_hi, h_lo = ([st.sb(f"{n}{s}", [P, J, S], F32R) for s in range(2)] for n in ("h_hi", "h_lo"))
        hs = [st.sb(f"hs{s}", [P, J, P], F32R) for s in range(2)]
        pos = [st.sb(f"pos{s}", [P, CH]) for s in range(2)]
        lo_part, hid_s = st.sb("lo_part", [NS, GF]), st.sb("hid_s", [P, GF])
        (w1_in, w2_in, w1_free, w2_free, w1_hi_done, w2_hi_done, w1_ready, w2_ready, made1, relu_done, sq_done, h_hi_done,
         h_ready, s_made, s_lo, s_sum, hid_done, s_turned, hs_hi, hs_ready, made2, added, h_free, zeroed) = (st.sem(n) for n in (
            "w1_in", "w2_in", "w1_free", "w2_free", "w1_hi_done", "w2_hi_done", "w1_ready", "w2_ready", "made1", "relu_done",
            "sq_done", "h_hi_done", "h_ready", "s_made", "s_lo", "s_sum", "hid_done", "s_turned", "hs_hi", "hs_ready",
            "made2", "added", "h_free", "zeroed"))
        rows_in = st.sem("rows_in")
        w1v = io["w_ff1"].rearrange("o (k p) n -> p (o k) n", p=P)
        w2v = io["w_ff2"].rearrange("o (j p) n -> p (o j) n", p=P)
        block = st.block()


        @block.sync
        def _(sp):
            for dst, m in zip(last_rows, (G_F, SC_L, SH_L)):
                load_rows(sp, io, dst, None, m, rows_in)
            with sp.Fori(0, NG) as g:
                col, tile = sp.snap(g * GF), sp.snap(g * J)
                sp.wait_ge(w1_ready, g + 1)
                sp.dma_start(w1_raw[:], w1v[:, :, ds(col, GF)]).then_inc(w1_in, 16)
                sp.wait_ge(w2_ready, g + 1)
                sp.dma_start(w2_raw[:], w2v[:, ds(tile, J), :]).then_inc(w2_in, 16)
            sp.wait_ge(rows_in, 16 * len(last_rows))

        @block.gpsimd
        def _(pool):
            pool.sem_inc(w1_ready, 1)
            pool.sem_inc(w2_ready, 1)
            pool.memset(y[:], 0.0).then_inc(zeroed, 1)
            pool.memset(ys[:], 0.0).then_inc(zeroed, 1)
            pool.memset(hid_s[:], 0.0).then_inc(zeroed, 1)

            def split_lo(lo, raw, hi, hi_done, ready, g):
                pool.wait_ge(hi_done, g + 1)
                pool.tensor_tensor(lo[:], raw[:], hi[:].bitcast(F32), ALU.subtract).then_inc(ready, 1)

            def square(g, s, u):
                j, half = divmod(u, 2)
                pool.wait_ge(relu_done, MAIN * g + u + 1)
                x = pos[u % 2][:]
                pool.tensor_tensor(x, x, x, ALU.mult).then_inc(sq_done, 1)

            def group(g, s, last=False):
                for u in range(MAIN):
                    square(g, s, u)
                if not last:
                    split_lo(w1_lo, w1_raw, w1_hi, w1_hi_done, w1_ready, g + 1)
                split_lo(w2_lo, w2_raw, w2_hi, w2_hi_done, w2_ready, g)

            split_lo(w1_lo, w1_raw, w1_hi, w1_hi_done, w1_ready, 0)
            with pool.Fori(0, NG // 2 - 1) as i:
                for s in range(2):
                    group(2 * i + s, s)
            group(NG - 2, 0)
            group(NG - 1, 1, last=True)

        @block.scalar
        def _(act):
            def split_hi(hi, raw, raw_in, free, hi_done, g):
                act.wait_ge(raw_in, 16 * g + 16)
                act.wait_ge(free, g + 1)
                act.copy(hi[:], raw[:]).then_inc(hi_done, 1)

            def hidden(g, s, u):
                j, half = divmod(u, 2)
                act.wait_ge(sq_done, MAIN * g + u + 1)
                act.copy(h_hi[s][:, j, half * CH:(half + 1) * CH], pos[u % 2][:]).then_inc(h_hi_done, 1)

            def group(g, s, last=False):
                for u in range(MAIN):
                    act.wait_ge(made1, MAIN * g + u + 1)
                    act.wait_ge(h_ready, MAIN * g + u + 1)
                    act.activation(pos[u % 2][:], ps[:, u, :], ACT.Relu).then_inc(relu_done, 1)
                    if u == 0:
                        act.wait_ge(h_free, g + 1)
                    if u:
                        hidden(g, s, u - 1)
                hidden(g, s, MAIN - 1)
                act.wait_ge(s_made, g + 1)
                act.copy(lo_part[:], ps[NS:P, 4, 0:GF]).then_inc(s_lo, 1)
                if not last:
                    split_hi(w1_hi, w1_raw, w1_in, w1_free, w1_hi_done, g + 1)
                act.wait_ge(s_turned, g + 1)
                act.copy(hs[s][:, :, 0:NS], turned_s(ps)).then_inc(hs_hi, 1)
                split_hi(w2_hi, w2_raw, w2_in, w2_free, w2_hi_done, g)

            split_hi(w1_hi, w1_raw, w1_in, w1_free, w1_hi_done, 0)
            with act.Fori(0, NG // 2 - 1) as i:
                for s in range(2):
                    group(2 * i + s, s)
            group(NG - 2, 0)
            group(NG - 1, 1, last=True)

        @block.vector
        def _(dve):
            dve.sem_inc(h_ready, 2)
            dve.sem_inc(added, 3)
            dve.sem_inc(hs_ready, 1)
            dve.wait_ge(zeroed, 3)

            def hidden(g, s):
                for u in range(MAIN):
                    j, half = divmod(u, 2)
                    cols = slice(half * CH, (half + 1) * CH)
                    dve.wait_ge(h_hi_done, MAIN * g + u + 1)
                    dve.tensor_tensor(h_lo[s][:, j, cols], pos[u % 2][:], h_hi[s][:, j, cols].bitcast(F32),
                                      ALU.subtract).then_inc(h_ready, 1)
                dve.wait_ge(s_lo, g + 1)
                dve.tensor_tensor(hid_s[0:NS, :], ps[0:NS, 4, 0:GF], lo_part[:], ALU.add).then_inc(s_sum, 1)
                dve.wait_ge(s_sum, g + 1)
                dve.scalar_tensor_tensor(out=hid_s[0:NS, :], in0=hid_s[0:NS, :], scalar=0.0, in1=hid_s[0:NS, :], op0=ALU.max,
                                         op1=ALU.mult).then_inc(hid_done, 1)

            def hidden_sample(g, s):
                dve.wait_ge(hs_hi, g + 1)
                dve.tensor_tensor(hs[s][:, :, NS:P], turned_s(ps),
                                  hs[s][:, :, 0:NS].bitcast(F32), ALU.subtract).then_inc(hs_ready, 1)

            def add(g):
                for o in range(OUTS):
                    t, c = divmod(o, 2)
                    cols = slice(c * CH, (c + 1) * CH)
                    dst = y[:, t, cols] if t < TT else ys[:, cols]
                    dve.wait_ge(made2, OUTS * g + o + 1)
                    dve.tensor_tensor(dst, dst, ps[:, 5 + o % 3, :], ALU.add).then_inc(added, 1)
                dve.wait_ge(added, OUTS * g + OUTS + 3)

            hidden(0, 0)
            hidden_sample(0, 0)
            with dve.Fori(0, NG // 2 - 1) as i:
                for s in range(2):
                    g = 2 * i + s
                    hidden(g + 1, 1 - s)
                    add(g)
                    hidden_sample(g + 1, 1 - s)
            hidden(NG - 1, 1)
            add(NG - 2)
            hidden_sample(NG - 1, 1)
            add(NG - 1)

        @block.tensor
        def _(pe):
            pe.sem_inc(w1_free, 1)
            pe.sem_inc(w2_free, 1)
            pe.sem_inc(h_free, 2)

            def first(g, s):
                pe.wait_ge(w1_ready, g + 2)
                for u in range(MAIN):
                    j, half = divmod(u, 2)
                    rows = slice(half * CH, (half + 1) * CH)
                    for k in range(KT):
                        for a, (w, z) in enumerate(((w1_hi, z_hi), (w1_hi, z_lo), (w1_lo, z_hi))):
                            mm = pe.matmul(ps[:, u, :], w[:, k, j * P:(j + 1) * P], z[:, k, rows],
                                           start=(k == 0 and a == 0), stop=(k == KT - 1 and a == 2))
                    mm.then_inc(made1, 1)
                pe.wait_ge(hs_ready, g + 1)
                for k in range(KT):
                    for a, w in enumerate((w1_hi, w1_lo)):
                        mm = pe.matmul(ps[:, 4, 0:GF], zs[:, k, :], w[:, k, :], start=(k == 0 and a == 0),
                                       stop=(k == KT - 1 and a == 1))
                mm.then_inc(s_made, 1)
                pe.wait_ge(s_made, g + 1)
                pe.sem_inc(w1_free, 1)

            def turn_sample(g, s):
                pe.wait_ge(hid_done, g + 1)
                for j in range(J):
                    mm = pe.transpose(ps[:, 4, GF + j * P:GF + (j + 1) * P], hid_s[:, j * P:(j + 1) * P], ident[:])
                mm.then_inc(s_turned, 1)

            def second(g, s):
                pe.wait_ge(w2_ready, g + 2)
                pe.wait_ge(h_ready, MAIN * g + MAIN + 2)
                for o in range(OUTS):
                    t, c = divmod(o, 2)
                    cols = slice(c * CH, (c + 1) * CH)
                    out = ps[:, 5 + o % 3, :]
                    pe.wait_ge(added, OUTS * g + o + 1)
                    if t < TT:
                        parts = [(h[s][:, j, t * P:(t + 1) * P], w[:, j, cols]) for j in range(J)
                                 for h, w in ((h_hi, w2_hi), (h_hi, w2_lo), (h_lo, w2_hi))]
                    else:
                        if c == 0:
                            pe.wait_ge(hs_ready, g + 2)
                        parts = [(hs[s][:, j, :], w[:, j, cols]) for j in range(J) for w in (w2_hi, w2_lo)]
                    for a, (h, w) in enumerate(parts):
                        mm = pe.matmul(out, h, w, start=(a == 0), stop=(a == len(parts) - 1))
                    mm.then_inc(made2, 1)
                pe.wait_ge(made2, OUTS * g + OUTS)
                pe.sem_inc(w2_free, 1)
                pe.sem_inc(h_free, 1)

            first(0, 0)
            turn_sample(0, 0)
            with pe.Fori(0, NG // 2 - 1) as i:
                for s in range(2):
                    g = 2 * i + s
                    first(g + 1, 1 - s)
                    second(g, s)
                    turn_sample(g + 1, 1 - s)
            first(NG - 1, 1)
            second(NG - 2, 0)
            turn_sample(NG - 1, 1)
            second(NG - 1, 1)



def stage_last(nc, io, y, ys, last_rows):
    st = Stage(nc, "last")
    gate, sc, sh = last_rows
    HALVES = 2
    PER = TT // HALVES
    with st.ctx:
        x1 = st.sb("x1", [P, TT, D])
        x1s, y_lo = st.sb("x1s", [NS, D]), st.sb("y_lo", [NS, D])
        gate_s, sc_s, sh_s = (st.sb(n, [NS, D]) for n in ("gate_s", "sc_s", "sh_s"))
        T = [{n: st.sb(f"{n}{h}", [P, 8]) for n in ("ss", "v", "r", "t")} for h in range(HALVES)]
        sq = st.sb("sq", [P, D])
        x_in = [st.sem(f"x_in{t}") for t in range(TT + 1)]
        m_in, dve_s, v_ready, root, gated, summed, squared, scaled, done, put, sq_zeroed = (
            st.sem(n) for n in ("m_in", "dve_steps", "v_ready", "root", "gated", "summed", "squared", "scaled", "done", "put",
                                "sq_zeroed"))
        y_out = io["y_prompt"][0].rearrange("(t p) d -> p t d", p=P)
        block = st.block()

        @block.sync
        def _(sp):
            for t in range(TT):
                sp.dma_start(x1[:, t, :], io["x1"][t * P:(t + 1) * P, :]).then_inc(x_in[t], 16)
            sp.dma_start(x1s[:], io["x1"][S:, :]).then_inc(x_in[TT], 16)
            for s, m in ((gate_s, G_F), (sc_s, SC_L), (sh_s, SH_L)):
                load_rows(sp, io, None, s, m, m_in)
            for t in range(TT):
                sp.wait_ge(done, t + 1)
                sp.dma_start(y_out[:, t, :], y[:, t, :]).then_inc(put, 16)
            sp.wait_ge(done, TT + 1)
            sp.dma_start(io["y_sample"].rearrange("b t d -> (b t) d"), x1s[:]).then_inc(put, 16)
            sp.wait_ge(put, 16 * (TT + 1))

        @block.scalar
        def _(act):
            act.wait_ge(sq_zeroed, HALVES)
            for h in range(HALVES):
                for t in range(h * PER, (h + 1) * PER):
                    act.wait_ge(summed, t + 1)
                    if t:
                        act.wait_ge(squared, t)
                    act.activation(sq[:], x1[:, t, :], ACT.Square, accum_out=T[h]["ss"][:, t % PER:t % PER + 1]).then_inc(squared, 1)
                if h:
                    act.wait_ge(summed, TT + 1)
                    act.wait_ge(squared, TT)
                    act.activation(sq[0:NS, :], x1s[:], ACT.Square, accum_out=T[h]["ss"][0:NS, PER:PER + 1]).then_inc(squared, 1)
                act.wait_ge(v_ready, h + 1)
                act.activation(T[h]["t"][:, 0:PER + 1], T[h]["v"][:, 0:PER + 1], ACT.Sqrt).then_inc(root, 1)

        @block.gpsimd
        def _(pool):
            for t in range(0, TT, 2):
                pool.tensor_tensor(y[:, t, :], y[:, t, :], gate[:], ALU.mult).then_inc(gated, 1)
            for t in range(TT):
                pool.wait_ge(scaled, t + 1)
                pool.tensor_tensor(y[:, t, :], x1[:, t, :], sh[:], ALU.add).then_inc(done, 1)
            pool.wait_ge(scaled, TT + 1)
            pool.tensor_tensor(x1s[:], x1s[:], sh_s[:], ALU.add).then_inc(done, 1)

        @block.vector
        def _(dve):
            steps = Steps(dve, dve_s)
            for h in range(HALVES):
                dve.memset(T[h]["ss"][:], 1.0).then_inc(sq_zeroed, 1)

            def residual(t):
                if t % 2:
                    steps.then(dve.tensor_tensor(y[:, t, :], y[:, t, :], gate[:], ALU.mult))
                else:
                    dve.wait_ge(gated, t // 2 + 1)
                dve.wait_ge(x_in[t], 16)
                dve.tensor_tensor(x1[:, t, :], x1[:, t, :], y[:, t, :], ALU.add).then_inc(summed, 1)

            def scale(t):
                h, j = divmod(t, PER)
                dve.scalar_tensor_tensor(out=x1[:, t, :], in0=x1[:, t, :], scalar=T[h]["r"][:, j:j + 1], in1=sc[:],
                                         op0=ALU.mult, op1=ALU.mult).then_inc(scaled, 1)

            for t in range(PER):
                residual(t)
            residual(PER)
            dve.wait_ge(squared, PER)
            rms_rows(steps, v_ready, root, T[0], PER + 1, 1)
            for t in range(PER):
                scale(t)
                if PER + 1 + t < TT:
                    residual(PER + 1 + t)
            steps.then(dve.tensor_copy(y_lo[:], ys[NS:P, :]))
            steps.then(dve.tensor_tensor(y_lo[:], y_lo[:], ys[0:NS, :], ALU.add))
            dve.wait_ge(m_in, 16 * 3 * DB)
            steps.then(dve.tensor_tensor(y_lo[:], y_lo[:], gate_s[:], ALU.mult))
            dve.wait_ge(x_in[TT], 16)
            dve.tensor_tensor(x1s[:], x1s[:], y_lo[:], ALU.add).then_inc(summed, 1)
            dve.wait_ge(squared, TT + 1)
            rms_rows(steps, v_ready, root, T[1], PER + 1, 2)
            for t in range(PER, TT):
                scale(t)
            dve.scalar_tensor_tensor(out=x1s[:], in0=x1s[:], scalar=T[1]["r"][0:NS, PER:PER + 1], in1=sc_s[:],
                                     op0=ALU.mult, op1=ALU.mult).then_inc(scaled, 1)


def program(nc, io):
    with ExitStack() as ctx:
        held = lambda c, n, shape, dt=F32: c.enter_context(nc.sbuf_tensor(n, shape, dt))
        ps = ctx.enter_context(nc.psum_tensor("ps", [P, 8, CH], F32))
        ident, mod_p = held(ctx, "ident", [P, P]), held(ctx, "mod_p", [P, 4, KT])
        feature_parts = lambda c, n: (held(c, f"{n}_hi", [P, KT, S], F32R), held(c, f"{n}_lo", [P, KT, S], F32R),
                                      held(c, f"{n}_s", [P, KT, P], F32R))
        row_parts = lambda c, n: (held(c, n, [P, TT, D]), held(c, f"{n}_s", [P, D]), held(c, f"{n}_ss", [P, 2, 16]))
        with ExitStack() as c:
            x, xs, ss = row_parts(c, "x")
            stage_modulation(nc, io, ps, ident, mod_p, x, xs[0:NS, :], ss)
            z_hi, z_lo, zs = feature_parts(c, "z")
            stage_norm(nc, io, ps, ident, mod_p, z_hi, z_lo, zs, "norm_a", SH_A, SC_A, 0, 1, x, xs[0:NS, :], ss)
            stage_projection(nc, "inp", ps, io["w_in"], IN_W, io["proj"], z_hi, z_lo, zs, x)
        with ExitStack() as c:
            mix_hi, mix_lo, mix_s = feature_parts(c, "mix")
            stage_prompt_attention(nc, io, ps, ident, mix_hi, mix_lo)
            stage_prompt_retention(nc, io, ps, ident, mix_hi, mix_lo)
            with ExitStack() as cc:
                q_blocks, kT_new = held(cc, "q_blocks", [P, DB, 4, NS]), held(cc, "kT_new", [P, 4, NS])
                stage_sample_heads(nc, io, ps, ident, mix_s, q_blocks, kT_new)
                stage_sample_attention(nc, io, ps, ident, mix_s, q_blocks, kT_new)
            x, xs, ss = row_parts(c, "res")
            stage_output(nc, io, ps, mix_hi, mix_lo, mix_s, x, xs[0:NS, :], ss)
            stage_norm(nc, io, ps, ident, mod_p, mix_hi, mix_lo, mix_s, "norm_f", SH_F, SC_F, 2, 3, x, xs[0:NS, :], ss)
            last_rows = [held(c, n, [P, D]) for n in ("gate_row", "scale_row", "shift_row")]
            stage_mlp(nc, io, ps, ident, mix_hi, mix_lo, mix_s, x, xs, last_rows)
            stage_last(nc, io, x, xs, last_rows)


_INS = ["x_prompt", "x_sample", "c_prompt", "c_sample", "cache_k", "cache_v", "state_ret",
        "w_ada", "b_ada", "w_in", "ret_gain", "w_out", "w_ff1", "w_ff2", "w_ada_f", "b_ada_f"]
_OUTS = [("y_prompt", (1, S, D)), ("y_sample", (DB, DS, D)),
         ("k_prompt", (1, 1, S, H, HD)), ("v_prompt", (1, 1, S, H, HD)), ("ret_prompt", (1, 1, RH, RD, RV)),
         ("k_sample", (1, DB, DS, H, HD)), ("v_sample", (1, DB, DS, H, HD)), ("ret_sample", (1, DB, RH, RD, RV))]


def build(nc, shapes):
    io = {n: nc.dram_tensor(f"in_{n}", s, F32, kind="ExternalInput").ap() for n, s in shapes.items()}
    for n, s in _OUTS:
        io[n] = nc.dram_tensor(f"out_{n}", s, F32, kind="ExternalOutput").ap()
    io["mod"] = nc.dram_tensor("mod", (9, MOD_W), F32).ap()
    io["proj"] = nc.dram_tensor("proj", (S + P, IN_W), F32).ap()
    io["x1"] = nc.dram_tensor("x1", (S + NS, D), F32).ap()
    program(nc, io)


def kernel(**inputs):
    import concourse.bacc as bacc
    from concourse.bass_utils import run_bass_kernel_spmd

    arrays = {n: np.ascontiguousarray(inputs[n]) for n in _INS}
    arrays.update(constants())
    nc = bacc.Bacc("TRN2", target_bir_lowering=False, num_devices=1)
    build(nc, {n: a.shape for n, a in arrays.items()})
    r = run_bass_kernel_spmd(nc, [{f"in_{n}": a for n, a in arrays.items()}], core_ids=[0])
    return tuple(r.results[0][f"out_{n}"] for n, _ in _OUTS)
```

```python
import math
from contextlib import ExitStack

import numpy as np
import concourse.bass as bass
from concourse import mybir

F32 = mybir.dt.float32
F32R = mybir.dt.float32r
ALU = mybir.AluOpType
ACT = mybir.ActivationFunctionType
ds = bass.ds

P = 128
D = 1024
KT = D // P
S = 1024
TT = S // P
DB, DS = 8, 8
NS = DB * DS
PAST = 4096
L = 2048
H, HD = 8, 64
AW = H * HD
RH, RD, RV = 4, 64, 128
IN_W = 3 * AW + 2 * RH * RD + 2 * RH * RV
CH = 512
FF = 4 * D
MOD_W = 8 * D
SH_A, SC_A, G_A, SH_F, SC_F, G_F, SH_L, SC_L = range(8)
FIRST_MODS = 2
COLUMNS_OF = {SH_A: 0, SC_A: 1, SH_F: 2, SC_F: 3}
NC = 1 + DB
LO_ROW = 32
AW_CH = 256
EPS = 1e-6
NEG = -1e30
BRANCHES = ((128, 1), (512, 4), (2048, 16))
SCALE = HD ** -0.5
OLD = 1536
KTILES = 10
NKEYS = KTILES * P + DS
GF = 256
NG = FF // GF



def log_count(dist):
    n = np.zeros(dist.shape)
    for window, dil in BRANCHES:
        n += (dist >= 0) & (dist <= window) & (dist % dil == 0)
    return np.where(n > 0, np.log(np.maximum(n, 1)), NEG).astype(np.float32)


def sample_positions():
    old = [16 * (16 * j + g) + r for j in range(6) for g in range(16) for r in range(8)]
    return np.array(old + list(range(OLD, L)) + list(range(L, L + DS)))


def angles(theta_powers, pos):
    inv = theta_powers.astype(np.float32)
    return (pos.astype(np.float32)[:, None] * inv[None, :]).astype(np.float32)


def constants():
    f = np.float32
    c = {"ident": np.eye(P, dtype=f)}
    p = np.arange(P)
    c["bias_p"] = log_count(p[:, None] - np.arange(S)[None, :] + (S - P))
    keys = sample_positions()
    t = np.tile(np.arange(DS), 2 * H)
    c["bias_s"] = log_count(L + t[:, None] - keys[None, :])
    pos_p = np.arange(S)
    pos_s = PAST + np.tile(np.arange(DS), DB)
    att = 500000.0 ** (-np.arange(0, 16, 2) / 16.0)
    ret = 10000.0 ** (-np.linspace(0.0, 1.0, RD // 2, dtype=f).astype(np.float64))

    def table(fn, powers, pos, heads):
        a = fn(angles(powers, pos).astype(np.float64)).astype(f)
        return np.tile(a, (1, heads))

    def by_tile(a):
        return np.ascontiguousarray(a.reshape(TT, P, -1).transpose(1, 0, 2).reshape(P, -1))

    c["rope_p"] = np.concatenate([np.tile(by_tile(table(g, att, pos_p, 2)), (1, 2)) for g in (np.cos, np.sin)], 1)
    c["rope_s"] = np.concatenate([table(g, att, pos_s, 2 * H) for g in (np.cos, np.sin)], 1)
    c["rot_p"] = np.concatenate([by_tile(table(g, ret, pos_p, 2)) for g in (np.cos, np.sin)], 1)
    c["rot_s"] = np.concatenate([table(g, ret, pos_s, 2 * RH) for g in (np.cos, np.sin)], 1)
    log_g = np.log1p(-np.exp2(-5.0 - np.arange(RH)))
    rel = p[None, :] - p[:, None]
    c["dmask_p"] = np.concatenate(
        [np.where(rel >= 0, np.exp(np.maximum(rel, 0) * g), 0.0) for g in log_g], 1).astype(f)
    c["dout_p"] = np.concatenate(
        [np.repeat(np.exp((p + 1.0)[None, :] * log_g[2 * a:2 * a + 2, None]), RD, 0) for a in range(2)], 1).astype(f)
    c["din_p"] = (np.exp((P - 1.0 - p)[:, None] * log_g[None, :]) * RD ** -0.5).astype(f)
    c["gchunk_p"] = np.stack([np.repeat(np.exp(P * log_g[2 * a:2 * a + 2]), RD) for a in range(2)], 1).astype(f)
    i = np.arange(NS)
    same = i[:, None] // DS == i[None, :] // DS
    rel = i[None, :] - i[:, None]
    c["dmask_s"] = np.concatenate(
        [np.where(same & (rel >= 0), np.exp(np.maximum(rel, 0) * g), 0.0) for g in log_g], 1).astype(f)
    b2 = np.repeat(np.arange(2), RD)
    c["dout_s"] = np.stack([np.stack([
        np.where((i[None, :] // DS) == 2 * bp + b2[:, None], np.exp((i % DS + 1.0) * g)[None, :], 0.0)
        for bp in range(4)], 1) for g in log_g], 1).reshape(P, -1).astype(f)
    c["din_s"] = np.stack([np.stack([
        np.where((i[:, None] // DS) == 2 * bp + b2[None, :],
                 (np.exp((DS - 1.0 - i % DS) * g) * RD ** -0.5)[:, None], 0.0)
        for bp in range(4)], 1) for g in log_g], 1).reshape(NS, -1).astype(f)
    return c


GCHUNK_S = [float(np.float32(math.exp(DS * math.log1p(-2.0 ** (-5 - h))))) for h in range(RH)]


class Steps:

    def __init__(self, eng, sem):
        self.eng, self.sem, self.n, self.base = eng, sem, 0, 0

    def done(self, ins):
        ins.then_inc(self.sem, 1)
        self.n += 1
        return self.n

    def then(self, ins):
        self.done(ins)
        self.eng.wait_ge(self.sem, self.base + self.n)

    def wait(self):
        self.eng.wait_ge(self.sem, self.base + self.n)


class Stage:

    used = []

    def __init__(self, nc, name, clear=False):
        self.nc, self.name, self.ctx = nc, name, ExitStack()
        if clear:
            self.ctx.callback(self.clear)

    def sb(self, name, shape, dt=F32):
        return self.ctx.enter_context(self.nc.sbuf_tensor(f"{self.name}_{name}", shape, dt))

    def sem(self, name):
        self.used.append(self.nc.alloc_semaphore(f"{self.name}_{name}"))
        return self.used[-1]

    def clear(self):
        self.nc.clear_and_free_semaphores(self.used)
        self.nc.all_engine_barrier()
        self.used.clear()

    def block(self):
        return self.ctx.enter_context(self.nc.Block())



def stage_modulation(nc, io, ps, ident, mod_p, x, xs, ss, c_parts):
    st = Stage(nc, "mod")
    CHUNKS = FIRST_MODS * D // CH
    with st.ctx:
        crow, ex, srow = (st.sb(n, [NC, D]) for n in ("crow", "ex", "srow"))
        cT = st.sb("cT", [P, KT, NC])
        mrow = st.sb("mrow", [NC, FIRST_MODS * D])
        sq = [st.sb(f"sq{s}", [P, D]) for s in range(2)]
        w = [st.sb(f"w{s}", [P, KT, CH]) for s in range(CHUNKS)]
        c_in, b_in, exp_done, dve, turned, squared, made, stored, mod_done, mod_turned = (st.sem(n) for n in (
            "c_in", "b_in", "exp_done", "dve", "turned", "squared", "made", "stored", "mod_done", "mod_turned"))
        w_in = [st.sem(f"w_in{s}") for s in range(CHUNKS)]
        x_in = [st.sem(f"x_in{t}") for t in range(TT + 1)]
        wv = io["w_ada"].rearrange("o (k p) n -> p (o k) n", p=P)
        block = st.block()

        @block.sync
        def _(sp):
            sp.dma_start(crow[0:1, :], io["c_prompt"]).then_inc(c_in, 16)
            sp.dma_start(crow[1:NC, :], io["c_sample"]).then_inc(c_in, 16)
            sp.dma_start(ident[:], io["ident"]).then_inc(c_in, 16)
            sp.dma_start(mrow[:], io["b_ada"][0, 0:FIRST_MODS * D].partition_broadcast(NC)).then_inc(b_in, 16)
            for s in range(CHUNKS):
                sp.dma_start(w[s][:], wv[:, :, s * CH:(s + 1) * CH]).then_inc(w_in[s], 16)
            for t in range(TT):
                sp.dma_start(x[:, t, :], io["x_prompt"][0, t * P:(t + 1) * P, :]).then_inc(x_in[t], 16)
            sp.dma_start(xs[:], io["x_sample"].rearrange("b t d -> (b t) d")).then_inc(x_in[TT], 16)
            sp.wait_ge(mod_done, CHUNKS)
            sp.dma_start(io["mod"][:, 0:FIRST_MODS * D], mrow[:]).then_inc(stored, 16)
            sp.wait_ge(stored, 16)

        @block.scalar
        def _(act):
            act.wait_ge(c_in, 48)
            act.activation(ex[:], crow[:], ACT.Exp, scale=-1.0).then_inc(exp_done, 1)

        @block.tensor
        def _(pe):
            pe.wait_ge(dve, 4)
            for k in range(KT):
                last = pe.transpose(ps[:, 7, k * 10:k * 10 + NC], srow[:, k * P:(k + 1) * P], ident[0:NC, 0:NC])
            last.then_inc(turned, 1)
            pe.wait_ge(dve, 5)
            for s in range(CHUNKS):
                pe.wait_ge(w_in[s], 16)
                for k in range(KT):
                    mm = pe.matmul(ps[0:NC, s, :], cT[:, k, :], w[s][:, k, :], start=(k == 0), stop=(k == KT - 1))
                mm.then_inc(made, 1)
            pe.wait_ge(mod_done, CHUNKS)
            for k in range(FIRST_MODS * KT):
                mm = pe.transpose(ps[:, 6, k * 10:k * 10 + NC], mrow[:, k * P:(k + 1) * P], ident[0:NC, 0:NC])
            mm.then_inc(mod_turned, 1)

        @block.vector
        def _(dve_):
            steps = Steps(dve_, dve)
            steps.then(dve_.memset(c_parts[:].bitcast(F32), 0.0))
            dve_.wait_ge(exp_done, 1)
            steps.then(dve_.tensor_scalar(ex[:], ex[:], 1.0, None, ALU.add))
            steps.then(dve_.reciprocal(ex[:], ex[:]))
            steps.done(dve_.tensor_tensor(srow[:], crow[:], ex[:], ALU.mult))
            assert steps.n == 4
            dve_.wait_ge(turned, 1)
            cols = ps[:, 7, 0:10 * KT].rearrange("p (k c) -> p k c", c=10)[:, :, 0:NC]
            steps.done(dve_.tensor_copy(cT[:], cols))
            steps.then(dve_.tensor_copy(c_parts[:, :, 0:NC], cols))
            steps.done(dve_.tensor_tensor(c_parts[:, :, LO_ROW:LO_ROW + NC], cols, c_parts[:, :, 0:NC].bitcast(F32), ALU.subtract))

            dve_.memset(ss[:], 0.0).then_inc(squared, 1)
            dve_.wait_ge(squared, 1)

            def squares(t):
                dve_.wait_ge(x_in[t], 16)
                if t >= 2:
                    dve_.wait_ge(squared, t)
                dve_.tensor_tensor_reduce(sq[t % 2][:], x[:, t, :], x[:, t, :], 1.0, 0.0, ALU.mult, ALU.add,
                                          ss[:, 0, t:t + 1]).then_inc(squared, 1)

            dve_.wait_ge(b_in, 16)
            for s in range(CHUNKS):
                dve_.wait_ge(made, s + 1)
                dve_.tensor_tensor(mrow[:, s * CH:(s + 1) * CH], ps[0:NC, s, :], mrow[:, s * CH:(s + 1) * CH],
                                   ALU.add).then_inc(mod_done, 1)
                squares(s)
            for t in range(CHUNKS, TT):
                squares(t)
            dve_.wait_ge(mod_turned, 1)
            steps.done(dve_.tensor_copy(mod_p[:, 0:FIRST_MODS, :],
                                        ps[:, 6, 0:10 * FIRST_MODS * KT].rearrange("p (m k c) -> p m k c", k=KT, c=10)[:, :, :, 0]))
            dve_.wait_ge(x_in[TT], 16)
            dve_.wait_ge(squared, TT)
            dve_.tensor_tensor_reduce(sq[0][0:NS, :], xs[:], xs[:], 1.0, 0.0, ALU.mult, ALU.add,
                                      ss[0:NS, 0, TT:TT + 1]).then_inc(squared, 1)


def load_columns(eng, io, mod_p, vectors, sem):
    for m in vectors:
        eng.dma_start(mod_p[:, COLUMNS_OF[m], :], io["mod"][0, m * D:(m + 1) * D].rearrange("(k p) -> p k", p=P),
                      allow_slow_non_contiguous=True).then_inc(sem, 16)



def load_rows(eng, io, prompt, sample, m, sem):
    if prompt is not None:
        eng.dma_start(prompt[:], io["mod"][0, m * D:(m + 1) * D].partition_broadcast(P)).then_inc(sem, 16)
    if sample is not None:
        for b in range(DB):
            eng.dma_start(sample[b * DS:(b + 1) * DS],
                          io["mod"][1 + b, m * D:(m + 1) * D].partition_broadcast(DS)).then_inc(sem, 16)


def rms_rows(steps, act_ready, root_ready, T, n, nth=1):
    dve, ss, v, r, t = steps.eng, T["ss"], T["v"], T["r"], T["t"]
    steps.wait()
    steps.then(dve.tensor_scalar(v[:, 0:n], ss[:, 0:n], 1.0 / D, EPS, ALU.mult, ALU.add))
    dve.sem_inc(act_ready, 1)
    dve.wait_ge(root_ready, nth)
    steps.then(dve.reciprocal(r[:, 0:n], t[:, 0:n]))
    steps.then(dve.tensor_tensor(ss[:, 0:n], r[:, 0:n], r[:, 0:n], ALU.mult))
    steps.then(dve.tensor_tensor(ss[:, 0:n], ss[:, 0:n], v[:, 0:n], ALU.mult))
    steps.then(dve.tensor_scalar(ss[:, 0:n], ss[:, 0:n], -0.5, 1.5, ALU.mult, ALU.add))
    steps.then(dve.tensor_tensor(r[:, 0:n], r[:, 0:n], ss[:, 0:n], ALU.mult))


def norm_part(st, block, io, ps, ident, mod_p, z_hi, z_lo, zs, sh, sc, jsh, jsc, x, xs, ss, scs, shs, zf,
              sp_extra=None, act_extra=None, pool_extra=None):
    T = {n: st.sb(f"norm_{n}", [P, 16]) for n in ("v", "r", "t", "ss")}
    s_in, dve, v_ready, root = (st.sem(n) for n in ("s_in", "dve", "v_ready", "root"))
    r_ready, xn_dve, xn_act, xs_ready, turned, zf_ready, hi_ready, lo_dve, lo_pool = (
        st.sem(n) for n in ("r_ready", "xn_dve", "xn_act", "xs_ready", "turned", "zf_ready", "hi_ready", "lo_dve", "lo_pool"))
    zs_turned, zs_hi = st.sem("zs_turned"), st.sem("zs_hi")
    units = [(h, k) for h in range(2) for k in range(KT)]

    @block.sync
    def _(sp):
        if sp_extra:
            sp_extra(sp)
        for dst, m in ((scs, sc), (shs, sh)):
            load_rows(sp, io, None, dst, m, s_in)

    def low_part(eng, u, done):
        h, k = units[u]
        cols = slice(h * CH, (h + 1) * CH)
        eng.wait_ge(hi_ready, u + 1)
        eng.tensor_tensor(z_lo[:, k, cols], zf[u % 4], z_hi[:, k, cols].bitcast(F32), ALU.subtract).then_inc(done, 1)

    @block.scalar
    def _(act):
        act.wait_ge(v_ready, 1)
        act.activation(T["t"][:, 0:9], T["v"][:, 0:9], ACT.Sqrt).then_inc(root, 1)
        act.wait_ge(r_ready, 1)
        for t in range(1, TT, 2):
            act.mul(x[:, t, :], x[:, t, :], T["r"][:, t:t + 1]).then_inc(xn_act, 1)
        if act_extra:
            act_extra(act)
        for u, (h, k) in enumerate(units):
            act.wait_ge(zf_ready, u + 1)
            act.copy(z_hi[:, k, h * CH:(h + 1) * CH], zf[u % 4]).then_inc(hi_ready, 1)
        act.wait_ge(zs_turned, 1)
        act.copy(zs[:, :, 0:NS], ps[:, 7, :].rearrange("p (k n) -> p k n", n=NS)).then_inc(zs_hi, 1)

    @block.gpsimd
    def _(pool):
        if pool_extra:
            pool_extra(pool)
        for u in range(1, len(units), 2):
            low_part(pool, u, lo_pool)

    @block.vector
    def _(dve_):
        steps = Steps(dve_, dve)
        steps.done(dve_.tensor_scalar(mod_p[:, jsc, :], mod_p[:, jsc, :], 1.0, None, ALU.add))
        steps.then(dve_.tensor_tensor(T["ss"][:, 0:9], ss[:, 0, 0:9], ss[:, 1, 0:9], ALU.add))
        rms_rows(steps, v_ready, root, T, 9)
        dve_.sem_inc(r_ready, 1)
        for t in range(0, TT, 2):
            dve_.tensor_scalar(x[:, t, :], x[:, t, :], T["r"][:, t:t + 1], None, ALU.mult).then_inc(xn_dve, 1)

        def sample():
            dve_.wait_ge(s_in, 16 * 16)
            steps.then(dve_.tensor_scalar(scs, scs, 1.0, None, ALU.add))
            steps.then(dve_.scalar_tensor_tensor(out=xs[:], in0=xs[:], scalar=T["r"][0:NS, 8:9], in1=scs,
                                                 op0=ALU.mult, op1=ALU.mult))
            dve_.tensor_tensor(xs[:], xs[:], shs, ALU.add).then_inc(xs_ready, 1)

        for u, (h, k) in enumerate(units):
            dve_.wait_ge(turned, u + 1)
            if u >= 4 and u % 2:
                dve_.wait_ge(lo_pool, u // 2 - 1)
            elif u >= 4:
                dve_.wait_ge(lo_dve, u // 2 - 1)
            dve_.tensor_scalar(zf[u % 4], ps[:, u % 6, :], mod_p[:, jsc, k:k + 1], mod_p[:, jsh, k:k + 1],
                               ALU.mult, ALU.add).then_inc(zf_ready, 1)
            if u == KT:
                sample()
            if u % 2:
                low_part(dve_, u - 1, lo_dve)
        dve_.wait_ge(zs_hi, 1)
        dve_.tensor_tensor(zs[:, :, NS:P], ps[:, 7, :].rearrange("p (k n) -> p k n", n=NS),
                           zs[:, :, 0:NS].bitcast(F32), ALU.subtract).then_inc(zf_ready, 1)

    @block.tensor
    def _(pe):
        for u, (h, k) in enumerate(units):
            pe.wait_ge(xn_dve, 2 * (h + 1))
            pe.wait_ge(xn_act, 2 * (h + 1))
            if u >= 6:
                pe.wait_ge(zf_ready, u - 5)
            for j in range(4):
                mm = pe.transpose(ps[:, u % 6, j * P:(j + 1) * P], x[:, 4 * h + j, k * P:(k + 1) * P], ident[:])
            mm.then_inc(turned, 1)
        pe.wait_ge(xs_ready, 1)
        for k in range(KT):
            mm = pe.transpose(ps[:, 7, k * NS:(k + 1) * NS], xs[:, k * P:(k + 1) * P], ident[0:NS, 0:NS])
        mm.then_inc(zs_turned, 1)
    n = len(units)
    return ([(hi_ready, n), (lo_dve, n // 2), (lo_pool, n // 2), (zs_hi, 1), (zf_ready, n + 1)],
            [(hi_ready, n // 2), (lo_dve, n // 4), (lo_pool, n // 4), (zf_ready, n - 3)],
            [(turned, n // 2)], [(turned, n), (zs_turned, 1)])


def wait_all(eng, waits):
    for sem, count in waits:
        eng.wait_ge(sem, count)



def stage_projection(nc, io, ps, ident, mod_p, z_hi, z_lo, zs, x, xs_room, ss, c_parts):
    st = Stage(nc, "inp")
    w_dram, out = io["w_in"], io["proj"]
    NCH = IN_W // CH
    OUTS = TT + 1
    BANKS, ROWS = 6, 2
    QUARTERS = 4
    quarter = lambda q: slice(q * KT // QUARTERS, (q + 1) * KT // QUARTERS)
    ADA = (6 - FIRST_MODS) * D // AW_CH
    PIECES = ADA + 2 * D // AW_CH
    PER = PIECES // NCH
    assert PIECES == NCH * PER and 2 * PER == TT
    with st.ctx:
        raw = [x[:, s * TT // 2:(s + 1) * TT // 2, :].rearrange("p t (a c) -> p (t a) c", c=CH) for s in range(2)]
        w_hi = [st.sb(f"whi{s}", [P, KT, CH], F32R) for s in range(2)]
        w_lo = [st.sb(f"wlo{s}", [P, KT, CH], F32R) for s in range(2)]
        row = [st.sb(f"row{s}", [P, CH]) for s in range(ROWS)]
        room = st.sb("room", [P, 2 * KT * AW_CH])
        a_hi, a_lo = (st.sb(n, [P, KT, AW_CH], F32R) for n in ("a_hi", "a_lo"))
        a_raw = [room[:, s * KT * AW_CH:(s + 1) * KT * AW_CH].rearrange("p (k c) -> p k c", k=KT) for s in range(2)]
        a_row = [xs_room[0:NC, s * AW_CH:(s + 1) * AW_CH] for s in range(2)]
        a_low = [xs_room[0:NC, (2 + s) * AW_CH:(3 + s) * AW_CH] for s in range(2)]
        raw_in = [[st.sem(f"raw_in{s}_{q}") for q in range(QUARTERS)] for s in range(2)]
        raw_free, w_free, w_hi_done, made, bank_free, a_hi_done, a_ready, a_made, a_low_done, added, a_sum = (
            st.sem(n) for n in ("raw_free", "w_free", "w_hi_done", "made", "bank_free", "a_hi_done", "a_ready", "a_made",
                                "a_low_done", "added", "a_sum"))
        row_free = [st.sem(f"row_free{s}") for s in range(ROWS)]
        a_in, stored = ([st.sem(f"{n}{s}") for s in range(2)] for n in ("a_in", "stored"))
        wv = w_dram.rearrange("o (k p) n -> p (o k) n", p=P)
        ada = io["w_ada"].rearrange("o (k p) n -> p (o k) n", p=P)
        ada_f = io["w_ada_f"].rearrange("(k p) n -> p k n", p=P)
        xs = xs_room[0:NS, :]
        scs, shs = room[0:NS, 0:D], room[0:NS, D:2 * D]
        zf = [room[:, 2 * D + u * CH:2 * D + (u + 1) * CH] for u in range(4)]
        block = st.block()
        z_ready, _, half_read, x_read = norm_part(st, block, io, ps, ident, mod_p, z_hi, z_lo, zs, SH_A, SC_A, 0, 1, x, xs, ss,
                                                  scs, shs, zf)

        def load_weights(eng, i, s):
            eng.wait_ge(raw_free, QUARTERS * (2 * i + s) + QUARTERS)
            for q in range(QUARTERS):
                eng.dma_start(raw[s][:, quarter(q), :],
                              wv[:, quarter(q), ds(i * 2 * CH + s * CH, CH)]).then_inc(raw_in[s][q], 16)

        @block.sync
        def _(sp):
            def load(s, w, b, col):
                sp.dma_start(a_raw[s], w[:, :, ds(col, AW_CH)]).then_inc(a_in[s], 16)
                sp.dma_start(a_row[s], b[ds(col, AW_CH)].partition_broadcast(NC)).then_inc(a_in[s], 16)

            def store(t, s, col):
                sp.wait_ge(a_sum, t + 1)
                sp.dma_start(io["mod"][:, ds(col, AW_CH)], a_row[s]).then_inc(stored[s], 16)

            first, last = FIRST_MODS * D, 6 * D
            sp.sem_inc(raw_free, 2 * QUARTERS)
            wait_all(sp, half_read)
            load_weights(sp, 0, 0)
            wait_all(sp, x_read)
            load_weights(sp, 0, 1)
            wait_all(sp, z_ready)
            load(0, ada_f, io["b_ada_f"], 0)
            load(1, ada_f, io["b_ada_f"], AW_CH)
            for t in range(2):
                store(t, t, last + t * AW_CH)
                sp.wait_ge(stored[t], 16)
                load(t, ada, io["b_ada"][0], first + t * AW_CH)
            with sp.Fori(1, ADA // 2) as i:
                for s in range(2):
                    to, fro = sp.snap(i * 2 * AW_CH + (first + (s - 2) * AW_CH)), sp.snap(i * 2 * AW_CH + (first + s * AW_CH))
                    store(2 * i + s, s, to)
                    sp.wait_ge(stored[s], 16 * i + 16)
                    load(s, ada, io["b_ada"][0], fro)
            for t in range(ADA, PIECES):
                s = t % 2
                store(t, s, first + (t - 2) * AW_CH if t < ADA + 2 else last + (t - ADA) * AW_CH)
                sp.wait_ge(stored[s], 16 * (t // 2) + 16)
                if t + 2 < PIECES:
                    load(s, ada_f, io["b_ada_f"], (t + 2 - ADA) * AW_CH)

        @block.vector
        def _(dve):
            def split(i, s):
                dve.wait_ge(w_free, 2 * i + s + 1)
                for q in range(QUARTERS):
                    k = quarter(q)
                    dve.wait_ge(raw_in[s][q], 16 * i + 16)
                    dve.tensor_copy(w_hi[s][:, k, :], raw[s][:, k, :]).then_inc(w_hi_done, 1)
                    dve.wait_ge(w_hi_done, QUARTERS * (2 * i + s) + q + 1)
                    dve.tensor_tensor(w_lo[s][:, k, :], raw[s][:, k, :], w_hi[s][:, k, :].bitcast(F32),
                                      ALU.subtract).then_inc(raw_free, 1)

            def pieces(i, s):
                for j in range(PER):
                    t = PER * (2 * i + s) + j
                    dve.wait_ge(a_low_done, t + 1)
                    dve.tensor_tensor(a_row[j % 2], ps[0:NC, 6 + j % 2, 0:AW_CH], a_row[j % 2], ALU.add).then_inc(added, 1)
                    dve.wait_ge(added, t + 3)
                    dve.tensor_tensor(a_row[j % 2], a_row[j % 2], a_low[j % 2], ALU.add).then_inc(a_sum, 1)

            dve.sem_inc(added, 2)
            split(0, 0)
            with dve.Fori(0, NCH // 2 - 1) as i:
                split(i, 1)
                pieces(i, 0)
                split(i + 1, 0)
                pieces(i, 1)
            split(NCH // 2 - 1, 1)
            pieces(NCH // 2 - 1, 0)
            pieces(NCH // 2 - 1, 1)

        @block.gpsimd
        def _(pool):
            with pool.Fori(0, PIECES // 2) as i:
                for s in range(2):
                    pool.wait_ge(a_hi_done, 2 * i + s + 1)
                    pool.tensor_tensor(a_lo[:], a_raw[s], a_hi[:].bitcast(F32), ALU.subtract).then_inc(a_ready, 1)

        @block.tensor
        def _(pe):
            pe.sem_inc(w_free, 2)
            wait_all(pe, z_ready)
            with pe.Fori(0, NCH // 2) as i:
                for s in range(2):
                    for o in range(OUTS):
                        n = s * OUTS + o
                        bank = ps[:, n % BANKS, :]
                        pe.wait_ge(bank_free, i * 2 * OUTS + n + 1)
                        if o < TT:
                            parts = ((z_hi, w_hi), (z_hi, w_lo), (z_lo, w_hi))
                            cols = slice(o * P, (o + 1) * P)
                        else:
                            parts = ((zs, w_hi), (zs, w_lo))
                            cols = slice(0, P)
                        for k in range(KT):
                            if o == 0 and k % (KT // QUARTERS) == 0:
                                pe.wait_ge(raw_free, QUARTERS * (2 * i + s) + 2 * QUARTERS + k // (KT // QUARTERS) + 1)
                            for a, (z, w) in enumerate(parts):
                                mm = pe.matmul(bank, z[:, k, cols], w[s][:, k, :], start=(k == 0 and a == 0),
                                               stop=(k == KT - 1 and a == len(parts) - 1))
                        mm.then_inc(made, 1)
                        if o % 2 and o < TT:
                            j = o // 2
                            t = PER * (2 * i + s) + j
                            pe.wait_ge(a_ready, t + 1)
                            pe.wait_ge(added, t + 1)
                            for k in range(KT):
                                for a, w in enumerate((a_hi, a_lo)):
                                    mm = pe.matmul(ps[0:NS, 6 + j % 2, 0:AW_CH], c_parts[:, k, :], w[:, k, :],
                                                   start=(k == 0 and a == 0), stop=(k == KT - 1 and a == 1))
                            mm.then_inc(a_made, 1)
                    pe.wait_ge(made, i * 2 * OUTS + (s + 1) * OUTS)
                    pe.sem_inc(w_free, 1)

        @block.scalar
        def _(act):
            def high_piece(t, s, turn):
                act.wait_ge(a_in[s], 32 * turn + 32)
                act.copy(a_hi[:], a_raw[s]).then_inc(a_hi_done, 1)

            def chunk(i, s, more_weights=True, last=False):
                if more_weights:
                    load_weights(act, i + 1, s)
                for o in range(OUTS):
                    n = s * OUTS + o
                    act.wait_ge(made, i * 2 * OUTS + n + 1)
                    act.wait_ge(row_free[n % ROWS], i * (16 * 2 * OUTS // ROWS) + 16 * (n // ROWS) + 16)
                    act.copy(row[n % ROWS][:], ps[:, n % BANKS, :]).then_inc(bank_free, 1)
                    act.wait_ge(bank_free, i * 2 * OUTS + n + BANKS + 1)
                    act.dma_start(out[o * P:(o + 1) * P, ds(i * 2 * CH + s * CH, CH)],
                                  row[n % ROWS][:]).then_inc(row_free[n % ROWS], 16)
                    if o % 2 and o < TT:
                        j = o // 2
                        t = PER * (2 * i + s) + j
                        act.wait_ge(a_made, t + 1)
                        act.copy(a_low[j % 2], ps[LO_ROW:LO_ROW + NC, 6 + j % 2, 0:AW_CH]).then_inc(a_low_done, 1)
                        if not (last and j == PER - 1):
                            high_piece(t + 1, (j + 1) % 2, PER * i + (PER * s + j + 1) // 2)

            wait_all(act, z_ready)
            act.sem_inc(bank_free, BANKS)
            for r in range(ROWS):
                act.sem_inc(row_free[r], 16)
            high_piece(0, 0, 0)
            with act.Fori(0, NCH // 2 - 1) as i:
                for s in range(2):
                    chunk(i, s)
            chunk(NCH // 2 - 1, 0, more_weights=False)
            chunk(NCH // 2 - 1, 1, more_weights=False, last=True)
            for r in range(ROWS):
                act.wait_ge(row_free[r], 16 * (NCH * OUTS // ROWS) + 16)



def banks(ps, first, n):
    return ps[:, first:first + n, :].rearrange("p b c -> p (b c)")


def stage_prompt_attention(nc, io, ps, ident, mix_hi, mix_lo):
    st = Stage(nc, "att", clear=True)
    UNITS = 2 * TT
    HALF = HD // 8
    with st.ctx:
        bias = st.sb("bias", [P, S])
        rope = st.sb("rope", [P, 2, 2 * TT, 2, HALF])
        qk = [st.sb(f"qk{s}", [P, 2 * TT, P]) for s in range(2)]
        v = [st.sb(f"v{s}", [P, TT, P]) for s in range(2)]
        tmp = [st.sb(f"tmp{s}", [P, 2 * TT, 2, HALF]) for s in range(4)]
        q_hi = [st.sb(f"qhi{h}", [P, S], F32R) for h in range(2)]
        q_lo = [st.sb(f"qlo{h}", [P, S], F32R) for h in range(2)]
        k_hi, k_lo = st.sb("khi", [P, S], F32R), st.sb("klo", [P, S], F32R)
        prob = [st.sb(f"prob{s}", [P, S]) for s in range(3)]
        probT = [st.sb(f"probT{s}", [P, S]) for s in range(2)]
        top, neg, total, inv = (st.sb(n, [P, UNITS]) for n in ("top", "neg", "total", "inv"))
        waited = st.sb("waited", [P, 1])
        rope_in, bias_in, zeroed, roped, heads_free, turned, hi_done, split_done = (st.sem(n) for n in (
            "rope_in", "bias_in", "zeroed", "roped", "heads_free", "turned", "hi_done", "split_done"))
        made, scored, neg_done, exp_done, inv_done, prob_done, prob_turned, probT_done, pv_done, mix_hi_done = (
            st.sem(n) for n in ("made", "scored", "neg_done", "exp_done", "inv_done", "prob_done",
                                "prob_turned", "probT_done", "pv_done", "mix_hi_done"))
        mix_done = st.sem("mix_done")
        qkv_in = [st.sem(f"qkv_in{s}") for s in range(2)]
        kv_put = [st.sem(f"kv_put{s}") for s in range(2)]

        def unit(u):
            h, q = divmod(u, TT)
            return h, (TT - 1 - q if h else q)

        proj = io["proj"][0:S, :].rearrange("(t p) c -> p t c", p=P)
        k_out = io["k_prompt"].rearrange("o b (t p) h d -> p (o b t) (h d)", p=P)
        v_out = io["v_prompt"].rearrange("o b (t p) h d -> p (o b t) (h d)", p=P)
        block = st.block()

        @block.sync
        def _(sp):
            for s in range(2):
                sp.sem_inc(kv_put[s], 32)
            sp.dma_start(rope[:].rearrange("p a b c d -> p (a b c d)"), io["rope_p"]).then_inc(rope_in, 16)
            with sp.Fori(0, 2) as i:
                for s in range(2):
                    cols = [sp.snap(i * 2 * P + s * P + j * AW) for j in range(3)]
                    sp.wait_ge(heads_free, 2 * i + s + 1)
                    sp.wait_ge(kv_put[s], 32 * i + 32)
                    for j, dst in ((0, qk[s][:, 0:TT, :]), (1, qk[s][:, TT:, :]), (2, v[s][:])):
                        sp.dma_start(dst, proj[:, :, ds(cols[j], P)]).then_inc(qkv_in[s], 16)
                    sp.wait_ge(roped, 6 * (2 * i + s) + 6)
                    sp.dma_start(k_out[:, :, ds(cols[0], P)], qk[s][:, TT:, :]).then_inc(kv_put[s], 16)
                    sp.dma_start(v_out[:, :, ds(cols[0], P)], v[s][:]).then_inc(kv_put[s], 16)
            for s in range(2):
                sp.wait_ge(kv_put[s], 96)

        @block.gpsimd
        def _(pool):
            pool.wait_ge(rope_in, 16)
            with pool.Fori(0, 2) as i:
                for s in range(2):
                    n = 6 * (2 * i + s)
                    pool.wait_ge(qkv_in[s], 48 * i + 48)
                    x = qk[s][:].rearrange("p t (h d) -> p t h d", h=2)
                    a, b = x[:, :, :, 0:HALF], x[:, :, :, HALF:2 * HALF]
                    for dst, u, w in ((0, a, 0), (1, b, 1), (2, b, 0), (3, a, 1)):
                        pool.tensor_tensor(tmp[dst][:], u, rope[:, w], ALU.mult).then_inc(roped, 1)
                    pool.wait_ge(roped, n + 4)
                    pool.tensor_tensor(a, tmp[0][:], tmp[1][:], ALU.subtract).then_inc(roped, 1)
                    pool.tensor_tensor(b, tmp[2][:], tmp[3][:], ALU.add).then_inc(roped, 1)
                    pool.wait_ge(roped, n + 6)

        @block.tensor
        def _(pe):
            pe.sem_inc(heads_free, 2)
            pe.sem_inc(prob_turned, 3)
            pe.sem_inc(pv_done, 2)
            with pe.Fori(0, 2) as i:
                for s in range(2):
                    base = i * 2 * UNITS + s * UNITS

                    def scores(u):
                        h, q = unit(u)
                        if u >= 2:
                            pe.wait_ge(scored, base + u - 1)
                        width = (q + 1) * P
                        for c in range(0, width, CH):
                            e = min(width, c + CH)
                            out = banks(ps, 2 * (u % 2), 2)[:, c:e]
                            for a, (x, y) in enumerate(((q_hi, k_hi), (q_hi, k_lo), (q_lo, k_hi))):
                                mm = pe.matmul(out, x[h][:, q * P:(q + 1) * P], y[:, c:e], start=(a == 0), stop=(a == 2))
                        mm.then_inc(made, 1)

                    def turn(u):
                        pe.wait_ge(prob_done, base + u + 1)
                        for k in range(unit(u)[1] + 1):
                            mm = pe.transpose(banks(ps, 4, 2)[:, k * P:(k + 1) * P], prob[u % 3][:, k * P:(k + 1) * P], ident[:])
                        mm.then_inc(prob_turned, 1)

                    def values(u):
                        h, q = unit(u)
                        for k in range(q + 1):
                            mm = pe.matmul(banks(ps, 6, 2)[HD * h:HD * (h + 1), q * P:(q + 1) * P],
                                           v[s][:, k, HD * h:HD * (h + 1)], probT[u % 2][:, k * P:(k + 1) * P],
                                           start=(k == 0), stop=(k == q))
                        mm.then_inc(pv_done, 1)

                    def turn_heads(s, part):
                        pe.wait_ge(roped, 6 * (2 * i + s) + 6)
                        for t in range(TT):
                            mm = pe.transpose(banks(ps, 2 * part, 2)[:, t * P:(t + 1) * P], qk[s][:, part * TT + t, :], ident[:])
                        mm.then_inc(turned, 1)

                    if s == 0:
                        turn_heads(0, 0)
                        turn_heads(0, 1)
                    pe.wait_ge(split_done, 3 * (2 * i + s) + 3)
                    scores(0)
                    scores(1)
                    scores(2)
                    turn(0)
                    for u in range(UNITS):
                        if u + 3 < UNITS:
                            scores(u + 3)
                        elif s == 0 and u < UNITS - 1:
                            part = u - (UNITS - 3)
                            pe.wait_ge(scored, base + UNITS - 1 + part)
                            turn_heads(1, part)
                        pe.wait_ge(probT_done, base + u + 1)
                        if u + 1 < UNITS:
                            turn(u + 1)
                        values(u)
                    pe.wait_ge(pv_done, base + UNITS + 2)
                    pe.sem_inc(heads_free, 1)

        @block.scalar
        def _(act):
            act.dma_start(bias[:], io["bias_p"]).then_inc(bias_in, 16)
            act.wait_ge(zeroed, 4)
            with act.Fori(0, 2) as i:
                for s in range(2):
                    base = i * 2 * UNITS + s * UNITS

                    def exponent(u):
                        act.wait_ge(neg_done, base + u + 1)
                        x = prob[u % 3][:, 0:(unit(u)[1] + 1) * P]
                        act.activation(x, x, ACT.Exp, bias=neg[:, u:u + 1], accum_out=total[:, u:u + 1]).then_inc(exp_done, 1)

                    def take_queries(s):
                        act.wait_ge(turned, 2 * (2 * i + s) + 1)
                        for h in range(2):
                            rows = slice(HD * h, HD * (h + 1))
                            act.mul(q_hi[h][rows, :], banks(ps, 0, 2)[rows, :], SCALE).then_inc(hi_done, 1)

                    def take_keys(s):
                        act.wait_ge(turned, 2 * (2 * i + s) + 2)
                        act.copy(k_hi[:], banks(ps, 2, 2)).then_inc(hi_done, 1)

                    if s == 0:
                        take_queries(0)
                        take_keys(0)
                    exponent(0)
                    for u in range(UNITS):
                        if u + 1 < UNITS:
                            exponent(u + 1)
                        act.wait_ge(prob_turned, base + u + 4)
                        act.wait_ge(pv_done, base + u + 1)
                        w = (unit(u)[1] + 1) * P
                        act.copy(probT[u % 2][:, 0:w], banks(ps, 4, 2)[:, 0:w]).then_inc(probT_done, 1)
                        if s == 0 and u == UNITS - 2:
                            take_queries(1)
                        if s == 0 and u == UNITS - 1:
                            take_keys(1)
                    act.wait_ge(pv_done, base + UNITS + 2)
                    act.copy(mix_hi[:, ds(2 * i + s, 1), :], banks(ps, 6, 2)).then_inc(mix_hi_done, 1)

        @block.vector
        def _(dve):
            for x in (q_hi, q_lo):
                for h in range(2):
                    rows = slice(HD * (1 - h), HD * (2 - h))
                    dve.memset(x[h][rows, :].bitcast(F32), 0.0).then_inc(zeroed, 1)
            dve.wait_ge(zeroed, 4)
            dve.wait_ge(bias_in, 16)
            with dve.Fori(0, 2) as i:
                for s in range(2):
                    base = i * 2 * UNITS + s * UNITS

                    def score(u):
                        w = (unit(u)[1] + 1) * P
                        dve.wait_ge(made, base + u + 1)
                        dve.wait_ge(prob_turned, base + u + 1)
                        dve.memset(waited[:], 0.0)
                        dve.tensor_tensor_reduce(prob[u % 3][:, 0:w], banks(ps, 2 * (u % 2), 2)[:, 0:w],
                                                 bias[:, S - w:S], 1.0, NEG, ALU.add, ALU.max,
                                                 top[:, u:u + 1]).then_inc(scored, 1)
                        dve.wait_ge(scored, base + u + 1)
                        dve.tensor_scalar(neg[:, u:u + 1], top[:, u:u + 1], -1.0, None, ALU.mult).then_inc(neg_done, 1)

                    def normalise(u):
                        w = (unit(u)[1] + 1) * P
                        dve.wait_ge(exp_done, base + u + 1)
                        dve.reciprocal(inv[:, u:u + 1], total[:, u:u + 1]).then_inc(inv_done, 1)
                        dve.wait_ge(inv_done, base + u + 1)
                        dve.tensor_scalar(prob[u % 3][:, 0:w], prob[u % 3][:, 0:w], inv[:, u:u + 1], None,
                                          ALU.mult).then_inc(prob_done, 1)

                    def low_parts(s):
                        for h in range(2):
                            rows = slice(HD * h, HD * (h + 1))
                            dve.wait_ge(hi_done, 3 * (2 * i + s) + h + 1)
                            dve.scalar_tensor_tensor(out=q_lo[h][rows, :], in0=banks(ps, 0, 2)[rows, :], scalar=SCALE,
                                                     in1=q_hi[h][rows, :].bitcast(F32), op0=ALU.mult,
                                                     op1=ALU.subtract).then_inc(split_done, 1)
                        dve.wait_ge(hi_done, 3 * (2 * i + s) + 3)
                        dve.tensor_tensor(k_lo[:], banks(ps, 2, 2), k_hi[:].bitcast(F32), ALU.subtract).then_inc(split_done, 1)

                    if s == 0:
                        low_parts(0)
                    score(0)
                    for u in range(UNITS):
                        if u + 1 < UNITS:
                            score(u + 1)
                        normalise(u)
                    if s == 0:
                        low_parts(1)
                    dve.wait_ge(mix_hi_done, 2 * i + s + 1)
                    dve.tensor_tensor(mix_lo[:, ds(2 * i + s, 1), :], banks(ps, 6, 2),
                                      mix_hi[:, ds(2 * i + s, 1), :].bitcast(F32), ALU.subtract).then_inc(mix_done, 1)



def signal(steps, sem):
    steps.wait()
    steps.eng.sem_inc(sem, 1)


def rotate(steps, x, out, table, tmp):
    e = steps.eng
    a, b = x[..., 0], x[..., 1]
    cos, sin = table
    for dst, u, w in ((0, a, cos), (1, b, sin), (2, b, cos), (3, a, sin)):
        steps.done(e.tensor_tensor(tmp[dst], u, w, ALU.mult))
    steps.wait()
    steps.done(e.tensor_tensor(out[..., 0], tmp[0], tmp[1], ALU.subtract))
    steps.done(e.tensor_tensor(out[..., 1], tmp[2], tmp[3], ALU.add))


def group_norm(steps, v_ready, root, nth, src, dst, stats, mv, rows, n):
    e = steps.eng
    for j in range(n):
        steps.done(e.bn_stats(stats[rows, j, :], src(j)))
    steps.wait()
    for j in range(n):
        steps.done(e.bn_aggr(mv[rows, j, 0:2], stats[rows, j, :]))
    steps.wait()
    col = lambda c: mv[rows, 0:n, c]
    steps.done(e.tensor_scalar(col(1), col(1), EPS, None, ALU.add))
    signal(steps, v_ready)
    e.wait_ge(root, nth)
    steps.then(e.reciprocal(col(3), col(2)))
    steps.then(e.tensor_tensor(col(4), col(3), col(3), ALU.mult))
    steps.then(e.tensor_tensor(col(4), col(4), col(1), ALU.mult))
    steps.then(e.tensor_scalar(col(4), col(4), -0.5, 1.5, ALU.mult, ALU.add))
    steps.then(e.tensor_tensor(col(3), col(3), col(4), ALU.mult))
    for j in range(n):
        steps.done(e.tensor_scalar(dst(j), src(j), mv[rows, j, 0:1], mv[rows, j, 3:4], ALU.subtract, ALU.mult))
    steps.wait()


def stage_prompt_retention(nc, io, ps, ident, mix_hi, mix_lo):
    st = Stage(nc, "ret")
    W2 = 2 * RV
    with st.ctx:
        rot = st.sb("rot", [P, 2, TT, RD])
        dmask = st.sb("dmask", [P, RH, P])
        dout = st.sb("dout", [P, 2, P])
        din, gch = st.sb("din", [P, RH]), st.sb("gch", [P, 2])
        gain = st.sb("gain", [P, RH * RV])
        q_in = [st.sb(f"q{a}", [P, TT, P]) for a in range(2)]
        k_in = [st.sb(f"k{a}", [P, TT, P]) for a in range(2)]
        v = [st.sb(f"v{a}", [P, TT, W2]) for a in range(2)]
        g = [st.sb(f"g{a}", [P, TT, W2]) for a in range(2)]
        eg = st.sb("eg", [P, TT, W2])
        q_rot, k_rot = ([st.sb(f"{n}{a}", [P, TT, P]) for a in range(2)] for n in ("q_rot", "k_rot"))
        kd = st.sb("kd", [P, TT, P])
        qT, kT, qdT = (st.sb(n, [P, S]) for n in ("qT", "kT", "qdT"))
        sT = [st.sb(f"sT{h}", [P, S]) for h in range(2)]
        state = st.sb("state", [P, TT, P])
        on = [st.sb(f"on{h}", [P, S]) for h in range(2)]
        tmp_q, tmp_k = ([st.sb(f"{n}{j}", [P, TT, RD]) for j in range(4)] for n in ("tmp_q", "tmp_k"))
        stats = st.sb("stats", [P, TT, 6])
        mv = st.sb("mv", [P, TT, 5])
        tables, rot_in, silu_done = st.sem("tables"), st.sem("rot_in"), st.sem("silu_done")
        q_ready = [st.sem(f"q_ready{a}") for a in range(2)]
        qk_in, vg_in = ([st.sem(f"{n}_in{a}") for a in range(2)] for n in ("qk", "vg"))
        dve_s, pool_s = st.sem("dve_steps"), st.sem("pool_steps")
        (k_ready, q_turned, k_turned, qT_done, kT_done, qd_done, kd_done, kv_made, states_done, sT_made,
         sT_done, o_made, v_ready, root, on_ready, o_turned, hi_done, sigmoid_done, gate_done, mixed, state_put) = (
            st.sem(n) for n in (
                "k_ready", "q_turned", "k_turned", "qT_done", "kT_done", "qd_done", "kd_done", "kv_made",
                "states_done", "sT_made", "sT_done", "o_made", "v_ready", "root", "on_ready", "o_turned", "hi_done",
                "sigmoid_done", "gate_done", "mixed", "state_put"))
        proj = io["proj"][0:S, :].rearrange("(t p) c -> p t c", p=P)
        QC, KC, VC, GC = 3 * AW, 3 * AW + RH * RD, 3 * AW + 2 * RH * RD, 3 * AW + 2 * RH * RD + RH * RV
        even_odd = lambda x: x.rearrange("p t (j e) -> p t j e", e=2)
        by_chunk = lambda x: x.rearrange("p (t c) -> p t c", t=TT)
        Q_BANK, K_BANK, KV_BANK = 6, 0, 4
        O_BANK = (2, KV_BANK)
        T_BANK = (Q_BANK, K_BANK)
        block = st.block()

        @block.sync
        def _(sp):
            for a in range(2):
                sp.dma_start(q_in[a][:], proj[:, :, QC + a * P:QC + (a + 1) * P]).then_inc(qk_in[a], 16)
                sp.dma_start(k_in[a][:], proj[:, :, KC + a * P:KC + (a + 1) * P]).then_inc(qk_in[a], 16)
                if a == 0:
                    sp.dma_start(rot[:].rearrange("p a b c -> p (a b c)"), io["rot_p"]).then_inc(rot_in, 16)
                    for dst, n in ((din[:], "din_p"), (dout[:].rearrange("p a b -> p (a b)"), "dout_p"), (gch[:], "gchunk_p"),
                                   (dmask[:].rearrange("p a b -> p (a b)"), "dmask_p")):
                        sp.dma_start(dst, io[n]).then_inc(tables, 16)
                    sp.dma_start(gain[:], io["ret_gain"][0].partition_broadcast(P)).then_inc(tables, 16)
                sp.dma_start(v[a][:], proj[:, :, VC + a * W2:VC + (a + 1) * W2]).then_inc(vg_in[a], 16)
                sp.dma_start(g[a][:], proj[:, :, GC + a * W2:GC + (a + 1) * W2]).then_inc(vg_in[a], 16)
            for a in range(2):
                sp.wait_ge(states_done, a + 1)
                sp.dma_start(io["ret_prompt"][0, 0, 2 * a:2 * a + 2].rearrange("h d e -> (h d) e"),
                             state[:, TT - 1, :]).then_inc(state_put, 16)
            sp.wait_ge(state_put, 32)

        @block.gpsimd
        def _(pool):
            steps = Steps(pool, pool_s)
            angles_of = (rot[:, 0], rot[:, 1])
            pool.wait_ge(rot_in, 16)
            pool.wait_ge(qk_in[0], 32)
            rotate(steps, even_odd(k_in[0][:]), even_odd(k_rot[0][:]), angles_of, [x[:] for x in tmp_k])
            signal(steps, k_ready)
            pool.wait_ge(qk_in[1], 32)
            rotate(steps, even_odd(k_in[1][:]), even_odd(k_rot[1][:]), angles_of, [x[:] for x in tmp_k])
            signal(steps, k_ready)
            rotate(steps, even_odd(q_in[1][:]), even_odd(q_rot[1][:]), angles_of, [x[:] for x in tmp_k])
            signal(steps, q_ready[1])
            pool.wait_ge(tables, 80)
            for a in range(2):
                if a:
                    pool.wait_ge(sigmoid_done, a + 1)
                    steps.then(pool.tensor_tensor(g[a][:], g[a][:], eg[:], ALU.mult))
                else:
                    pool.wait_ge(silu_done, 1)
                steps.then(pool.tensor_tensor(g[a][:], g[a][:], gain[:, a * W2:(a + 1) * W2].unsqueeze(1).broadcast_to([P, TT, W2]),
                                              ALU.mult))
                signal(steps, gate_done)

        @block.scalar
        def _(act):
            def sigmoid(a):
                act.wait_ge(vg_in[a], 32)
                if a:
                    act.wait_ge(gate_done, a)
                act.activation(eg[:], g[a][:], ACT.Sigmoid).then_inc(sigmoid_done, 1)

            def take_turned(a):
                act.wait_ge(q_turned, a + 1)
                if a:
                    act.wait_ge(o_made, 2 * a)
                act.copy(qT[:], banks(ps, Q_BANK, 2)).then_inc(qT_done, 1)
                act.wait_ge(k_turned, a + 1)
                act.mul(kT[:], banks(ps, K_BANK, 2), RD ** -0.5).then_inc(kT_done, 1)

            def square_root(n):
                act.wait_ge(v_ready, n + 1)
                act.activation(mv[:, :, 2], mv[:, :, 1], ACT.Sqrt).then_inc(root, 1)

            def high_part(n):
                act.wait_ge(o_turned, n + 1)
                act.copy(mix_hi[:, 4 + n, :], banks(ps, T_BANK[n % 2], 2)).then_inc(hi_done, 1)

            take_turned(0)
            sigmoid(0)
            square_root(0)
            take_turned(1)
            high_part(0)
            square_root(1)
            high_part(1)
            sigmoid(1)
            square_root(2)
            high_part(2)
            square_root(3)
            high_part(3)

        @block.vector
        def _(dve):
            steps = Steps(dve, dve_s)

            def decayed_keys(a):
                dve.wait_ge(k_ready, a + 1)
                if a:
                    dve.wait_ge(kv_made, a)
                for h in range(2):
                    cols = slice(RD * h, RD * (h + 1))
                    steps.done(dve.tensor_scalar(kd[:, :, cols], k_rot[a][:, :, cols], din[:, 2 * a + h:2 * a + h + 1],
                                                 None, ALU.mult))
                signal(steps, kd_done)

            def decayed_queries(a):
                dve.wait_ge(qT_done, a + 1)
                steps.done(dve.tensor_tensor(by_chunk(qdT[:]), by_chunk(qT[:]),
                                             dout[:, a, :].unsqueeze(1).broadcast_to([P, TT, P]), ALU.mult))
                signal(steps, qd_done)

            def states(a):
                dve.wait_ge(kv_made, a + 1)
                if a:
                    dve.wait_ge(state_put, 16 * a)
                kv = by_chunk(banks(ps, KV_BANK, 2))
                steps.then(dve.tensor_copy(state[:, 0, :], kv[:, 0, :]))
                for t in range(1, TT):
                    steps.then(dve.scalar_tensor_tensor(out=state[:, t, :], in0=state[:, t - 1, :], scalar=gch[:, a:a + 1],
                                                        in1=kv[:, t, :], op0=ALU.mult, op1=ALU.add))
                signal(steps, states_done)

            def masked_scores(a):
                for h in range(2):
                    dve.wait_ge(sT_made, 2 * a + h + 1)
                    steps.done(dve.tensor_tensor(by_chunk(sT[h][:]), by_chunk(banks(ps, T_BANK[h], 2)),
                                                 dmask[:, 2 * a + h, :].unsqueeze(1).broadcast_to([P, TT, P]), ALU.mult))
                    signal(steps, sT_done)

            def norm_and_gate(a, h):
                n = 2 * a + h
                o = by_chunk(banks(ps, O_BANK[h], 2))
                dst = by_chunk(on[h][:])
                dve.wait_ge(o_made, n + 1)
                group_norm(steps, v_ready, root, n + 1, lambda j: o[:, j, :], lambda j: dst[:, j, :],
                           stats, mv, slice(0, P), TT)
                dve.wait_ge(gate_done, a + 1)
                steps.done(dve.tensor_tensor(dst, dst, g[a][:, :, RV * h:RV * (h + 1)], ALU.mult))
                signal(steps, on_ready)

            def low_part(n):
                dve.wait_ge(hi_done, n + 1)
                steps.done(dve.tensor_tensor(mix_lo[:, 4 + n, :], banks(ps, T_BANK[n % 2], 2),
                                             mix_hi[:, 4 + n, :].bitcast(F32), ALU.subtract))
                signal(steps, mixed)

            dve.wait_ge(rot_in, 16)
            dve.wait_ge(qk_in[0], 32)
            rotate(steps, even_odd(q_in[0][:]), even_odd(q_rot[0][:]), (rot[:, 0], rot[:, 1]), [x[:] for x in tmp_q])
            signal(steps, q_ready[0])
            dve.wait_ge(tables, 80)
            decayed_keys(0)
            decayed_queries(0)
            states(0)
            masked_scores(0)
            decayed_keys(1)
            dve.wait_ge(sigmoid_done, 1)
            steps.done(dve.tensor_tensor(g[0][:], g[0][:], eg[:], ALU.mult))
            signal(steps, silu_done)
            norm_and_gate(0, 0)
            norm_and_gate(0, 1)
            low_part(0)
            decayed_queries(1)
            low_part(1)
            states(1)
            masked_scores(1)
            norm_and_gate(1, 0)
            low_part(2)
            norm_and_gate(1, 1)
            low_part(3)

        @block.tensor
        def _(pe):
            def turn(src, first, sem):
                for t in range(TT):
                    mm = pe.transpose(banks(ps, first, 2)[:, t * P:(t + 1) * P], src(t), ident[:])
                mm.then_inc(sem, 1)

            def turn_queries_and_keys(a):
                if a:
                    pe.wait_ge(sT_done, 2 * a)
                pe.wait_ge(q_ready[a], 1)
                turn(lambda t: q_rot[a][:, t, :], Q_BANK, q_turned)
                pe.wait_ge(k_ready, a + 1)
                turn(lambda t: k_rot[a][:, t, :], K_BANK, k_turned)

            def chunk_products(a):
                pe.wait_ge(kd_done, a + 1)
                pe.wait_ge(vg_in[a], 32)
                if a:
                    pe.wait_ge(on_ready, 2 * a)
                for h in range(2):
                    for t in range(TT):
                        mm = pe.matmul(banks(ps, KV_BANK, 2)[RD * h:RD * (h + 1), t * P:(t + 1) * P],
                                       kd[:, t, RD * h:RD * (h + 1)], v[a][:, t, RV * h:RV * (h + 1)],
                                       start=True, stop=True)
                mm.then_inc(kv_made, 1)

            def scores(a):
                pe.wait_ge(qT_done, a + 1)
                pe.wait_ge(kT_done, a + 1)
                for h in range(2):
                    rows = slice(RD * h, RD * (h + 1))
                    if a:
                        pe.wait_ge(mixed, 2 * (a - 1) + h + 1)
                    for t in range(TT):
                        cols = slice(t * P, (t + 1) * P)
                        mm = pe.matmul(banks(ps, T_BANK[h], 2)[:, cols], kT[rows, cols], qT[rows, cols], start=True, stop=True)
                    mm.then_inc(sT_made, 1)

            def outputs(a):
                pe.wait_ge(qd_done, a + 1)
                pe.wait_ge(states_done, a + 1)
                for h in range(2):
                    rows = slice(RD * h, RD * (h + 1))
                    pe.wait_ge(sT_done, 2 * a + h + 1)
                    for t in range(TT):
                        cols = slice(t * P, (t + 1) * P)
                        out = banks(ps, O_BANK[h], 2)[:, cols]
                        mm = pe.matmul(out, sT[h][:, cols], v[a][:, t, RV * h:RV * (h + 1)], start=True, stop=(t == 0))
                        if t:
                            mm = pe.matmul(out, qdT[rows, cols], state[rows, t - 1, :], start=False, stop=True)
                    mm.then_inc(o_made, 1)

            def turn_output(a, h):
                pe.wait_ge(on_ready, 2 * a + h + 1)
                if a == 0:
                    pe.wait_ge((qT_done, kT_done)[h], 2)
                turn(lambda t: on[h][:, t * P:(t + 1) * P], T_BANK[h], o_turned)

            turn_queries_and_keys(0)
            chunk_products(0)
            scores(0)
            outputs(0)
            turn_queries_and_keys(1)
            turn_output(0, 0)
            turn_output(0, 1)
            chunk_products(1)
            scores(1)
            outputs(1)
            turn_output(1, 0)
            turn_output(1, 1)



def load_cached(sp, io, cache, dst, sem, seq):
    src = io[cache][0, ds(seq, 1)].rearrange("o n h d -> (o n) (h d)")
    old = src[0:OLD, :].rearrange("(j g r) c -> j g r c", g=16, r=16)
    for j in range(6):
        sp.dma_start(dst[:, j, :], old[j, :, 0:8]).then_inc(sem, 16)
    sp.dma_start(dst[:, 6:, :], src[OLD:, :].rearrange("(j p) c -> p j c", p=P)).then_inc(sem, 16)


def stage_sample_heads(nc, io, ps, ident, mix_s, q_blocks, kT_new, K, k_in):
    st = Stage(nc, "smp", clear=True)
    QC, VC, GC = 3 * AW, 3 * AW + 2 * RH * RD, 3 * AW + 2 * RH * RD + RH * RV
    with st.ctx:
        x, lo_rows = st.sb("x", [NS, IN_W]), st.sb("lo_rows", [NS, IN_W])
        rope = st.sb("rope", [NS, 2, 2 * H, 8])
        rot = st.sb("rot", [NS, 2, 2 * RH * RD // 2])
        dmask = st.sb("dmask", [NS, RH * NS])
        dout = st.sb("dout", [P, RH, 4, NS])
        din = st.sb("din", [NS, RH, 4, P])
        gain = st.sb("gain", [NS, RH * RV])
        state = st.sb("state", [P, 4, RH, RV])
        tmp = [st.sb(f"tmp{j}", [NS, 256]) for j in range(4)]
        turned_qk = st.sb("rotated", [NS, 1, 2 * RH * RD])
        twice = st.sb("twice", [NS, 2 * RH, 2, RD])
        qT, kT = st.sb("qT", [P, RH, NS]), st.sb("kT", [P, RH, NS])
        q_masked = st.sb("q_masked", [P, RH, 4, NS])
        k_masked = st.sb("k_masked", [NS, RH, 4, P])
        sT = st.sb("sT", [NS, RH * NS])
        on = st.sb("on", [NS, RH * RV])
        eg = st.sb("eg", [NS, RH * RV])
        stats, mv = st.sb("stats", [NS, RH, 6]), st.sb("mv", [NS, RH, 5])
        (tables, x_in, s_in, dve_s, roped, put, rotated, att_turned, ret_turned, qT_done, sT_made, sT_done, kv_made, o_made,
         v_ready, root, on_ready, o_turned, hi_done, sigmoid_done, state_done, g_ready) = (st.sem(n) for n in (
            "tables", "x_in", "s_in", "dve_steps", "roped", "put", "rotated", "att_turned", "ret_turned", "qT_done", "sT_made",
            "sT_done", "kv_made", "o_made", "v_ready", "root", "on_ready", "o_turned", "hi_done", "sigmoid_done", "state_done",
            "g_ready"))
        flat = lambda t: t[:].rearrange("p a b -> p (a b)")
        flat4 = lambda t: t[:].rearrange("p a b c -> p (a b c)")
        st_in = io["state_ret"][0].rearrange("(q b) h d e -> b d q h e", b=2)
        st_out = io["ret_sample"][0].rearrange("(q b) h d e -> b d q h e", b=2)
        block = st.block()

        @block.sync
        def _(sp):
            sp.dma_start(x[:], io["proj"][S:S + NS, :]).then_inc(x_in, 16)
            sp.dma_start(lo_rows[:], io["proj"][S + NS:S + P, :]).then_inc(x_in, 16)
            sp.dma_start(flat4(rope), io["rope_s"]).then_inc(tables, 16)
            for dst, n in ((flat(rot), "rot_s"), (dmask[:], "dmask_s"), (flat4(dout), "dout_s"), (flat4(din), "din_s")):
                sp.dma_start(dst, io[n]).then_inc(tables, 16)
            sp.dma_start(gain[:], io["ret_gain"][0].partition_broadcast(NS)).then_inc(tables, 16)
            for b in range(2):
                for q in range(4):
                    sp.dma_start(state[RD * b:RD * (b + 1), q], st_in[b, :, q]).then_inc(s_in, 16)
            for b in range(2):
                load_cached(sp, io, "cache_k", K[b], k_in[b], b)
            sp.wait_ge(roped, 1)
            sp.dma_start(io["k_sample"].rearrange("o b t h d -> (o b t) (h d)"), x[:, AW:2 * AW]).then_inc(put, 16)
            sp.dma_start(io["v_sample"].rearrange("o b t h d -> (o b t) (h d)"), x[:, 2 * AW:3 * AW]).then_inc(put, 16)
            sp.wait_ge(state_done, 1)
            for b in range(2):
                for q in range(4):
                    sp.dma_start(st_out[b, :, q], state[RD * b:RD * (b + 1), q]).then_inc(put, 16)
            sp.wait_ge(put, 16 * 10)

        @block.vector
        def _(dve):
            steps = Steps(dve, dve_s)
            steps.done(dve.memset(q_blocks[:], 0.0))
            dve.wait_ge(x_in, 32)
            steps.then(dve.tensor_tensor(x[:], x[:], lo_rows[:], ALU.add))
            signal(steps, g_ready)
            dve.wait_ge(tables, 96)
            heads = x[:, 0:2 * AW].rearrange("p (h d) -> p h d", d=HD)
            a, b = heads[:, :, 0:8], heads[:, :, 8:16]
            t8 = [t[:, 0:128].rearrange("p (h j) -> p h j", j=8) for t in tmp]
            for dst, u, w in ((0, a, 0), (1, b, 1), (2, b, 0), (3, a, 1)):
                steps.done(dve.tensor_tensor(t8[dst], u, rope[:, w], ALU.mult))
            steps.wait()
            steps.done(dve.tensor_tensor(a, t8[0], t8[1], ALU.subtract))
            steps.done(dve.tensor_tensor(b, t8[2], t8[3], ALU.add))
            signal(steps, roped)
            qk = x[:, QC:VC].rearrange("p (o j e) -> p o j e", o=1, e=2)
            rotate(steps, qk, turned_qk[:].rearrange("p o (j e) -> p o j e", e=2),
                   (rot[:, 0:1], rot[:, 1:2]), [t[:].unsqueeze(1) for t in tmp])
            steps.wait()
            rr = turned_qk[:, 0].rearrange("p (h d) -> p h d", d=RD)
            steps.done(dve.tensor_copy(twice[:], rr.unsqueeze(2).broadcast_to([NS, 2 * RH, 2, RD])))
            signal(steps, rotated)
            for h in range(RH):
                dup = twice[:, RH + h].rearrange("p a d -> p (a d)")
                steps.done(dve.tensor_tensor(k_masked[:, h], dup.unsqueeze(1).broadcast_to([NS, 4, P]), din[:, h], ALU.mult))
            dve.wait_ge(att_turned, 1)
            for h in range(H):
                rows = slice(HD * (h % 2), HD * (h % 2 + 1))
                src = ps[rows, 0, (h // 2) * NS:(h // 2 + 1) * NS].rearrange("p (b t) -> p b t", b=DB)
                steps.done(dve.tensor_scalar(q_blocks[rows, :, h // 2, h * DS:(h + 1) * DS], src, SCALE, None, ALU.mult))
            steps.done(dve.tensor_copy(kT_new[:], ps[:, 0, 4 * NS:8 * NS].rearrange("p (c n) -> p c n", n=NS)))
            dve.wait_ge(ret_turned, 1)
            steps.done(dve.tensor_copy(flat(qT), ps[:, 1, 0:RH * NS]))
            steps.done(dve.tensor_scalar(flat(kT), ps[:, 1, RH * NS:2 * RH * NS], RD ** -0.5, None, ALU.mult))
            steps.wait()
            for h in range(RH):
                steps.done(dve.tensor_tensor(q_masked[:, h], qT[:, h].unsqueeze(1).broadcast_to([P, 4, NS]), dout[:, h], ALU.mult))
            signal(steps, qT_done)
            dve.wait_ge(sT_made, 1)
            steps.done(dve.tensor_tensor(sT[:], ps[0:NS, 2, 0:RH * NS], dmask[:], ALU.mult))
            signal(steps, sT_done)
            dve.wait_ge(sigmoid_done, 1)
            steps.then(dve.tensor_tensor(eg[:], eg[:], x[:, GC:], ALU.mult))
            steps.then(dve.tensor_tensor(eg[:], eg[:], gain[:], ALU.mult))
            dve.wait_ge(o_made, 1)
            dve.wait_ge(kv_made, 1)
            for h in range(RH):
                steps.done(dve.scalar_tensor_tensor(out=state[:, :, h, :], in0=state[:, :, h, :], scalar=GCHUNK_S[h],
                                                    in1=ps[:, 4:8, h * RV:(h + 1) * RV], op0=ALU.mult, op1=ALU.add))
            signal(steps, state_done)
            o = ps[0:NS, 3, :].rearrange("p (h e) -> p h e", e=RV)
            oo = on[:].rearrange("p (h e) -> p h e", e=RV)
            group_norm(steps, v_ready, root, 1, lambda j: o[:, j, :], lambda j: oo[:, j, :], stats, mv, slice(0, NS), RH)
            steps.done(dve.tensor_tensor(on[:], on[:], eg[:], ALU.mult))
            signal(steps, on_ready)
            dve.wait_ge(hi_done, 1)
            src = ps[:, 2, 0:RH * NS].rearrange("p (h n) -> p h n", n=NS)
            steps.then(dve.tensor_tensor(mix_s[:, 4:8, NS:P], src, mix_s[:, 4:8, 0:NS].bitcast(F32), ALU.subtract))

        @block.scalar
        def _(act):
            act.wait_ge(g_ready, 1)
            act.activation(eg[:], x[:, GC:], ACT.Sigmoid).then_inc(sigmoid_done, 1)
            act.wait_ge(v_ready, 1)
            act.activation(mv[:, :, 2], mv[:, :, 1], ACT.Sqrt).then_inc(root, 1)
            act.wait_ge(o_turned, 1)
            act.copy(mix_s[:, 4:8, 0:NS], ps[:, 2, 0:RH * NS].rearrange("p (h n) -> p h n", n=NS)).then_inc(hi_done, 1)

        @block.tensor
        def _(pe):
            pe.wait_ge(roped, 1)
            for c in range(8):
                mm = pe.transpose(ps[:, 0, c * NS:(c + 1) * NS], x[:, c * P:(c + 1) * P], ident[0:NS, 0:NS])
            mm.then_inc(att_turned, 1)
            pe.wait_ge(rotated, 1)
            for c in range(2 * RH):
                mm = pe.transpose(ps[:, 1, c * NS:(c + 1) * NS], twice[:, c].rearrange("p a d -> p (a d)"), ident[0:NS, 0:NS])
            mm.then_inc(ret_turned, 1)
            pe.wait_ge(qT_done, 1)
            pe.wait_ge(s_in, 128)
            vcols = lambda h: x[:, VC + h * RV:VC + (h + 1) * RV]
            for h in range(RH):
                mm = pe.matmul(ps[0:NS, 2, h * NS:(h + 1) * NS], kT[0:RD, h, :], qT[0:RD, h, :], start=True, stop=True)
            mm.then_inc(sT_made, 1)
            for h in range(RH):
                for b in range(4):
                    mm = pe.matmul(ps[:, 4 + b, h * RV:(h + 1) * RV], k_masked[:, h, b, :], vcols(h), start=True, stop=True)
            mm.then_inc(kv_made, 1)
            pe.wait_ge(sT_done, 1)
            for h in range(RH):
                out = ps[0:NS, 3, h * RV:(h + 1) * RV]
                pe.matmul(out, sT[:, h * NS:(h + 1) * NS], vcols(h), start=True, stop=False)
                for b in range(4):
                    mm = pe.matmul(out, q_masked[:, h, b, :], state[:, b, h, :], start=False, stop=(b == 3))
            mm.then_inc(o_made, 1)
            pe.wait_ge(on_ready, 1)
            for h in range(RH):
                mm = pe.transpose(ps[:, 2, h * NS:(h + 1) * NS], on[:, h * RV:(h + 1) * RV], ident[0:NS, 0:NS])
            mm.then_inc(o_turned, 1)



def stage_sample_attention(nc, io, ps, ident, mix_s, q_blocks, kT_new, K, k_in):
    st = Stage(nc, "cache")
    CHUNKS = ((0, 4), (4, 4), (8, 2))
    PAIRS = DB // 2
    with st.ctx:
        bias = st.sb("bias", [P, NKEYS])
        V = [st.sb(f"V{b}", [P, KTILES, AW]) for b in range(2)]
        v_new = [st.sb(f"v_new{b}", [DS, AW]) for b in range(2)]
        q_now = st.sb("q_now", [P, 2, 4, NS])
        k_now = st.sb("k_now", [P, 4, 2 * DS])
        kT = [st.sb(f"kT{s}", [P, 4, CH]) for s in range(2)]
        prob = st.sb("prob", [P, NKEYS])
        probT = st.sb("probT", [P, KTILES + 1, P])
        rows = st.sb("rows", [P, AW])
        top, neg, total, inv, waited = (st.sb(n, [P, 1]) for n in ("top", "neg", "total", "inv", "waited"))
        mix_f = st.sb("mix_f", [P, 4, NS])
        v_in = [st.sem(f"v_in{b}") for b in range(2)]
        (tables, k_free, v_free, q_staged, turned, kT_act, kT_dve, scored, s_made, neg_done, exp_done, inv_done, p_turned,
         pT_act, pT_dve, pv_made, rows_done, rows_turned, out_act, out_dve, hi_done, mixed) = (st.sem(n) for n in (
            "tables", "k_free", "v_free", "q_staged", "turned", "kT_act", "kT_dve", "scored", "s_made", "neg_done", "exp_done",
            "inv_done", "p_turned", "pT_act", "pT_dve", "pv_made", "rows_done", "rows_turned", "out_act", "out_dve",
            "hi_done", "mixed"))
        v_put = io["v_sample"].rearrange("o b t h d -> t (o b) (h d)")
        block = st.block()


        @block.sync
        def _(sp):
            def keys(i, b):
                sp.wait_ge(k_free, 2 * i + b - 1)
                load_cached(sp, io, "cache_k", K[b], k_in[b], 2 * i + b)

            def values(i, b, first=False):
                if not first:
                    sp.wait_ge(v_free, 2 * i + b - 1)
                load_cached(sp, io, "cache_v", V[b], v_in[b], 2 * i + b)
                sp.dma_start(v_new[b][:], v_put[:, ds(2 * i + b, 1), :]).then_inc(v_in[b], 16)

            sp.dma_start(bias[:], io["bias_s"]).then_inc(tables, 16)
            values(0, 0, first=True)
            values(0, 1, first=True)
            keys(1, 0)
            keys(1, 1)
            with sp.Fori(1, PAIRS - 1) as i:
                keys(i + 1, 0)
                values(i, 0)
                values(i, 1)
                keys(i + 1, 1)
            values(PAIRS - 1, 0)
            values(PAIRS - 1, 1)

        @block.tensor
        def _(pe):
            def turn(i, n):
                b, (first, count) = n // 3, CHUNKS[n % 3]
                if n % 3 == 0:
                    pe.wait_ge(k_in[b], 16 * 7 * i + 16 * 7)
                for c in range(4):
                    for t in range(count):
                        mm = pe.transpose(ps[:, c, t * P:(t + 1) * P], K[b][:, first + t, c * P:(c + 1) * P], ident[:])
                mm.then_inc(turned, 1)

            def scores(i, n):
                b, (first, count) = n // 3, CHUNKS[n % 3]
                w = count * P + (DS if n % 3 == 2 else 0)
                if n == 0:
                    pe.wait_ge(q_staged, 2 * i + 2)
                for c in range(4):
                    mm = pe.matmul(ps[NS * b:NS * (b + 1), 4 + n % 3, 0:w], q_now[:, b, c, :], kT[n % 2][:, c, 0:w],
                                   start=(c == 0), stop=(c == 3))
                mm.then_inc(scored, 1)
                if n % 3 == 2:
                    pe.wait_ge(scored, 6 * i + n + 1)
                    pe.sem_inc(k_free, 1)

            def turn_probs(j):
                pe.wait_ge(exp_done, j + 1)
                for t in range(KTILES + 1):
                    w = P if t < KTILES else DS
                    out = ps[:, t // 4, (t % 4) * P:(t % 4 + 1) * P] if t < KTILES else ps[0:DS, 3, 0:P]
                    mm = pe.transpose(out, prob[:, t * P:t * P + w], ident[:])
                mm.then_inc(p_turned, 1)

            def wait_probs(j):
                pe.wait_ge(pT_act, 2 * j + 2)
                pe.wait_ge(pT_dve, 2 * j + 2)

            def values(j, b):
                cols = slice(NS * b, NS * (b + 1))
                if b == 0:
                    pe.wait_ge(out_dve, 4 * j + 4)
                pe.wait_ge(v_in[b], 16 * 8 * j + 16 * 8)
                for t in range(KTILES):
                    pe.matmul(ps[cols, 7, :], probT[:, t, cols], V[b][:, t, :], start=(t == 0), stop=False)
                mm = pe.matmul(ps[cols, 7, :], probT[0:DS, KTILES, cols], v_new[b][:], start=False, stop=True)
                mm.then_inc(pv_made, 1)
                pe.wait_ge(pv_made, 2 * j + b + 1)
                pe.sem_inc(v_free, 1)

            def turn_rows(j):
                pe.wait_ge(rows_done, j + 1)
                for c in range(4):
                    mm = pe.transpose(ps[:, 7, c * P:(c + 1) * P], rows[:, c * P:(c + 1) * P], ident[:])
                mm.then_inc(rows_turned, 1)

            def pair(i, first=False):
                j = i - 1
                turn(i, 0)
                for n in range(6):
                    pe.wait_ge(kT_act, 6 * i + n + 1)
                    pe.wait_ge(kT_dve, 6 * i + n + 1)
                    if n == 0 and not first:
                        turn_probs(j)
                        scores(i, 0)
                        wait_probs(j)
                        turn(i, 1)
                        continue
                    if n + 1 < 6:
                        turn(i, n + 1)
                    scores(i, n)
                    if n in (1, 2) and not first:
                        values(j, n - 1)
                    if n == 4 and not first:
                        turn_rows(j)

            pair(0, first=True)
            with pe.Fori(1, PAIRS) as i:
                pair(i)
            j = PAIRS - 1
            turn_probs(j)
            wait_probs(j)
            values(j, 0)
            values(j, 1)
            turn_rows(j)

        def head_rows(j, h):
            part = slice(HD * (h % 2), HD * (h % 2 + 1))
            src = ps[part, 7, (h // 2) * P:(h // 2 + 1) * P].rearrange("p (b h t) -> p b h t", b=2, t=DS)[:, :, h, :]
            dst = mix_f[part, h // 2, ds(j * 2 * DS, 2 * DS)].rearrange("p (b t) -> p b t", b=2)
            return dst, src

        @block.scalar
        def _(act):
            def exponent(j):
                act.wait_ge(neg_done, j + 1)
                act.activation(prob[:], prob[:], ACT.Exp, bias=neg[:], accum_out=total[:]).then_inc(exp_done, 1)

            def take_probs(j):
                act.wait_ge(p_turned, j + 1)
                act.copy(probT[:, 0:4, :], ps[:, 0, :].rearrange("p (j n) -> p j n", n=P)).then_inc(pT_act, 1)
                act.copy(probT[:, 4:8, :], ps[:, 1, :].rearrange("p (j n) -> p j n", n=P)).then_inc(pT_act, 1)

            def take_rows(j):
                act.wait_ge(rows_turned, j + 1)
                for h in range(0, H, 2):
                    dst, src = head_rows(j, h)
                    act.copy(dst, src).then_inc(out_act, 1)

            def pair(i, first=False):
                j = i - 1
                if not first:
                    exponent(j)
                act.copy(q_now[:], q_blocks[:, ds(2 * i, 2)]).then_inc(q_staged, 1)
                act.copy(k_now[:], kT_new[:, :, ds(i * 2 * DS, 2 * DS)]).then_inc(q_staged, 1)
                for n in range(6):
                    w = CHUNKS[n % 3][1] * P
                    act.wait_ge(turned, 6 * i + n + 1)
                    act.copy(kT[n % 2][:, 0:2, 0:w], ps[:, 0:2, 0:w]).then_inc(kT_act, 1)
                    if n == 0 and not first:
                        take_probs(j)
                if not first:
                    take_rows(j)

            pair(0, first=True)
            with act.Fori(1, PAIRS) as i:
                pair(i)
            exponent(PAIRS - 1)
            take_probs(PAIRS - 1)
            take_rows(PAIRS - 1)
            act.wait_ge(out_act, 4 * PAIRS)
            act.wait_ge(out_dve, 4 * PAIRS + 4)
            act.copy(mix_s[:, 0:4, 0:NS], mix_f[:]).then_inc(hi_done, 1)

        @block.vector
        def _(dve):
            dve.sem_inc(out_dve, 4)
            dve.wait_ge(tables, 16)

            def softmax_top(j):
                dve.wait_ge(scored, 6 * j + 6)
                dve.memset(waited[:], 0.0)
                dve.tensor_tensor_reduce(prob[:], banks(ps, 4, 3)[:, 0:NKEYS], bias[:], 1.0, NEG, ALU.add, ALU.max,
                                         top[:]).then_inc(s_made, 1)
                dve.wait_ge(s_made, j + 1)
                dve.tensor_scalar(neg[:], top[:], -1.0, None, ALU.mult).then_inc(neg_done, 1)

            def take_probs(j):
                dve.wait_ge(exp_done, j + 1)
                dve.reciprocal(inv[:], total[:]).then_inc(inv_done, 1)
                dve.wait_ge(p_turned, j + 1)
                dve.tensor_copy(probT[:, 8:10, :], ps[:, 2, 0:2 * P].rearrange("p (j n) -> p j n", n=P)).then_inc(pT_dve, 1)
                dve.tensor_copy(probT[0:DS, 10, :], ps[0:DS, 3, 0:P]).then_inc(pT_dve, 1)

            def scale_rows(j):
                dve.wait_ge(pv_made, 2 * j + 2)
                dve.wait_ge(inv_done, j + 1)
                dve.tensor_scalar(rows[:], ps[:, 7, :], inv[:], None, ALU.mult).then_inc(rows_done, 1)

            def take_rows(j):
                dve.wait_ge(out_act, 4 * j + 4)
                for h in range(1, H, 2):
                    dst, src = head_rows(j, h)
                    dve.tensor_copy(dst, src).then_inc(out_dve, 1)

            def pair(i, first=False):
                j = i - 1
                if not first:
                    softmax_top(j)
                for n in range(6):
                    w = CHUNKS[n % 3][1] * P
                    dve.wait_ge(turned, 6 * i + n + 1)
                    copy = dve.tensor_copy(kT[n % 2][:, 2:4, 0:w], ps[:, 2:4, 0:w])
                    if n % 3 == 2:
                        b = n // 3
                        dve.wait_ge(q_staged, 2 * i + 2)
                        copy = dve.tensor_copy(kT[n % 2][:, :, w:w + DS], k_now[:, :, b * DS:(b + 1) * DS])
                    copy.then_inc(kT_dve, 1)
                    if n == 0 and not first:
                        take_probs(j)
                    if n == 3 and not first:
                        scale_rows(j)
                if not first:
                    take_rows(j)

            pair(0, first=True)
            with dve.Fori(1, PAIRS) as i:
                pair(i)
            softmax_top(PAIRS - 1)
            take_probs(PAIRS - 1)
            scale_rows(PAIRS - 1)
            take_rows(PAIRS - 1)
            dve.wait_ge(hi_done, 1)
            dve.tensor_tensor(mix_s[:, 0:4, NS:P], mix_f[:], mix_s[:, 0:4, 0:NS].bitcast(F32), ALU.subtract).then_inc(mixed, 1)



def stage_output(nc, io, ps, mod_p, mix_hi, mix_lo, mix_s, x, xs, ss):
    st = Stage(nc, "outp", clear=True)
    NCH, OUTS, BANKS = D // CH, TT + 1, 6
    QUARTERS = 4
    quarter = lambda q: slice(q * KT // QUARTERS, (q + 1) * KT // QUARTERS)
    with st.ctx:
        raw = st.sb("raw", [P, KT, CH])
        w_hi = [st.sb(f"whi{s}", [P, KT, CH], F32R) for s in range(NCH)]
        w_lo = [st.sb(f"wlo{s}", [P, KT, CH], F32R) for s in range(NCH)]
        gate, gate_s = st.sb("gate", [P, D]), st.sb("gate_s", [NS, D])
        row = [st.sb(f"row{s}", [P, CH]) for s in range(2)]
        sq = st.sb("sq", [P, CH])
        raw_in = [st.sem(f"raw_in{q}") for q in range(QUARTERS)]
        x_in = [st.sem(f"x_in{t}") for t in range(TT + 1)]
        g_in, gs_in, w_hi_done, w_lo_done, made, lo_done, sum_done, gated, added, squared, put, zeroed = (st.sem(n) for n in (
            "g_in", "gs_in", "w_hi_done", "w_lo_done", "made", "lo_done", "sum_done", "gated", "added", "squared", "put", "zeroed"))
        columns_in = st.sem("columns_in")
        wv = io["w_out"].rearrange("o (k p) n -> p (o k) n", p=P)
        block = st.block()

        @block.sync
        def _(sp):
            def weights(c):
                for q in range(QUARTERS):
                    if c:
                        sp.wait_ge(w_lo_done, q + 1)
                    sp.dma_start(raw[:, quarter(q), :], wv[:, quarter(q), c * CH:(c + 1) * CH]).then_inc(raw_in[q], 16)

            weights(0)
            load_rows(sp, io, gate, None, G_A, g_in)
            load_rows(sp, io, None, gate_s, G_A, gs_in)
            load_columns(sp, io, mod_p, (SH_F, SC_F), columns_in)
            for t in range(TT):
                sp.dma_start(x[:, t, :], io["x_prompt"][0, t * P:(t + 1) * P, :]).then_inc(x_in[t], 16)
            sp.dma_start(xs[:], io["x_sample"].rearrange("b t d -> (b t) d")).then_inc(x_in[TT], 16)
            weights(1)
            for t in range(TT):
                sp.wait_ge(added, OUTS + t + 1)
                sp.dma_start(io["x1"][t * P:(t + 1) * P, :], x[:, t, :]).then_inc(put, 16)
            sp.wait_ge(added, 2 * OUTS)
            sp.dma_start(io["x1"][S:S + NS, :], xs[:]).then_inc(put, 16)
            sp.wait_ge(put, 16 * (TT + 1))
            sp.wait_ge(columns_in, 32)

        @block.gpsimd
        def _(pool):
            pool.memset(ss[:], 0.0).then_inc(zeroed, 1)
            for c in range(NCH):
                for o in range(OUTS):
                    n = c * OUTS + o
                    dst = x[:, o, c * CH:(c + 1) * CH] if o < TT else xs[:, c * CH:(c + 1) * CH]
                    r = row[n % 2][:] if o < TT else row[n % 2][0:NS, :]
                    pool.wait_ge(gated, n + 1)
                    pool.wait_ge(x_in[o], 16)
                    pool.tensor_tensor(dst, dst, r, ALU.add).then_inc(added, 1)

        @block.scalar
        def _(act):
            act.wait_ge(zeroed, 1)
            for c in range(NCH):
                for q in range(QUARTERS):
                    act.wait_ge(raw_in[q], 16 * c + 16)
                    act.copy(w_hi[c][:, quarter(q), :], raw[:, quarter(q), :]).then_inc(w_hi_done, 1)
            for c in range(NCH):
                for o in range(OUTS):
                    n = c * OUTS + o
                    if o == TT:
                        act.wait_ge(made, n + 1)
                        act.wait_ge(squared, n)
                        act.copy(sq[0:NS, :], ps[NS:P, n % BANKS, :]).then_inc(lo_done, 1)
                        act.wait_ge(sum_done, c + 1)
                    dst = x[:, o, c * CH:(c + 1) * CH] if o < TT else xs[:, c * CH:(c + 1) * CH]
                    rows = slice(0, P if o < TT else NS)
                    act.wait_ge(added, n + 1)
                    if n:
                        act.wait_ge(squared, n)
                    act.activation(sq[rows, :], dst, ACT.Square, accum_out=ss[rows, c, o:o + 1]).then_inc(squared, 1)

        @block.vector
        def _(dve):
            for c in range(NCH):
                for q in range(QUARTERS):
                    dve.wait_ge(w_hi_done, QUARTERS * c + q + 1)
                    dve.tensor_tensor(w_lo[c][:, quarter(q), :], raw[:, quarter(q), :],
                                      w_hi[c][:, quarter(q), :].bitcast(F32), ALU.subtract).then_inc(w_lo_done, 1)
            dve.wait_ge(g_in, 16)
            dve.wait_ge(gs_in, 16 * DB)
            for c in range(NCH):
                cols = slice(c * CH, (c + 1) * CH)
                for o in range(OUTS):
                    n = c * OUTS + o
                    dve.wait_ge(made, n + 1)
                    if n >= 2:
                        dve.wait_ge(added, n - 1)
                    if o < TT:
                        dve.tensor_tensor(row[n % 2][:], ps[:, n % BANKS, :], gate[:, cols], ALU.mult).then_inc(gated, 1)
                    else:
                        dve.wait_ge(lo_done, c + 1)
                        dve.tensor_tensor(row[n % 2][0:NS, :], ps[0:NS, n % BANKS, :], sq[0:NS, :], ALU.add).then_inc(sum_done, 1)
                        dve.wait_ge(sum_done, c + 1)
                        dve.tensor_tensor(row[n % 2][0:NS, :], row[n % 2][0:NS, :], gate_s[:, cols], ALU.mult).then_inc(gated, 1)

        @block.tensor
        def _(pe):
            for c in range(NCH):
                for o in range(OUTS):
                    n = c * OUTS + o
                    bank = ps[:, n % BANKS, :]
                    if n >= BANKS:
                        pe.wait_ge(gated, n - BANKS + 1)
                    if o < TT:
                        parts = ((mix_hi, w_hi), (mix_hi, w_lo), (mix_lo, w_hi))
                        cols = slice(o * P, (o + 1) * P)
                    else:
                        parts = ((mix_s, w_hi), (mix_s, w_lo))
                        cols = slice(0, P)
                    for k in range(KT):
                        if o == 0 and k % (KT // QUARTERS) == 0:
                            pe.wait_ge(w_lo_done, QUARTERS * c + k // (KT // QUARTERS) + 1)
                        for a, (z, w) in enumerate(parts):
                            mm = pe.matmul(bank, z[:, k, cols], w[c][:, k, :], start=(k == 0 and a == 0),
                                           stop=(k == KT - 1 and a == len(parts) - 1))
                    mm.then_inc(made, 1)



def stage_mlp(nc, io, ps, ident, mod_p, z_hi, z_lo, zs, y, ys, ss, last_rows, last_ss):
    st = Stage(nc, "mlp")
    J = GF // P
    turned_s = lambda ps: ps[:, 4, GF:GF + J * P].rearrange("p (j n) -> p j n", n=P)[:, :, 0:NS]
    MAIN = 2 * J
    OUTS = 2 * (TT + 1)
    with st.ctx:
        w1_raw, w2_raw = st.sb("w1_raw", [P, KT, GF]), st.sb("w2_raw", [P, J, D])
        w1_hi, w1_lo = (st.sb(n, [P, KT, GF], F32R) for n in ("w1_hi", "w1_lo"))
        w2_hi, w2_lo = (st.sb(n, [P, J, D], F32R) for n in ("w2_hi", "w2_lo"))
        h_hi, h_lo = ([st.sb(f"{n}{s}", [P, J, S], F32R) for s in range(2)] for n in ("h_hi", "h_lo"))
        hs = [st.sb(f"hs{s}", [P, J, P], F32R) for s in range(2)]
        pos = [st.sb(f"pos{s}", [P, CH]) for s in range(2)]
        lo_part, hid_s = st.sb("lo_part", [NS, GF]), st.sb("hid_s", [P, GF])
        (w1_in, w2_in, w1_free, w2_free, w1_hi_done, w2_hi_done, w1_ready, w2_ready, made1, relu_done, sq_done, h_hi_done,
         h_ready, s_made, s_lo, s_sum, hid_done, s_turned, hs_hi, hs_ready, made2, added, h_free, zeroed) = (st.sem(n) for n in (
            "w1_in", "w2_in", "w1_free", "w2_free", "w1_hi_done", "w2_hi_done", "w1_ready", "w2_ready", "made1", "relu_done",
            "sq_done", "h_hi_done", "h_ready", "s_made", "s_lo", "s_sum", "hid_done", "s_turned", "hs_hi", "hs_ready",
            "made2", "added", "h_free", "zeroed"))
        last_w2 = [w[:].rearrange("p k c -> p (k c)").rearrange("p (j n) -> p j n", j=J) for w in (w1_hi, w1_lo)]
        rows_in, ss_zeroed, gated, summed, squared = (st.sem(n) for n in ("rows_in", "ss_zeroed", "gated", "summed", "squared"))
        x1_in = [st.sem(f"x1_in{s}") for s in range(2)]
        x1_room = w1_raw[:].rearrange("p k c -> p (k c)").rearrange("p (s d) -> p s d", s=2)
        w1v = io["w_ff1"].rearrange("o (k p) n -> p (o k) n", p=P)
        w2v = io["w_ff2"].rearrange("o (j p) n -> p (o j) n", p=P)
        block = st.block()

        def split_hi(act, hi, raw, raw_in, free, hi_done, g):
            act.wait_ge(raw_in, 16 * g + 16)
            act.wait_ge(free, g + 1)
            act.copy(hi[:], raw[:]).then_inc(hi_done, 1)

        def split_lo(pool, lo, raw, hi, hi_done, ready, g):
            pool.wait_ge(hi_done, g + 1)
            pool.tensor_tensor(lo, raw[:], hi.bitcast(F32), ALU.subtract).then_inc(ready, 1)

        def load_w1(sp, g):
            sp.wait_ge(w1_ready, g + 1)
            sp.dma_start(w1_raw[:], w1v[:, :, ds(g * GF, GF)]).then_inc(w1_in, 16)

        def load_w2(sp, g):
            sp.wait_ge(w2_ready, g + 1)
            sp.dma_start(w2_raw[:], w2v[:, ds(g * J, J), :]).then_inc(w2_in, 16)

        def sp_first(sp):
            sp.sem_inc(w1_free, 1)
            sp.sem_inc(w2_free, 1)
            sp.sem_inc(w1_ready, 1)
            sp.sem_inc(w2_ready, 1)
            load_w1(sp, 0)
            load_w2(sp, 0)

        def pool_first(pool):
            split_lo(pool, w1_lo[:], w1_raw, w1_hi[:], w1_hi_done, w1_ready, 0)

        zf = [last_rows[2][:, 0:CH], last_rows[2][:, CH:2 * CH], pos[0][:], pos[1][:]]
        z_ready, z_half, _, x_read = norm_part(
            st, block, io, ps, ident, mod_p, z_hi, z_lo, zs, SH_F, SC_F, 2, 3, y, ys[0:NS, :], ss,
            last_rows[0][0:NS, :], last_rows[1][0:NS, :], zf,
            sp_extra=sp_first, pool_extra=pool_first,
            act_extra=lambda act: split_hi(act, w1_hi, w1_raw, w1_in, w1_free, w1_hi_done, 0))


        @block.sync
        def _(sp):
            wait_all(sp, z_ready)
            for dst, m in zip(last_rows, (G_F, SC_L, SH_L)):
                load_rows(sp, io, dst, None, m, rows_in)
            with sp.Fori(1, NG) as g:
                load_w1(sp, g)
                load_w2(sp, g)
            sp.wait_ge(w1_ready, NG + 1)
            for t in range(TT):
                if t >= 2:
                    sp.wait_ge(summed, t - 1)
                sp.dma_start(x1_room[:, t % 2, :], io["x1"][t * P:(t + 1) * P, :]).then_inc(x1_in[t % 2], 16)

        @block.gpsimd
        def _(pool):
            wait_all(pool, x_read)
            pool.memset(y[:], 0.0).then_inc(zeroed, 1)
            pool.memset(ys[:], 0.0).then_inc(zeroed, 1)
            pool.memset(hid_s[:], 0.0).then_inc(zeroed, 1)

            def square(g, s, u):
                j, half = divmod(u, 2)
                pool.wait_ge(relu_done, MAIN * g + u + 1)
                x = pos[u % 2][:]
                pool.tensor_tensor(x, x, x, ALU.mult).then_inc(sq_done, 1)

            def group(g, s, last=False):
                for u in range(MAIN):
                    square(g, s, u)
                if not last:
                    split_lo(pool, w1_lo[:], w1_raw, w1_hi[:], w1_hi_done, w1_ready, g + 1)
                hi, lo = last_w2 if last else (w2_hi[:], w2_lo[:])
                split_lo(pool, lo, w2_raw, hi, w2_hi_done, w2_ready, g)

            with pool.Fori(0, NG // 2 - 1) as i:
                for s in range(2):
                    group(2 * i + s, s)
            group(NG - 2, 0)
            group(NG - 1, 1, last=True)
            pool.wait_ge(rows_in, 16 * len(last_rows))
            for t in range(TT):
                pool.wait_ge(added, OUTS * (NG - 1) + 2 * t + 2 + 3)
                pool.tensor_tensor(y[:, t, :], y[:, t, :], last_rows[0][:], ALU.mult).then_inc(gated, 1)

        @block.scalar
        def _(act):
            def hidden(g, s, u):
                j, half = divmod(u, 2)
                act.wait_ge(sq_done, MAIN * g + u + 1)
                act.copy(h_hi[s][:, j, half * CH:(half + 1) * CH], pos[u % 2][:]).then_inc(h_hi_done, 1)

            def group(g, s, last=False):
                for u in range(MAIN):
                    act.wait_ge(made1, MAIN * g + u + 1)
                    act.wait_ge(h_ready, MAIN * g + u + 1)
                    act.activation(pos[u % 2][:], ps[:, u, :], ACT.Relu).then_inc(relu_done, 1)
                    if u == 0:
                        act.wait_ge(h_free, g + 1)
                    if u:
                        hidden(g, s, u - 1)
                hidden(g, s, MAIN - 1)
                act.wait_ge(s_made, g + 1)
                act.copy(lo_part[:], ps[NS:P, 4, 0:GF]).then_inc(s_lo, 1)
                if not last:
                    split_hi(act, w1_hi, w1_raw, w1_in, w1_free, w1_hi_done, g + 1)
                else:
                    act.wait_ge(w2_in, 16 * g + 16)
                    act.wait_ge(w1_free, g + 2)
                    act.copy(last_w2[0], w2_raw[:]).then_inc(w2_hi_done, 1)
                act.wait_ge(s_turned, g + 1)
                act.copy(hs[s][:, :, 0:NS], turned_s(ps)).then_inc(hs_hi, 1)
                if not last:
                    split_hi(act, w2_hi, w2_raw, w2_in, w2_free, w2_hi_done, g)

            wait_all(act, z_ready)
            with act.Fori(0, NG // 2 - 1) as i:
                for s in range(2):
                    group(2 * i + s, s)
            group(NG - 2, 0)
            group(NG - 1, 1, last=True)
            act.wait_ge(w2_ready, NG + 1)
            act.wait_ge(ss_zeroed, 1)
            sq = w2_raw[:, 0, :]
            for t in range(TT):
                act.wait_ge(summed, t + 1)
                if t:
                    act.wait_ge(squared, t)
                act.activation(sq, y[:, t, :], ACT.Square, accum_out=last_ss[:, t:t + 1]).then_inc(squared, 1)

        @block.vector
        def _(dve):
            dve.sem_inc(h_ready, 2)
            dve.sem_inc(added, 3)
            dve.sem_inc(hs_ready, 1)
            dve.wait_ge(zeroed, 3)
            dve.memset(last_ss[:], 1.0).then_inc(ss_zeroed, 1)

            def hidden(g, s):
                for u in range(MAIN):
                    j, half = divmod(u, 2)
                    cols = slice(half * CH, (half + 1) * CH)
                    dve.wait_ge(h_hi_done, MAIN * g + u + 1)
                    dve.tensor_tensor(h_lo[s][:, j, cols], pos[u % 2][:], h_hi[s][:, j, cols].bitcast(F32),
                                      ALU.subtract).then_inc(h_ready, 1)
                dve.wait_ge(s_lo, g + 1)
                dve.tensor_tensor(hid_s[0:NS, :], ps[0:NS, 4, 0:GF], lo_part[:], ALU.add).then_inc(s_sum, 1)
                dve.wait_ge(s_sum, g + 1)
                dve.scalar_tensor_tensor(out=hid_s[0:NS, :], in0=hid_s[0:NS, :], scalar=0.0, in1=hid_s[0:NS, :], op0=ALU.max,
                                         op1=ALU.mult).then_inc(hid_done, 1)

            def hidden_sample(g, s):
                dve.wait_ge(hs_hi, g + 1)
                dve.tensor_tensor(hs[s][:, :, NS:P], turned_s(ps),
                                  hs[s][:, :, 0:NS].bitcast(F32), ALU.subtract).then_inc(hs_ready, 1)

            def residual(t):
                dve.wait_ge(gated, t + 1)
                dve.wait_ge(x1_in[t % 2], 16 * (t // 2) + 16)
                dve.tensor_tensor(y[:, t, :], y[:, t, :], x1_room[:, t % 2, :], ALU.add).then_inc(summed, 1)

            def add(g, last=False):
                for o in range(OUTS):
                    t, c = divmod(o, 2)
                    cols = slice(c * CH, (c + 1) * CH)
                    dst = y[:, t, cols] if t < TT else ys[:, cols]
                    dve.wait_ge(made2, OUTS * g + o + 1)
                    dve.tensor_tensor(dst, dst, ps[:, 5 + o % 3, :], ALU.add).then_inc(added, 1)
                    if last and o >= 5 and o % 2:
                        residual(o // 2 - 2)
                dve.wait_ge(added, OUTS * g + OUTS + 3)

            hidden(0, 0)
            hidden_sample(0, 0)
            with dve.Fori(0, NG // 2 - 1) as i:
                for s in range(2):
                    g = 2 * i + s
                    hidden(g + 1, 1 - s)
                    add(g)
                    hidden_sample(g + 1, 1 - s)
            hidden(NG - 1, 1)
            add(NG - 2)
            hidden_sample(NG - 1, 1)
            add(NG - 1, last=True)
            residual(TT - 1)

        @block.tensor
        def _(pe):
            pe.sem_inc(h_free, 2)
            wait_all(pe, z_half)

            def first(g, s, opening=False):
                pe.wait_ge(w1_ready, g + 2)
                for u in range(MAIN):
                    if opening and u == 1:
                        wait_all(pe, z_ready)
                    j, half = divmod(u, 2)
                    rows = slice(half * CH, (half + 1) * CH)
                    for k in range(KT):
                        for a, (w, z) in enumerate(((w1_hi, z_hi), (w1_hi, z_lo), (w1_lo, z_hi))):
                            mm = pe.matmul(ps[:, u, :], w[:, k, j * P:(j + 1) * P], z[:, k, rows],
                                           start=(k == 0 and a == 0), stop=(k == KT - 1 and a == 2))
                    mm.then_inc(made1, 1)
                pe.wait_ge(hs_ready, g + 1)
                for k in range(KT):
                    for a, w in enumerate((w1_hi, w1_lo)):
                        mm = pe.matmul(ps[:, 4, 0:GF], zs[:, k, :], w[:, k, :], start=(k == 0 and a == 0),
                                       stop=(k == KT - 1 and a == 1))
                mm.then_inc(s_made, 1)
                pe.wait_ge(s_made, g + 1)
                pe.sem_inc(w1_free, 1)

            def turn_sample(g, s):
                pe.wait_ge(hid_done, g + 1)
                for j in range(J):
                    mm = pe.transpose(ps[:, 4, GF + j * P:GF + (j + 1) * P], hid_s[:, j * P:(j + 1) * P], ident[:])
                mm.then_inc(s_turned, 1)

            def second(g, s, last=False):
                hi, lo = last_w2 if last else (w2_hi[:], w2_lo[:])
                pe.wait_ge(w2_ready, g + 2)
                pe.wait_ge(h_ready, MAIN * g + MAIN + 2)
                for o in range(OUTS):
                    t, c = divmod(o, 2)
                    cols = slice(c * CH, (c + 1) * CH)
                    out = ps[:, 5 + o % 3, :]
                    pe.wait_ge(added, OUTS * g + o + 1)
                    if t < TT:
                        parts = [(h[s][:, j, t * P:(t + 1) * P], w[:, j, cols]) for j in range(J)
                                 for h, w in ((h_hi, hi), (h_hi, lo), (h_lo, hi))]
                    else:
                        if c == 0:
                            pe.wait_ge(hs_ready, g + 2)
                        parts = [(hs[s][:, j, :], w[:, j, cols]) for j in range(J) for w in (hi, lo)]
                    for a, (h, w) in enumerate(parts):
                        mm = pe.matmul(out, h, w, start=(a == 0), stop=(a == len(parts) - 1))
                    mm.then_inc(made2, 1)
                pe.wait_ge(made2, OUTS * g + OUTS)
                pe.sem_inc(w2_free, 1)
                pe.sem_inc(h_free, 1)

            first(0, 0, opening=True)
            turn_sample(0, 0)
            with pe.Fori(0, NG // 2 - 1) as i:
                for s in range(2):
                    g = 2 * i + s
                    first(g + 1, 1 - s)
                    second(g, s)
                    turn_sample(g + 1, 1 - s)
            first(NG - 1, 1)
            second(NG - 2, 0)
            turn_sample(NG - 1, 1)
            second(NG - 1, 1, last=True)



def stage_last(nc, io, y, ys, last_rows, ss):
    st = Stage(nc, "last")
    _, sc, sh = last_rows
    with st.ctx:
        x1s, y_lo, sq = (st.sb(n, [NS, D]) for n in ("x1s", "y_lo", "sq"))
        gate_s, sc_s, sh_s = (st.sb(n, [NS, D]) for n in ("gate_s", "sc_s", "sh_s"))
        T = {n: st.sb(n, [P, 16]) for n in ("v", "r", "t")}
        T["ss"] = ss
        T_s = {n: st.sb(f"{n}_s", [P, 1]) for n in ("ss", "v", "r", "t")}
        x_in, m_in, dve_s, v_ready, root, scaled, done, put, sample_done, lo_done, summed, ss_ready, squared = (
            st.sem(n) for n in ("x_in", "m_in", "dve_steps", "v_ready", "root", "scaled", "done", "put", "sample_done",
                                "lo_done", "summed", "ss_ready", "squared"))
        y_out = io["y_prompt"][0].rearrange("(t p) d -> p t d", p=P)
        block = st.block()

        @block.sync
        def _(sp):
            sp.dma_start(x1s[:], io["x1"][S:, :]).then_inc(x_in, 16)
            for s, m in ((gate_s, G_F), (sc_s, SC_L), (sh_s, SH_L)):
                load_rows(sp, io, None, s, m, m_in)
            for t in range(TT):
                sp.wait_ge(done, t + 1)
                sp.dma_start(y_out[:, t, :], y[:, t, :]).then_inc(put, 16)
            sp.wait_ge(sample_done, 1)
            sp.dma_start(io["y_sample"].rearrange("b t d -> (b t) d"), x1s[:]).then_inc(put, 16)
            sp.wait_ge(put, 16 * (TT + 1))

        @block.scalar
        def _(act):
            act.wait_ge(v_ready, 1)
            act.activation(T["t"][:, 0:TT], T["v"][:, 0:TT], ACT.Sqrt).then_inc(root, 1)
            act.copy(y_lo[:], ys[NS:P, :]).then_inc(lo_done, 1)
            act.wait_ge(summed, 3)
            act.wait_ge(ss_ready, 1)
            act.activation(sq[:], x1s[:], ACT.Square, accum_out=T_s["ss"][0:NS, 0:1]).then_inc(squared, 1)
            act.wait_ge(v_ready, 2)
            act.activation(T_s["t"][:], T_s["v"][:], ACT.Sqrt).then_inc(root, 1)

        @block.gpsimd
        def _(pool):
            pool.wait_ge(lo_done, 1)
            pool.tensor_tensor(y_lo[:], y_lo[:], ys[0:NS, :], ALU.add).then_inc(summed, 1)
            pool.wait_ge(m_in, 16 * 3 * DB)
            pool.wait_ge(summed, 1)
            pool.tensor_tensor(y_lo[:], y_lo[:], gate_s[:], ALU.mult).then_inc(summed, 1)
            pool.wait_ge(x_in, 16)
            pool.wait_ge(summed, 2)
            pool.tensor_tensor(x1s[:], x1s[:], y_lo[:], ALU.add).then_inc(summed, 1)

        @block.vector
        def _(dve):
            steps = Steps(dve, dve_s)

            dve.memset(T_s["ss"][:], 1.0).then_inc(ss_ready, 1)
            steps.done(dve.tensor_scalar(sc[:], sc[:], 1.0, None, ALU.add))
            rms_rows(steps, v_ready, root, T, TT)
            for t in range(TT):
                dve.scalar_tensor_tensor(out=y[:, t, :], in0=y[:, t, :], scalar=T["r"][:, t:t + 1], in1=sc[:],
                                         op0=ALU.mult, op1=ALU.mult).then_inc(scaled, 1)
                dve.wait_ge(scaled, t + 1)
                dve.tensor_tensor(y[:, t, :], y[:, t, :], sh[:], ALU.add).then_inc(done, 1)
                if t == TT - 2:
                    dve.wait_ge(m_in, 16 * 3 * DB)
                    steps.done(dve.tensor_scalar(sc_s[:], sc_s[:], 1.0, None, ALU.add))
                    dve.wait_ge(squared, 1)
                    rms_rows(steps, v_ready, root, T_s, 1, 2)
            steps.then(dve.scalar_tensor_tensor(out=x1s[:], in0=x1s[:], scalar=T_s["r"][0:NS, 0:1], in1=sc_s[:],
                                                op0=ALU.mult, op1=ALU.mult))
            dve.tensor_tensor(x1s[:], x1s[:], sh_s[:], ALU.add).then_inc(sample_done, 1)


def program(nc, io):
    Stage.used.clear()
    with ExitStack() as ctx:
        held = lambda c, n, shape, dt=F32: c.enter_context(nc.sbuf_tensor(n, shape, dt))
        ps = ctx.enter_context(nc.psum_tensor("ps", [P, 8, CH], F32))
        ident, mod_p = held(ctx, "ident", [P, P]), held(ctx, "mod_p", [P, 4, KT])
        feature_parts = lambda c, n: (held(c, f"{n}_hi", [P, KT, S], F32R), held(c, f"{n}_lo", [P, KT, S], F32R),
                                      held(c, f"{n}_s", [P, KT, P], F32R))
        row_parts = lambda c, n: (held(c, n, [P, TT, D]), held(c, f"{n}_s", [P, D]), held(c, f"{n}_ss", [P, 2, 16]))
        with ExitStack() as c:
            x, xs, ss = row_parts(c, "x")
            c_parts = held(c, "c_parts", [P, KT, NS], F32R)
            stage_modulation(nc, io, ps, ident, mod_p, x, xs[0:NS, :], ss, c_parts)
            z_hi, z_lo, zs = feature_parts(c, "z")
            stage_projection(nc, io, ps, ident, mod_p, z_hi, z_lo, zs, x, xs, ss, c_parts)
        with ExitStack() as c:
            mix_hi, mix_lo, mix_s = feature_parts(c, "mix")
            stage_prompt_attention(nc, io, ps, ident, mix_hi, mix_lo)
            stage_prompt_retention(nc, io, ps, ident, mix_hi, mix_lo)
            with ExitStack() as cc:
                q_blocks, kT_new = held(cc, "q_blocks", [P, DB, 4, NS]), held(cc, "kT_new", [P, 4, NS])
                K = [held(cc, f"K{b}", [P, KTILES, AW]) for b in range(2)]
                k_in = [cc.enter_context(nc.semaphore(f"k_in{b}")) for b in range(2)]
                stage_sample_heads(nc, io, ps, ident, mix_s, q_blocks, kT_new, K, k_in)
                stage_sample_attention(nc, io, ps, ident, mix_s, q_blocks, kT_new, K, k_in)
            x, xs, ss = row_parts(c, "res")
            stage_output(nc, io, ps, mod_p, mix_hi, mix_lo, mix_s, x, xs[0:NS, :], ss)
            last_rows = [held(c, n, [P, D]) for n in ("gate_row", "scale_row", "shift_row")]
            last_ss = held(c, "last_ss", [P, 16])
            stage_mlp(nc, io, ps, ident, mod_p, mix_hi, mix_lo, mix_s, x, xs, ss, last_rows, last_ss)
            stage_last(nc, io, x, xs, last_rows, last_ss)


_INS = ["x_prompt", "x_sample", "c_prompt", "c_sample", "cache_k", "cache_v", "state_ret",
        "w_ada", "b_ada", "w_in", "ret_gain", "w_out", "w_ff1", "w_ff2", "w_ada_f", "b_ada_f"]
_OUTS = [("y_prompt", (1, S, D)), ("y_sample", (DB, DS, D)),
         ("k_prompt", (1, 1, S, H, HD)), ("v_prompt", (1, 1, S, H, HD)), ("ret_prompt", (1, 1, RH, RD, RV)),
         ("k_sample", (1, DB, DS, H, HD)), ("v_sample", (1, DB, DS, H, HD)), ("ret_sample", (1, DB, RH, RD, RV))]


def build(nc, shapes):
    io = {n: nc.dram_tensor(f"in_{n}", s, F32, kind="ExternalInput").ap() for n, s in shapes.items()}
    for n, s in _OUTS:
        io[n] = nc.dram_tensor(f"out_{n}", s, F32, kind="ExternalOutput").ap()
    io["mod"] = nc.dram_tensor("mod", (9, MOD_W), F32).ap()
    io["proj"] = nc.dram_tensor("proj", (S + P, IN_W), F32).ap()
    io["x1"] = nc.dram_tensor("x1", (S + NS, D), F32).ap()
    program(nc, io)


def kernel(**inputs):
    import concourse.bacc as bacc
    from concourse.bass_utils import run_bass_kernel_spmd

    arrays = {n: np.ascontiguousarray(inputs[n]) for n in _INS}
    arrays.update(constants())
    nc = bacc.Bacc("TRN2", target_bir_lowering=False, num_devices=1)
    build(nc, {n: a.shape for n, a in arrays.items()})
    r = run_bass_kernel_spmd(nc, [{f"in_{n}": a for n, a in arrays.items()}], core_ids=[0])
    return tuple(r.results[0][f"out_{n}"] for n, _ in _OUTS)
```
